# Optimizing a Trainium2 kernel written in Bass

```python
import jax
import jax.numpy as jnp
from jax import lax
import numpy as np

D_MODEL = 1024
BATCH = 1
SEQ = 256
DEPTH = 2

EPS = 1e-6
MIX_WIDTH = D_MODEL
A_WIDTH = D_MODEL // 2
A_HEAD_DIM = 64
A_HEADS = A_WIDTH // A_HEAD_DIM
A_LORA_W = 64
A_LORA_A = 64
A_LORA_G = 128
A_IN = 3 * A_WIDTH + A_LORA_W + A_LORA_A + A_LORA_G
A_GN_EPS = 64e-5
B_WIDTH = D_MODEL // 2
B_GROUPS = 4
B_GROUP_DIM = B_WIDTH // B_GROUPS
B_CHUNK = 128
EVEN_IN = A_IN + 2 * B_WIDTH
C_WIDTH = D_MODEL // 2
C_GROUP_CH = 16
C_GROUPS = C_WIDTH // C_GROUP_CH
C_STATE = 64
D_WIDTH = D_MODEL // 2
D_HEAD_DIM = 64
D_HEADS = D_WIDTH // D_HEAD_DIM
D_NGROUPS = 2
D_STATE = 128
D_CONV = 4
D_CHUNK = 128
D_XBC = D_WIDTH + 2 * D_NGROUPS * D_STATE
ODD_IN = C_WIDTH + D_WIDTH + D_XBC + D_HEADS
FFN_DENSE = 2816
N_EXPERTS = 8
TOP_K = 2
FFN_EXPERT = 3584
MOE_BLOCK = 256

kernel_name = 'hybrid_rwkv7_gmlp_s5_ssd_moe'

def rms_norm(z, g):
    zf = z.astype(jnp.float32)
    y = zf * lax.rsqrt(jnp.mean(zf * zf, axis=-1, keepdims=True) + EPS)
    return (y * g.astype(jnp.float32)).astype(z.dtype)

def layer_norm(z, w, b, eps):
    zf = z.astype(jnp.float32)
    mean = jnp.mean(zf, axis=-1, keepdims=True)
    var = jnp.mean(jnp.square(zf - mean), axis=-1, keepdims=True)
    return (zf - mean) * lax.rsqrt(var + eps) * w + b

def token_shift(z):
    return jnp.pad(z, ((0, 0), (1, 0), (0, 0)))[:, :-1]

def causal_dwconv(z, w, b):
    t = z.shape[1]
    zp = jnp.pad(z, ((0, 0), (D_CONV - 1, 0), (0, 0)))
    out = b
    for j in range(D_CONV):
        out = out + w[j] * zp[:, j:j + t]
    return out

def swiglu(h, w_gate, w_up, w_down):
    return (jax.nn.silu(h @ w_gate) * (h @ w_up)) @ w_down

def rwkv7_step(state, inp):
    r_t, w_t, k_t, v_t, a_t, b_t = inp
    sa = jnp.einsum('bhvk,bhk->bhv', state, a_t)
    state = (state * w_t[:, :, None, :] + sa[..., None] * b_t[:, :, None, :]
             + v_t[..., None] * k_t[:, :, None, :])
    return state, jnp.einsum('bhvk,bhk->bhv', state, r_t)

def rwkv7_mix(p, mu, w0, w2, a0, a2, g2, k_k, k_a, r_k, ln_w, ln_b):
    f32 = jnp.float32
    bsz, t, _ = p.shape
    p = p + (token_shift(p) - p) * mu
    i3 = 3 * A_WIDTH
    r, k, v, xw, xa, xg = jnp.split(
        p, [A_WIDTH, 2 * A_WIDTH, i3, i3 + A_LORA_W, i3 + A_LORA_W + A_LORA_A], axis=-1)
    w = -jax.nn.softplus(-(w0 + jnp.tanh(xw) @ w2).astype(f32)) - 0.5
    decay = jnp.exp(-jnp.exp(w))
    a = jax.nn.sigmoid((a0 + xa @ a2).astype(f32))
    g = jax.nn.sigmoid(xg) @ g2
    k = k.astype(f32)
    heads = lambda z: z.astype(f32).reshape(bsz, t, A_HEADS, A_HEAD_DIM)
    kk = heads(k * k_k)
    kk = kk / jnp.maximum(jnp.sqrt(jnp.sum(kk * kk, axis=-1, keepdims=True)), 1e-12)
    k = heads(k * (1.0 + (a - 1.0) * k_a))
    r, v, decay, a = heads(r), heads(v), heads(decay), heads(a)
    tm = lambda z: jnp.swapaxes(z, 0, 1)
    xs = (tm(r), tm(decay), tm(k), tm(v), tm(-kk), tm(kk * a))
    s0 = jnp.zeros((bsz, A_HEADS, A_HEAD_DIM, A_HEAD_DIM), f32)
    _, y = lax.scan(rwkv7_step, s0, xs)
    y = jnp.swapaxes(y, 0, 1)
    y = layer_norm(y, ln_w.reshape(A_HEADS, A_HEAD_DIM), ln_b.reshape(A_HEADS, A_HEAD_DIM), A_GN_EPS)
    y = y + jnp.sum(r * k * r_k, axis=-1, keepdims=True) * v
    y = y.reshape(bsz, t, A_WIDTH) * g
    return y.astype(p.dtype)

def gmlp_mix(p, ln_w, ln_b, ws, bs):
    bsz, t, _ = p.shape
    u, v = jnp.split(jax.nn.gelu(p), 2, axis=-1)
    nc = t // B_CHUNK
    v = v.reshape(bsz, nc, B_CHUNK, B_GROUPS, B_GROUP_DIM)
    v = layer_norm(v, ln_w, ln_b, EPS)
    causal = jnp.tril(jnp.ones((B_CHUNK, B_CHUNK), bool))
    ws_c = jnp.where(causal[None], ws, 0.0)
    s = jnp.einsum('gij,bcjgd->bcigd', ws_c, v) + bs.T[None, None, :, :, None]
    return (u * s.reshape(bsz, t, B_WIDTH).astype(u.dtype)).astype(p.dtype)

def s5_combine(e1, e2):
    a1r, a1i, b1r, b1i = e1
    a2r, a2i, b2r, b2i = e2
    return (a2r * a1r - a2i * a1i,
            a2r * a1i + a2i * a1r,
            a2r * b1r - a2i * b1i + b2r,
            a2r * b1i + a2i * b1r + b2i)

def s5_mix(u, a_re, a_im, log_dt, b_re, b_im, c_re, c_im, d_skip, glu_w, glu_b):
    f32 = jnp.float32
    bsz, t, _ = u.shape
    uf = u.astype(f32).reshape(bsz, t, C_GROUPS, C_GROUP_CH)
    lr, li = a_re.astype(f32), a_im.astype(f32)
    dt = jnp.exp(log_dt.astype(f32))[:, None]
    mag = jnp.exp(lr * dt)
    abar_r, abar_i = mag * jnp.cos(li * dt), mag * jnp.sin(li * dt)
    nr, ni = abar_r - 1.0, abar_i
    den = lr * lr + li * li
    fr, fi = (nr * lr + ni * li) / den, (ni * lr - nr * li) / den
    br, bi = b_re.astype(f32), b_im.astype(f32)
    bbar_r = fr[..., None] * br - fi[..., None] * bi
    bbar_i = fr[..., None] * bi + fi[..., None] * br
    bu_r = jnp.einsum('btgc,gpc->tbgp', uf, bbar_r)
    bu_i = jnp.einsum('btgc,gpc->tbgp', uf, bbar_i)
    shp = bu_r.shape
    a_r = jnp.broadcast_to(abar_r, shp)
    a_i = jnp.broadcast_to(abar_i, shp)
    _, _, xr, xi = lax.associative_scan(s5_combine, (a_r, a_i, bu_r, bu_i), axis=0)
    y = (jnp.einsum('tbgp,gcp->btgc', xr, c_re.astype(f32))
         - jnp.einsum('tbgp,gcp->btgc', xi, c_im.astype(f32)))
    y = y + d_skip.astype(f32).reshape(C_GROUPS, C_GROUP_CH) * uf
    y = jax.nn.gelu(y.reshape(bsz, t, C_WIDTH))
    y = y * jax.nn.sigmoid(y @ glu_w.astype(f32) + glu_b.astype(f32))
    return y.astype(u.dtype)

def segsum(a):
    l = a.shape[-1]
    z = jnp.broadcast_to(a[..., :, None], a.shape + (l,))
    z = jnp.where(jnp.tril(jnp.ones((l, l), bool), -1), z, 0.0)
    cs = jnp.cumsum(z, axis=-2)
    return jnp.where(jnp.tril(jnp.ones((l, l), bool)), cs, -jnp.inf)

def ssd_chunked(x, a, bm, cm):
    b, t, h, pd = x.shape
    g, n = bm.shape[2], bm.shape[3]
    r = h // g
    c, l = t // D_CHUNK, D_CHUNK
    x = x.reshape(b, c, l, g, r, pd)
    a = a.reshape(b, c, l, g, r).transpose(0, 3, 4, 1, 2)
    bm = bm.reshape(b, c, l, g, n)
    cm = cm.reshape(b, c, l, g, n)
    a_cs = jnp.cumsum(a, axis=-1)
    lmat = jnp.exp(segsum(a))
    cb = jnp.einsum('bclgn,bcsgn->bgcls', cm, bm)
    y_diag = jnp.einsum('bgcls,bgrcls,bcsgrp->bclgrp', cb, lmat, x)
    decay_states = jnp.exp(a_cs[..., -1:] - a_cs)
    states = jnp.einsum('bclgn,bgrcl,bclgrp->bcgrpn', bm, decay_states, x)
    states = jnp.concatenate([jnp.zeros_like(states[:, :1]), states], axis=1)
    chunk_tot = jnp.pad(a_cs[..., -1], ((0, 0), (0, 0), (0, 0), (1, 0)))
    decay_chunk = jnp.exp(segsum(chunk_tot))
    states = jnp.einsum('bgrzc,bcgrpn->bzgrpn', decay_chunk, states)[:, :-1]
    y_off = jnp.einsum('bclgn,bcgrpn,bgrcl->bclgrp', cm, states, jnp.exp(a_cs))
    return (y_diag + y_off).reshape(b, t, h, pd)

def mamba2_mix(p, conv_w, conv_b, dt_bias, a_log, d_skip, norm_w):
    f32 = jnp.float32
    bsz, t, _ = p.shape
    z, xbc, dt = jnp.split(p, [D_WIDTH, D_WIDTH + D_XBC], axis=-1)
    xbc = jax.nn.silu(causal_dwconv(xbc, conv_w, conv_b)).astype(f32)
    xh, bm, cm = jnp.split(xbc, [D_WIDTH, D_WIDTH + D_NGROUPS * D_STATE], axis=-1)
    dt = jax.nn.softplus((dt + dt_bias).astype(f32))
    a = -jnp.exp(a_log.astype(f32))
    xh = xh.reshape(bsz, t, D_HEADS, D_HEAD_DIM)
    bm = bm.reshape(bsz, t, D_NGROUPS, D_STATE)
    cm = cm.reshape(bsz, t, D_NGROUPS, D_STATE)
    y = ssd_chunked(xh * dt[..., None], a * dt, bm, cm)
    y = y + d_skip.astype(f32)[None, None, :, None] * xh
    y = y.reshape(bsz, t, D_WIDTH) * jax.nn.silu(z.astype(f32))
    yg = y.reshape(bsz, t, D_NGROUPS, D_WIDTH // D_NGROUPS)
    yg = yg * lax.rsqrt(jnp.mean(yg * yg, axis=-1, keepdims=True) + EPS)
    return (yg.reshape(bsz, t, D_WIDTH) * norm_w.astype(f32)).astype(p.dtype)

def moe_swiglu(h, w_router, w_gate, w_up, w_down):
    bsz, t, d = h.shape
    n = bsz * t
    hf = h.reshape(n, d)
    logits = (hf @ w_router).astype(jnp.float32)
    top_vals, top_idx = lax.top_k(logits, TOP_K)
    gates = jax.nn.softmax(top_vals, axis=-1).astype(h.dtype)
    flat_e = top_idx.reshape(-1).astype(jnp.int32)
    flat_tok = jnp.repeat(jnp.arange(n, dtype=jnp.int32), TOP_K)
    flat_gate = gates.reshape(-1)
    order = jnp.argsort(flat_e)
    sorted_e = flat_e[order]
    counts = jnp.bincount(flat_e, length=N_EXPERTS)
    padded = (counts + MOE_BLOCK - 1) // MOE_BLOCK * MOE_BLOCK
    start = jnp.cumsum(counts) - counts
    pend = jnp.cumsum(padded)
    pstart = pend - padded
    rank = jnp.arange(n * TOP_K, dtype=jnp.int32) - start[sorted_e]
    dest = pstart[sorted_e] + rank
    n_blocks = -(-(n * TOP_K + N_EXPERTS * MOE_BLOCK) // MOE_BLOCK)
    n_slots = n_blocks * MOE_BLOCK
    slot_tok = jnp.full((n_slots,), n, jnp.int32).at[dest].set(flat_tok[order])
    slot_gate = jnp.zeros((n_slots,), h.dtype).at[dest].set(flat_gate[order])
    block_start = jnp.arange(n_blocks, dtype=jnp.int32) * MOE_BLOCK
    block_expert = jnp.minimum(jnp.searchsorted(pend, block_start, side='right'), N_EXPERTS - 1)
    hpad = jnp.concatenate([hf, jnp.zeros((1, d), h.dtype)], axis=0)
    xs = hpad[slot_tok].reshape(n_blocks, MOE_BLOCK, d)

    def expert_block(args):
        xb, e = args
        return swiglu(xb, w_gate[e], w_up[e], w_down[e])

    ys = lax.map(expert_block, (xs, block_expert)).reshape(n_slots, d)
    out = jnp.zeros((n + 1, d), h.dtype).at[slot_tok].add(ys * slot_gate[:, None])
    return out[:n].reshape(bsz, t, d)

def even_layer(x, norm_pre_mix, w_in, rwkv_p, gmlp_p, w_out, norm_post_mix,
               norm_pre_ffn, ffn_p, norm_post_ffn):
    p = rms_norm(x, norm_pre_mix) @ w_in
    ya = rwkv7_mix(p[..., :A_IN], *rwkv_p)
    yb = gmlp_mix(p[..., A_IN:], *gmlp_p)
    y = jnp.concatenate([ya, yb], axis=-1) @ w_out
    x = x + rms_norm(y, norm_post_mix)
    x = x + rms_norm(swiglu(rms_norm(x, norm_pre_ffn), *ffn_p), norm_post_ffn)
    return x

def odd_layer(x, norm_pre_mix, w_in, s5_p, m2_p, w_out, norm_post_mix,
              norm_pre_ffn, moe_p, norm_post_ffn):
    p = rms_norm(x, norm_pre_mix) @ w_in
    yc = s5_mix(p[..., :C_WIDTH], *s5_p)
    yd = mamba2_mix(p[..., C_WIDTH:], *m2_p)
    y = jnp.concatenate([yc, yd], axis=-1) @ w_out
    x = x + rms_norm(y, norm_post_mix)
    x = x + rms_norm(moe_swiglu(rms_norm(x, norm_pre_ffn), *moe_p), norm_post_ffn)
    return x

def setup_inputs(seed: int = 0) -> dict:
    key = jax.random.key(seed)
    ks = iter(jax.random.split(key, 80))
    f32 = jnp.float32

    def nrm(shape, scale):
        return scale * jax.random.normal(next(ks), shape, f32)

    def unif(shape, lo, hi):
        return jax.random.uniform(next(ks), shape, f32, lo, hi)

    def gain(shape):
        return 1.0 + nrm(shape, 0.02)

    D = D_MODEL
    x = nrm((BATCH, SEQ, D), 1.0)
    l0_norm_pre_mix = gain((D,))
    l0_w_in = nrm((D, EVEN_IN), D ** -0.5)
    l0_rwkv_mu = unif((A_IN,), 0.0, 1.0)
    ramp = jnp.arange(A_WIDTH, dtype=f32) / (A_WIDTH - 1)
    l0_rwkv_w0 = -6.5 + 5.0 * ramp ** 0.9 + nrm((A_WIDTH,), 0.01)
    l0_rwkv_w2 = nrm((A_LORA_W, A_WIDTH), 0.1 * A_LORA_W ** -0.5)
    l0_rwkv_a0 = nrm((A_WIDTH,), 0.1)
    l0_rwkv_a2 = nrm((A_LORA_A, A_WIDTH), 0.1 * A_LORA_A ** -0.5)
    l0_rwkv_g2 = nrm((A_LORA_G, A_WIDTH), A_LORA_G ** -0.5)
    l0_rwkv_k_k = 0.85 + nrm((A_WIDTH,), 0.02)
    l0_rwkv_k_a = 1.0 + nrm((A_WIDTH,), 0.02)
    l0_rwkv_r_k = nrm((A_HEADS, A_HEAD_DIM), 0.1)
    l0_rwkv_ln_w = gain((A_WIDTH,))
    l0_rwkv_ln_b = nrm((A_WIDTH,), 0.01)
    l0_gmlp_ln_w = gain((B_GROUPS, B_GROUP_DIM))
    l0_gmlp_ln_b = nrm((B_GROUPS, B_GROUP_DIM), 0.01)
    l0_gmlp_ws = nrm((B_GROUPS, B_CHUNK, B_CHUNK), B_CHUNK ** -0.5)
    l0_gmlp_bs = 1.0 + nrm((B_GROUPS, B_CHUNK), 0.02)
    l0_w_out = nrm((MIX_WIDTH, D), MIX_WIDTH ** -0.5)
    l0_norm_post_mix = gain((D,))
    l0_norm_pre_ffn = gain((D,))
    l0_ffn_w_gate = nrm((D, FFN_DENSE), D ** -0.5)
    l0_ffn_w_up = nrm((D, FFN_DENSE), D ** -0.5)
    l0_ffn_w_down = nrm((FFN_DENSE, D), FFN_DENSE ** -0.5)
    l0_norm_post_ffn = gain((D,))
    l1_norm_pre_mix = gain((D,))
    l1_w_in = nrm((D, ODD_IN), D ** -0.5)
    l1_s5_a_re = -0.5 + nrm((C_GROUPS, C_STATE), 0.01)
    l1_s5_a_im = jnp.pi * jnp.arange(C_STATE, dtype=f32)[None, :] + nrm((C_GROUPS, C_STATE), 0.01)
    l1_s5_log_dt = unif((C_GROUPS,), float(np.log(1e-3)), float(np.log(1e-1)))
    l1_s5_b_re = nrm((C_GROUPS, C_STATE, C_GROUP_CH), (2 * C_GROUP_CH) ** -0.5)
    l1_s5_b_im = nrm((C_GROUPS, C_STATE, C_GROUP_CH), (2 * C_GROUP_CH) ** -0.5)
    l1_s5_c_re = nrm((C_GROUPS, C_GROUP_CH, C_STATE), C_STATE ** -0.5)
    l1_s5_c_im = nrm((C_GROUPS, C_GROUP_CH, C_STATE), C_STATE ** -0.5)
    l1_s5_d = nrm((C_WIDTH,), 0.5)
    l1_s5_glu_w = nrm((C_WIDTH, C_WIDTH), C_WIDTH ** -0.5)
    l1_s5_glu_b = nrm((C_WIDTH,), 0.01)
    l1_m2_conv_w = nrm((D_CONV, D_XBC), D_CONV ** -0.5)
    l1_m2_conv_b = nrm((D_XBC,), 0.01)
    dt0 = jnp.exp(unif((D_HEADS,), float(np.log(1e-3)), float(np.log(1e-1))))
    l1_m2_dt_bias = dt0 + jnp.log(-jnp.expm1(-dt0))
    l1_m2_a_log = jnp.log(unif((D_HEADS,), 1.0, 16.0))
    l1_m2_d = gain((D_HEADS,))
    l1_m2_norm_w = gain((D_WIDTH,))
    l1_w_out = nrm((MIX_WIDTH, D), MIX_WIDTH ** -0.5)
    l1_norm_post_mix = gain((D,))
    l1_norm_pre_ffn = gain((D,))
    l1_moe_router = nrm((D, N_EXPERTS), D ** -0.5)
    l1_moe_w_gate = nrm((N_EXPERTS, D, FFN_EXPERT), D ** -0.5)
    l1_moe_w_up = nrm((N_EXPERTS, D, FFN_EXPERT), D ** -0.5)
    l1_moe_w_down = nrm((N_EXPERTS, FFN_EXPERT, D), FFN_EXPERT ** -0.5)
    l1_norm_post_ffn = gain((D,))
    return {
        'x': x,
        'l0_norm_pre_mix': l0_norm_pre_mix, 'l0_w_in': l0_w_in,
        'l0_rwkv_mu': l0_rwkv_mu, 'l0_rwkv_w0': l0_rwkv_w0, 'l0_rwkv_w2': l0_rwkv_w2,
        'l0_rwkv_a0': l0_rwkv_a0, 'l0_rwkv_a2': l0_rwkv_a2, 'l0_rwkv_g2': l0_rwkv_g2,
        'l0_rwkv_k_k': l0_rwkv_k_k, 'l0_rwkv_k_a': l0_rwkv_k_a, 'l0_rwkv_r_k': l0_rwkv_r_k,
        'l0_rwkv_ln_w': l0_rwkv_ln_w, 'l0_rwkv_ln_b': l0_rwkv_ln_b,
        'l0_gmlp_ln_w': l0_gmlp_ln_w, 'l0_gmlp_ln_b': l0_gmlp_ln_b,
        'l0_gmlp_ws': l0_gmlp_ws, 'l0_gmlp_bs': l0_gmlp_bs,
        'l0_w_out': l0_w_out, 'l0_norm_post_mix': l0_norm_post_mix,
        'l0_norm_pre_ffn': l0_norm_pre_ffn, 'l0_ffn_w_gate': l0_ffn_w_gate,
        'l0_ffn_w_up': l0_ffn_w_up, 'l0_ffn_w_down': l0_ffn_w_down,
        'l0_norm_post_ffn': l0_norm_post_ffn,
        'l1_norm_pre_mix': l1_norm_pre_mix, 'l1_w_in': l1_w_in,
        'l1_s5_a_re': l1_s5_a_re, 'l1_s5_a_im': l1_s5_a_im, 'l1_s5_log_dt': l1_s5_log_dt,
        'l1_s5_b_re': l1_s5_b_re, 'l1_s5_b_im': l1_s5_b_im,
        'l1_s5_c_re': l1_s5_c_re, 'l1_s5_c_im': l1_s5_c_im, 'l1_s5_d': l1_s5_d,
        'l1_s5_glu_w': l1_s5_glu_w, 'l1_s5_glu_b': l1_s5_glu_b,
        'l1_m2_conv_w': l1_m2_conv_w, 'l1_m2_conv_b': l1_m2_conv_b,
        'l1_m2_dt_bias': l1_m2_dt_bias, 'l1_m2_a_log': l1_m2_a_log,
        'l1_m2_d': l1_m2_d, 'l1_m2_norm_w': l1_m2_norm_w,
        'l1_w_out': l1_w_out, 'l1_norm_post_mix': l1_norm_post_mix,
        'l1_norm_pre_ffn': l1_norm_pre_ffn, 'l1_moe_router': l1_moe_router,
        'l1_moe_w_gate': l1_moe_w_gate, 'l1_moe_w_up': l1_moe_w_up,
        'l1_moe_w_down': l1_moe_w_down, 'l1_norm_post_ffn': l1_norm_post_ffn,
    }

def reference(x,
              l0_norm_pre_mix, l0_w_in,
              l0_rwkv_mu, l0_rwkv_w0, l0_rwkv_w2, l0_rwkv_a0, l0_rwkv_a2, l0_rwkv_g2,
              l0_rwkv_k_k, l0_rwkv_k_a, l0_rwkv_r_k, l0_rwkv_ln_w, l0_rwkv_ln_b,
              l0_gmlp_ln_w, l0_gmlp_ln_b, l0_gmlp_ws, l0_gmlp_bs,
              l0_w_out, l0_norm_post_mix, l0_norm_pre_ffn,
              l0_ffn_w_gate, l0_ffn_w_up, l0_ffn_w_down, l0_norm_post_ffn,
              l1_norm_pre_mix, l1_w_in,
              l1_s5_a_re, l1_s5_a_im, l1_s5_log_dt, l1_s5_b_re, l1_s5_b_im,
              l1_s5_c_re, l1_s5_c_im, l1_s5_d, l1_s5_glu_w, l1_s5_glu_b,
              l1_m2_conv_w, l1_m2_conv_b, l1_m2_dt_bias, l1_m2_a_log, l1_m2_d, l1_m2_norm_w,
              l1_w_out, l1_norm_post_mix, l1_norm_pre_ffn,
              l1_moe_router, l1_moe_w_gate, l1_moe_w_up, l1_moe_w_down, l1_norm_post_ffn):
    layer_params = (
        (l0_norm_pre_mix, l0_w_in,
         (l0_rwkv_mu, l0_rwkv_w0, l0_rwkv_w2, l0_rwkv_a0, l0_rwkv_a2, l0_rwkv_g2,
          l0_rwkv_k_k, l0_rwkv_k_a, l0_rwkv_r_k, l0_rwkv_ln_w, l0_rwkv_ln_b),
         (l0_gmlp_ln_w, l0_gmlp_ln_b, l0_gmlp_ws, l0_gmlp_bs),
         l0_w_out, l0_norm_post_mix, l0_norm_pre_ffn,
         (l0_ffn_w_gate, l0_ffn_w_up, l0_ffn_w_down), l0_norm_post_ffn),
        (l1_norm_pre_mix, l1_w_in,
         (l1_s5_a_re, l1_s5_a_im, l1_s5_log_dt, l1_s5_b_re, l1_s5_b_im,
          l1_s5_c_re, l1_s5_c_im, l1_s5_d, l1_s5_glu_w, l1_s5_glu_b),
         (l1_m2_conv_w, l1_m2_conv_b, l1_m2_dt_bias, l1_m2_a_log, l1_m2_d, l1_m2_norm_w),
         l1_w_out, l1_norm_post_mix, l1_norm_pre_ffn,
         (l1_moe_router, l1_moe_w_gate, l1_moe_w_up, l1_moe_w_down), l1_norm_post_ffn),
    )
    for i in range(DEPTH):
        if i % 2 == 0:
            x = even_layer(x, *layer_params[i])
        else:
            x = odd_layer(x, *layer_params[i])
    return x


_drawn_inputs = setup_inputs


def setup_inputs(seed=0):
    import zlib

    import numpy as np

    out = dict(_drawn_inputs(seed))
    spreads = {}
    factors = {'l0_rwkv_w2': 8.0,
     'l0_rwkv_ln_b': 3.18,
     'l0_gmlp_ln_b': 7.148,
     'l1_s5_a_re': 64.0,
     'l1_s5_b_re': 2.817,
     'l1_s5_glu_b': 8.0,
     'l1_m2_conv_b': 3.928,
     'l1_norm_post_ffn': 19.392,
     'l1_s5_b_im': 3.873}
    for name, (base, spread) in spreads.items():
        noise = np.random.default_rng([zlib.crc32(name.encode()), seed]).standard_normal(out[name].shape)
        drawn = base * np.exp(spread * noise) if base else spread * noise
        out[name] = jnp.asarray(drawn.astype(out[name].dtype))
    for name, factor in factors.items():
        out[name] = (out[name] * factor).astype(out[name].dtype)
    return out
```

```python
import math
from contextlib import ExitStack

import concourse.bass as bass
from concourse import mybir

F32 = mybir.dt.float32
I32 = mybir.dt.int32
F32R = mybir.dt.float32r
ALU = mybir.AluOpType
ACT = mybir.ActivationFunctionType
AX = mybir.AxisListType

P = 128
T = 256
NC = T // P
D = 1024
KT = D // P
EPS = 1e-6
NB = 512

WID = D // 2
WT = WID // P
HD = 64
NH = WID // HD
A_IN = 3 * WID + 64 + 64 + 128
A_TILES = A_IN // P
EVEN_IN = A_IN + 2 * WID
GN_EPS = 64e-5
LEVELS = 7
K_DECAY = math.exp(-0.5)

S5_TILES = 16
D_XBC = 1024
ODD_MAIN = 2048
FFN = 2816
FT = FFN // P
NE = 8
FE = 3584
UNITS = FE // NB
MAX_OVER = 3
PASSES = NE + MAX_OVER

SLOT = 4096
SLOTS = 7
HALF = SLOT // 2
HALVES = 7

VECS = [("mu", A_TILES), ("w0", WT), ("a0", WT), ("k_k", WT), ("k_a", WT), ("r_k", WT),
        ("ln_w", WT), ("ln_b", WT), ("g_mix0", KT), ("g_ffn0", KT), ("g_mix1", KT), ("g_ffn1", KT),
        ("a_re", S5_TILES), ("a_im", S5_TILES), ("log_dt", S5_TILES), ("s5_d", WT), ("glu_b", WT),
        ("conv_w", 4 * KT), ("conv_b", KT), ("m2_d", WT), ("m2_norm", WT),
        ("dt_bias", NH), ("a_log", NH)]
VEC_AT = {}
_at = 0
for _n, _w in VECS:
    VEC_AT[_n] = (_at, _w)
    _at += _w
N_VEC = _at

CONSTS = [("ident", P), ("lt", P), ("le", P), ("gt", P), ("blk", P), ("iota", P), ("lower8", NE * NE),
          ("one", P), ("eps", 3)]
CONST_AT = {}
_at = 0
for _n, _w in CONSTS:
    CONST_AT[_n] = (_at, _w)
    _at += _w
N_CONST = _at


class Region:

    def __init__(self, ap):
        self.ap, self.at = ap, 0

    def take(self, *shape):
        n = math.prod(shape)
        got = self.ap[:, self.at:self.at + n]
        assert self.at + n <= self.ap.shape[1], (self.at, n)
        self.at += n
        if len(shape) == 1:
            return got
        names = "abcde"[:len(shape)]
        spec = f"p ({' '.join(names)}) -> p {' '.join(names)}"
        return got.rearrange(spec, **dict(zip(names[1:], shape[1:])))


class Order:

    def __init__(self, engine, sem):
        self.engine, self.sem, self.n = engine, sem, 0

    def then(self, ins):
        self.mark(ins)
        self.join()

    def mark(self, ins):
        ins.then_inc(self.sem, 1)
        self.n += 1

    def join(self):
        self.engine.wait_ge(self.sem, self.n)


def along(vec, n):
    return vec.rearrange("p (k o) -> p k o", o=1).broadcast_to([vec.shape[0], vec.shape[1], n])


def across(mat, k):
    return mat.rearrange("p (o n) -> p o n", o=1).broadcast_to([mat.shape[0], k, mat.shape[1]])


def trunk(nc, t, out, stop=None, dbg=None):
    ctx = ExitStack()
    with ctx:
        def sb(name, *shape):
            return ctx.enter_context(nc.sbuf_tensor(name, [P, *shape], F32))

        def sem(name):
            return ctx.enter_context(nc.semaphore(name))

        consts = sb("consts", N_CONST)
        vecs = sb("vecs", N_VEC)
        x_rows = sb("x_rows", NC, D)
        xn = sb("xn", KT, T)
        gain_rows = sb("gain_rows", D)
        w_small = sb("w_small", 2, KT, NE)
        stats = sb("stats", 16)
        work_a = sb("work_a", 9216)
        with ExitStack() as first:
            tables = first.enter_context(nc.sbuf_tensor("tables", [P, 8192], F32))
            ring = first.enter_context(nc.sbuf_tensor("ring", [P, SLOTS, SLOT], F32))
        sb("tables_front", 8192 - 2048)
        ht_parts = ctx.enter_context(nc.sbuf_tensor("ht_parts", [P, 2, 2, 4, P], F32R))
        xg_parts = ctx.enter_context(nc.sbuf_tensor("xg_parts", [P, 2, KT, P], F32R))
        sb("ring_front", 4 * SLOT - 2048)
        split = ctx.enter_context(nc.sbuf_tensor("split", [P, 3, 2, HALF], F32R))
        ps = ctx.enter_context(nc.psum_tensor("ps", [P, 8, NB], F32))
        ring_flat = ring[:, :, :].rearrange("p s n -> p (s n)")

        def const(name):
            a, w = CONST_AT[name]
            return consts[:, a:a + w]

        def vec(name):
            a, w = VEC_AT[name]
            return vecs[:, a:a + w]

        ident = const("ident")
        sumsq, root, rstd = stats[:, 0:2], stats[:, 2:4], stats[:, 4:6]

        def slot_tiles(s, n=NB, k=KT):
            return ring[:, s, 0:k * n].rearrange("p (k n) -> p k n", k=k)

        a0 = Region(work_a[:, :])
        praw = a0.take(A_TILES, T)
        pm = a0.take(A_TILES, T)
        u_cols = a0.take(WT, T)
        v_rows = a0.take(NC, WID)
        a0b = Region(work_a[:, 0:A_TILES * T])
        sig_w, cs, csc = a0b.take(WT, T), a0b.take(WT, T), a0b.take(WT, T)
        y8 = work_a[:, 0:KT * T].rearrange("p (k n) -> p k n", k=KT)
        xs = work_a[:, 2 * A_TILES * T:2 * A_TILES * T + NC * D].rearrange("p (c n) -> p c n", c=NC)
        b1 = Region(ring_flat[:, 2 * SLOT:6 * SLOT])
        early = Region(b1.take(8 * WT * T))
        csm, e_dec, e_prev, e_inv = (early.take(WT, T) for _ in range(4))
        gate_a, kk, kp, knorm = (early.take(WT, T) for _ in range(4))
        mats = ring_flat[:, 2 * SLOT:4 * SLOT].rearrange("p (m j n) -> p m j n", m=NH * NC, j=4)
        ar = b1.take(WT, NC, 2, P)
        bt, kt = b1.take(WT, T), b1.take(WT, T)
        v_tok = b1.take(NC, WID)
        bk_tok = b1.take(2, WID)
        bonus_in = b1.take(WT, T)
        rhs_tok, sa_tok = b1.take(WID), b1.take(WID)
        y_cols = ar.rearrange("p a b c d -> p (a b c d)")[:, 0:WT * T].rearrange("p (a n) -> p a n", a=WT)
        y_sq = ar.rearrange("p a b c d -> p (a b c d)")[:, WT * T:].rearrange("p (a n) -> p a n", a=WT)
        b2 = Region(ring[:, 6, :])
        inv_mask = b2.take(LEVELS, P)
        lora_wa, lora_g = b2.take(WID), b2.take(WID)
        gln = b2.take(2, WID)
        ws_t = b2.take(WT, P)
        state = b2.take(WT, 2, HD)
        half_sum = b2.take(WT, NC)
        state_scale = b2.take(WT)
        bn6 = b2.take(NC * WT, 6)
        bn2 = b2.take(NC * WT, 2)
        bs_row = gain_rows[:, 0:WID]
        tb = Region(tables[:, :])
        inv_t, inv_tt, inv_v, inv_m = (tb.take(4, 4, P) for _ in range(4))

        f_area = Region(ring_flat[:, 4 * SLOT:])
        f_w = [(f_area.take(2, KT, P), f_area.take(D)) for _ in range(4)]
        f_silu = [work_a[:, b * 512:b * 512 + T] for b in range(2)]
        f_act = [work_a[:, b * 512 + T:b * 512 + 2 * T] for b in range(2)]

        angle = sb("angle", LEVELS + 1, S5_TILES)
        turns = sb("turns", LEVELS + 1, S5_TILES)
        rot_c, rot_s = sb("rot_c", LEVELS + 1, S5_TILES), sb("rot_s", LEVELS + 1, S5_TILES)
        s5v = sb("s5v", 7, S5_TILES)
        s5_dt, s5_mag, f_re, f_im, s5_den, s5_nr, s5_ni = (s5v[:, i, :] for i in range(7))
        cos_t = tables[:, 0:S5_TILES * T].rearrange("p (j n) -> p j n", j=S5_TILES)
        sin_t = tables[:, S5_TILES * T:].rearrange("p (j n) -> p j n", j=S5_TILES)
        rot_tmp = [work_a[:, 1024 + i * 2048:3072 + i * 2048] for i in range(2)]
        a1 = Region(work_a[:, :])
        p1 = a1.take(2 * KT, T)
        xc = a1.take(KT, T)
        ce = a1.take(NH, P)
        yz = xs[:, 0, :].rearrange("p (i n) -> p i n", i=WT)
        yz_sq = xs[:, 1, :].rearrange("p (i n) -> p i n", i=WT)
        xdec = p1[:, 8:10, :].rearrange("p a n -> p (a n)")
        st_rows = p1[:, 10:12, :].rearrange("p a n -> p (a n)")
        c1 = Region(ring_flat[:, 4 * SLOT:])
        b_in, c_in, c_out = c1.take(2, 4, P), c1.take(2, S5_TILES, 32), c1.take(2, S5_TILES, 32)
        tmp1, tmp2, v_re, v_im, z_re, z_im, q_re, q_im = (c1.take(4, T) for _ in range(8))
        y5 = c1.take(WT, T)
        glu_w = ring[:, 2, 0:2048].rearrange("p (k n) -> p k n", k=WT)
        d1 = Region(ring_flat[:, 2 * SLOT + 2048:4 * SLOT])
        seg_in = d1.take(NC, NH, P)
        lmat = d1.take(NC, NH, P)
        cb = d1.take(NC, 2, P)
        xdt = d1.take(NC, WID)
        b_rows = d1.take(2 * P)
        acs_in = seg_in[:, 0, :, :]
        ssd = d1.take(8, NC * NH)
        dt_v, sp_e, sp_w, sp_l, adt, dec_s, a_neg, sp_m = (ssd[:, i, :] for i in range(8))

        e1 = Region(work_a[:, 0:2 * A_TILES * T])
        xg = e1.take(KT, P)
        perm, perm_gate = e1.take(NC, P), e1.take(NC, P)
        perm_t = e1.take(NC, P)
        e_silu, e_h = [e1.take(NB) for _ in range(2)], [e1.take(NB) for _ in range(2)]
        e_y = e1.take(2, NB)
        g1 = Region(tables[:, 0:8192 - 2048])
        moe = g1.take(NC, D)
        logits, beaten, sel, e_exp = (g1.take(NC, NE) for _ in range(4))
        cmp1, cmp2 = g1.take(NC, NE, NE), g1.take(NC, NE, NE)
        top, den = g1.take(NC), g1.take(NC)
        rank_all, gate_all = g1.take(NC, PASSES + 1), g1.take(NC, PASSES + 1)
        chosen = g1.take(NC, NE)
        counts, over, over_sum, pick = (g1.take(NE) for _ in range(4))
        plan_f = g1.take(1 + MAX_OVER)
        plan = g1.take(1 + MAX_OVER).bitcast(I32)

        s_init = sem("params_loaded")
        s_x = sem("x_loaded")
        s_b2 = sem("mixer0_params_loaded")
        s_gain = sem("gain_rows_loaded")
        loaded = [sem(f"slot{i}_loaded") for i in range(SLOTS)]
        used = sem("slots_used")
        x_ready = sem("x_rows_ready")
        rms_ready = sem("norm_root_ready")
        scaled = sem("norm_rows_scaled")
        norm_t = sem("norm_transposed")
        xn_ready = sem("xn_ready")
        y_done = sem("out_product_done")
        out_root = sem("post_norm_root_ready")
        o_act, o_dve, o_pool = sem("act_order"), sem("dve_order"), sem("pool_order")
        in_done = sem("in_product_done")
        in_dve, in_act = sem("in_copied_by_dve"), sem("in_copied_by_act")
        lora_mixed, mixed = sem("loras_mixed"), sem("p_mixed")
        lora_act = sem("loras_activated")
        wl_done, al_done = sem("w_lora_done"), sem("a_lora_done")
        sig_ready, ga_ready = sem("sig_w_ready"), sem("gate_a_ready")
        kksq_ready, kksum_done, knorm_ready = sem("kk_squared"), sem("kk_summed"), sem("kk_norm_ready")
        cs_ready, exps_ready = sem("decay_sums_ready"), sem("decays_ready")
        half_ready, scale_ready = sem("state_exponent_ready"), sem("state_scale_ready")
        ab_ready, bonus_ready = sem("abrk_ready"), sem("bonus_in_ready")
        rows_done, rows_copied = sem("vbk_transposed"), sem("vbk_rows_ready")
        mat_zero, mat_done, mat_ready = sem("mat_zeroed"), sem("mat_done"), sem("mat_ready")
        m_ready, u_done, v_ready = sem("inv_m_ready"), sem("inv_u_done"), sem("inv_v_ready")
        tt_done, t_copied, tt_copied = sem("inv_t_done"), sem("inv_t_copied"), sem("inv_tt_copied")
        rhs_done, rhs_ready = sem("rhs_done"), sem("rhs_ready")
        sa_done, sa_ready = sem("sa_done"), sem("sa_ready")
        yk_done, st_done, st_ready = sem("rwkv_y_done"), sem("state_done"), sem("state_ready")
        ysum_in, ysum_done, gn_root = sem("group_norm_in"), sem("group_norm_summed"), sem("group_norm_root")
        bg_done = sem("bonus_and_gate_done")
        ya_ready, yb_ready = sem("ya_ready"), sem("yb_ready")
        gv_ready, ws_ready, gs_done = sem("gmlp_v_ready"), sem("spatial_weights_ready"), sem("spatial_done")
        gv_root = sem("gmlp_root_ready")
        gv_stats = sem("gmlp_stats_ready")
        f_loaded = [sem(f"ffn_weights{b}_loaded") for b in range(4)]
        f_prod, f_silu_ready, f_act_ready = sem("ffn_gate_up_done"), sem("ffn_silu_ready"), sem("ffn_act_ready")
        f_free, f_down_done = sem("ffn_weights_free"), sem("ffn_down_done")
        s_small = sem("small_weights_loaded")
        ang_ready, ang_reduced, rot_ready = sem("dt_ready"), sem("angles_reduced"), sem("rotations_ready")
        rot_table = sem("rotation_tables_ready")
        s5_loaded, glu_loaded = sem("s5_maps_loaded"), sem("glu_loaded")
        p1_done, p1_ready, dt_done = sem("in1_product_done"), sem("in1_copied"), sem("dt_product_done")
        bu_done, v_done, q_done, y5_done = sem("s5_bu_done"), sem("s5_bu_used"), sem("s5_x_ready"), sem("s5_y_done")
        c_ready = sem("s5_output_map_ready")
        conv_done, xc_ready = sem("conv_done"), sem("xbc_ready")
        sp1, sp2, sp3, dt_ready = sem("softplus_in"), sem("softplus_exp"), sem("softplus_ln"), sem("dt_and_a_ready")
        seg_ready, jobs = sem("segment_weights_ready"), sem("ssd_products_done")
        ssd_act, ssd_dve = sem("ssd_copied_by_act"), sem("ssd_copied_by_dve")
        m_act, xdec_ready, mats1 = sem("xdec_in"), sem("xdec_ready"), sem("ssd_matrices_ready")
        ce_ready, ssd_y = sem("ce_ready"), sem("ssd_y_done")
        yz_ready, yz_sum, yz_root = sem("ssd_gated_ready"), sem("ssd_gated_summed"), sem("ssd_gated_root")
        y5_in, gy_ready, glu_done, glu_sig = sem("s5_y_ready"), sem("s5_gelu_ready"), sem("glu_done"), sem("glu_sigmoid")
        yc_ready, yd_ready = sem("yc_ready"), sem("yd_ready")
        logits_done, router_max, router_exp = sem("logits_done"), sem("router_max"), sem("router_exp")
        sel_ready, ranks_done, plan_ready = sem("selection_ready"), sem("ranks_done"), sem("plan_ready")
        e_loaded = [sem(f"expert_half{i}_loaded") for i in range(HALVES)]
        hi_ready, lo_ready = sem("expert_high_part_ready"), sem("expert_low_part_ready")
        part_done = sem("expert_half_used")
        perm_ready, gather_done, xg_ready = sem("perm_parts_ready"), sem("gather_done"), sem("xg_ready")
        xg_hi, xg_lo = sem("xg_high_part_ready"), sem("xg_low_part_ready")
        pgt_done, pgt_copied = sem("perm_transposed"), sem("perm_t_ready")
        silu_ready, h_ready = sem("expert_silu_ready"), sem("expert_h_ready")
        t_done, ht_hi, ht_lo = sem("expert_h_transposed"), sem("expert_ht_high_ready"), sem("expert_ht_low_ready")
        ey_ready = sem("expert_y_ready")
        comb_done, comb_added = sem("scatter_done"), sem("scatter_added")
        moe_ready = sem("moe_sum_ready")
        out_done = sem("output_written")
        dbg_sem = sem("dbg")

        block = ctx.enter_context(nc.Block())

        def act_norm(act, order, k):
            if k:
                act.wait_ge(x_ready, 2 * k)
            else:
                act.wait_ge(s_x, 16)
                act.wait_ge(s_init, 32)
            for c in range(NC):
                order.mark(act.activation(xs[:, c, :], x_rows[:, c, :], ACT.Square,
                                          accum_out=sumsq[:, c:c + 1]))
            order.join()
            act.activation(root, sumsq, ACT.Sqrt, scale=1.0 / D, bias=eps_col).then_inc(rms_ready, 1)

        def dve_norm(dve, order, k, gain):
            dve.wait_ge(rms_ready, k + 1)
            order.then(dve.reciprocal(rstd, root))
            for c in range(NC):
                dve.tensor_scalar(xs[:, c, :], x_rows[:, c, :], rstd[:, c:c + 1], None,
                                  ALU.mult).then_inc(scaled, 1)
            for c in range(NC):
                for q in range(2):
                    i = 2 * c + q
                    dve.wait_ge(norm_t, 4 * k + i + 1)
                    dve.tensor_tensor(xn[:, 4 * q:4 * q + 4, c * P:(c + 1) * P],
                                      ps[:, i, :].rearrange("p (k n) -> p k n", k=4),
                                      along(gain[:, 4 * q:4 * q + 4], P), ALU.mult).then_inc(xn_ready, 1)

        def pe_norm(pe, k):
            for c in range(NC):
                pe.wait_ge(scaled, 2 * k + c + 1)
                for q in range(2):
                    for j in range(4):
                        f = (4 * q + j) * P
                        last = pe.transpose(ps[:, 2 * c + q, j * P:(j + 1) * P], xs[:, c, f:f + P], ident)
                    last.then_inc(norm_t, 1)

        def pe_out(pe, k, ready):
            for s in range(2):
                pe.wait_ge(loaded[s], ready)
            for c in range(NC):
                for h in range(2):
                    w = slot_tiles(h)
                    for j in range(KT):
                        last = pe.matmul(ps[:, 4 + 2 * c + h, :], y8[:, j, c * P:(c + 1) * P], w[:, j, :],
                                         start=j == 0, stop=j == KT - 1)
                last.then_inc(y_done, 1)

        def act_post(act, order, k, banks=True):
            for c in range(NC):
                act.wait_ge(y_done, 2 * k + c + 1)
                order.mark(act.activation(xs[:, c, :].rearrange("p (a n) -> p a n", a=2),
                                          ps[:, 4 + 2 * c:6 + 2 * c, :], ACT.Square,
                                          accum_out=sumsq[:, c:c + 1]))
            order.join()
            act.activation(root, sumsq, ACT.Sqrt, scale=1.0 / D, bias=eps_col).then_inc(out_root, 1)

        def dve_post(dve, order, k):
            dve.wait_ge(out_root, k + 1)
            order.then(dve.reciprocal(rstd, root))
            dve.wait_ge(s_gain, 16 * (k + 1))
            for c in range(NC):
                order.mark(dve.scalar_tensor_tensor(
                    xs[:, c, :].rearrange("p (a n) -> p a n", a=2), ps[:, 4 + 2 * c:6 + 2 * c, :],
                    rstd[:, c:c + 1], gain_rows[:, :].rearrange("p (a n) -> p a n", a=2), ALU.mult, ALU.mult))
            order.join()
            for c in range(NC):
                dve.tensor_tensor(x_rows[:, c, :], x_rows[:, c, :], xs[:, c, :], ALU.add).then_inc(x_ready, 1)

        eps_col = const("eps")[:, 0:1]
        gn_eps_col = const("eps")[:, 1:2]
        mask_ar = consts[:, CONST_AT["lt"][0]:CONST_AT["lt"][0] + 2 * P].bitcast(I32)

        def pe_mix0(pe):
            pe.wait_ge(s_init, 32)
            pe_norm(pe, 0)
            pe.wait_ge(xn_ready, 4)
            for i in range(18):
                job = i // 2
                if i % 4 == 0:
                    pe.wait_ge(loaded[i // 4], 16)
                if i % 2 == 0 and job >= 4:
                    pe.wait_ge(in_act if job % 2 else in_dve, job // 2 - 1)
                w = slot_tiles(i // 4)
                for j in range(KT):
                    last = pe.matmul(ps[:, job % 4, (i % 2) * T:(i % 2) * T + T],
                                     w[:, j, (i % 4) * P:(i % 4) * P + P], xn[:, j, :],
                                     start=j == 0, stop=j == KT - 1)
                if i % 2 == 1:
                    last.then_inc(in_done, 1)
            pe.wait_ge(loaded[5], 16)
            for c in range(NC):
                for h in range(2):
                    w = slot_tiles(4)[:, :, T:2 * T] if h == 0 else slot_tiles(5, n=T)
                    for j in range(KT):
                        last = pe.matmul(ps[:, 4 + c, h * T:(h + 1) * T], xn[:, j, c * P:(c + 1) * P],
                                         w[:, j, :], start=j == 0, stop=j == KT - 1)
                last.then_inc(in_done, 1)
            pe.wait_ge(s_b2, 16 * 6)
            pe.wait_ge(lora_act, 1)
            pe.wait_ge(in_act, 5)
            pe.wait_ge(in_dve, 4)
            for i in range(WT):
                last = pe.matmul(ps[:, i // 2, (i % 2) * T:(i % 2) * T + T], lora_wa[0:64, i * P:(i + 1) * P],
                                 pm[0:64, 12, :], start=True, stop=True)
            last.then_inc(wl_done, 1)
            for i in range(WT):
                last = pe.matmul(ps[:, 2 + i // 2, (i % 2) * T:(i % 2) * T + T],
                                 lora_wa[64:128, i * P:(i + 1) * P], pm[64:128, 12, :], start=True, stop=True)
            last.then_inc(al_done, 1)
            pe.wait_ge(kksq_ready, 1)
            for i in range(WT):
                last = pe.matmul(ps[:, 6 + i // 2, (i % 2) * T:(i % 2) * T + T], const("blk"), kp[:, i, :],
                                 start=True, stop=True)
            last.then_inc(kksum_done, 1)
            pe.wait_ge(sig_ready, 1)
            pe.wait_ge(mixed, 1)
            for c in range(NC):
                for i in range(WT):
                    last = pe.transpose(ps[:, c, i * P:(i + 1) * P], pm[:, 8 + i, c * P:(c + 1) * P], ident)
                last.then_inc(rows_done, 1)
            pe.wait_ge(ws_ready, 1)
            pe.wait_ge(gv_ready, 1)
            for c in range(NC):
                for g in range(WT):
                    o = ps[:, 4 + c, g * P:(g + 1) * P]
                    pe.matmul(o, v_rows[:, c, g * P:(g + 1) * P], ws_t[:, g, :], start=True, stop=False)
                    last = pe.matmul(o, const("one")[0:1, :], bs_row[0:1, g * P:(g + 1) * P],
                                     start=False, stop=True)
                last.then_inc(gs_done, 1)
            pe.wait_ge(ab_ready, 1)
            pe.wait_ge(ga_ready, 1)
            for n, src in enumerate((bt, kt)):
                for i in range(WT):
                    last = pe.transpose(ps[:, 2 + n, i * P:(i + 1) * P], src[:, i, 0:P], ident)
                last.then_inc(rows_done, 1)
            pe.wait_ge(rows_copied, 4)
            pe.wait_ge(yb_ready, 2)
            pe.wait_ge(knorm_ready, 1)
            for m in range(NH * NC):
                h, c = divmod(m, NC)
                lo = HD * (h % 2)
                if m >= 8:
                    pe.wait_ge(mat_ready, m - 7)
                for n, src in enumerate((bt, kt)):
                    last = pe.matmul(ps[:, m % 8, n * 2 * P:(n + 1) * 2 * P],
                                     src[lo:lo + HD, h // 2, c * P:(c + 1) * P],
                                     ar[lo:lo + HD, h // 2, c, :, :].rearrange("p a n -> p (a n)"),
                                     start=True, stop=True)
                last.then_inc(mat_done, 1)
            pe.wait_ge(mat_ready, NH * NC)
            for i in range(4 * LEVELS + 1):
                if i < 4 * LEVELS:
                    lev, q = divmod(i, 4)
                    pe.wait_ge(m_ready, i + 1)
                    if i >= 2:
                        pe.wait_ge(v_ready, i - 1)
                    if lev > 1:
                        pe.wait_ge(t_copied, i - 7)
                    elif lev == 1:
                        pe.wait_ge(v_ready, i - 3)
                    for j in range(4):
                        o = ps[:, i % 2, j * P:(j + 1) * P]
                        if lev == 0:
                            last = pe.transpose(o, inv_m[:, q, j, :], ident)
                        else:
                            last = pe.matmul(o, inv_m[:, q, j, :], inv_t[:, q, j, :], start=True, stop=True)
                    last.then_inc(u_done, 1)
                n = i - 1
                if n >= 4:
                    lev, q = divmod(n, 4)
                    pe.wait_ge(v_ready, n + 1)
                    if lev > 1:
                        pe.wait_ge(tt_copied, n - 7)
                    b = 2 + 2 * (n % 3)
                    if n >= 7:
                        pe.wait_ge(tt_copied, n - 6)
                        pe.wait_ge(t_copied, min(n - 6, 20))
                    for j in range(4):
                        if lev < LEVELS - 1:
                            pe.matmul(ps[:, b, j * P:(j + 1) * P], inv_tt[:, q, j, :], inv_v[:, q, j, :],
                                      start=True, stop=True)
                        last = pe.matmul(ps[:, b + 1, j * P:(j + 1) * P], inv_v[:, q, j, :],
                                         inv_tt[:, q, j, :], start=True, stop=True)
                    last.then_inc(tt_done, 1)
            pe.wait_ge(tt_copied, 24)
            for c in range(NC):
                if c:
                    pe.wait_ge(st_ready, 2)
                for h in range(NH):
                    if c and h % 2 == 0:
                        pe.matmul(ps[:, 0, h * HD:(h + 2) * HD], ar[:, h // 2, c, 0, :],
                                  state[:, h // 2, :, :].rearrange("p a n -> p (a n)"), start=True, stop=False)
                    last = pe.matmul(ps[:, 0, h * HD:(h + 1) * HD], mats[:, 2 * h + c, 2, :],
                                     v_tok[:, c, h * HD:(h + 1) * HD], start=c == 0, stop=c == 0 or h % 2 == 1)
                last.then_inc(rhs_done, 1)
                pe.wait_ge(rhs_ready, c + 1)
                for h in range(NH):
                    m = 2 * h + c
                    last = pe.matmul(ps[:, 1, h * HD:(h + 1) * HD], inv_tt[:, m // 4, m % 4, :],
                                     rhs_tok[:, h * HD:(h + 1) * HD], start=True, stop=True)
                last.then_inc(sa_done, 1)
                pe.wait_ge(sa_ready, c + 1)
                if c == 0:
                    for h in range(NH):
                        lo, o = HD * (h % 2), ps[HD * (h % 2):HD * (h % 2) + HD, 2, (h // 2) * HD:(h // 2 + 1) * HD]
                        hs = slice(h * HD, (h + 1) * HD)
                        pe.matmul(o, bk_tok[:, 0, hs], sa_tok[:, hs], start=True, stop=False)
                        last = pe.matmul(o, bk_tok[:, 1, hs], v_tok[:, 0, hs], start=False, stop=True)
                    last.then_inc(st_done, 1)
                for h in range(NH):
                    lo, m = HD * (h % 2), 2 * h + c
                    if c and h % 2 == 0:
                        pe.matmul(ps[:, 4 + c, (h // 2) * P:(h // 2 + 1) * P],
                                  state[:, h // 2, :, :].rearrange("p a n -> p (a n)"),
                                  ar[:, h // 2, c, 1, :], start=True, stop=False)
                    o = ps[lo:lo + HD, 4 + c, (h // 2) * P:(h // 2 + 1) * P]
                    hs = slice(h * HD, (h + 1) * HD)
                    pe.matmul(o, sa_tok[:, hs], mats[:, m, 1, :], start=c == 0, stop=False)
                    last = pe.matmul(o, v_tok[:, c, hs], mats[:, m, 3, :], start=False, stop=True)
                last.then_inc(yk_done, 1)
            def head_sums(src, b):
                for i in range(WT):
                    last = pe.matmul(ps[:, b + i // 2, (i % 2) * T:(i % 2) * T + T], const("blk"), src[:, i, :],
                                     start=True, stop=True)
                return last
            pe.wait_ge(bonus_ready, 1)
            head_sums(bonus_in, 0)
            for i in range(WT):
                last = pe.matmul(ps[:, 2 + i // 2, (i % 2) * T:(i % 2) * T + T], lora_g[:, i * P:(i + 1) * P],
                                 pm[:, 13, :], start=True, stop=True)
            last.then_inc(bg_done, 1)
            pe.wait_ge(ysum_in, 1)
            head_sums(y_cols, 6).then_inc(ysum_done, 1)
            pe.wait_ge(ysum_in, 2)
            head_sums(y_sq, 4).then_inc(ysum_done, 1)
            pe.wait_ge(ya_ready, 1)
            pe_out(pe, 0, 32)

        def act_mix0(act, order):
            act_norm(act, order, 0)
            for job in (1, 3, 5):
                act.wait_ge(in_done, job + 1)
                act.activation(praw[:, 2 * job:2 * job + 2, :], ps[:, job % 4, :].rearrange("p (a n) -> p a n", a=2),
                               ACT.Copy).then_inc(in_act, 1)
            for job in (7, 8):
                act.wait_ge(in_done, job + 1)
                act.activation(u_cols[:, 2 * job - 14:2 * job - 12, :],
                               ps[:, job % 4, :].rearrange("p (a n) -> p a n", a=2),
                               ACT.Gelu_apprx_tanh).then_inc(in_act, 1)
            for c in range(NC):
                act.wait_ge(in_done, 10 + c)
                act.activation(v_rows[:, c, :], ps[:, 4 + c, :], ACT.Gelu_apprx_tanh).then_inc(in_act, 1)
            act.wait_ge(lora_mixed, 2)
            order.mark(act.activation(pm[:, 13, :], pm[:, 13, :], ACT.Sigmoid))
            order.mark(act.activation(pm[0:64, 12, :], pm[0:64, 12, :], ACT.Tanh))
            order.join()
            act.nop().then_inc(lora_act, 1)
            act.wait_ge(wl_done, 1)
            act.wait_ge(mixed, 1)
            for i in range(WT):
                order.mark(act.activation(sig_w[:, i, :], ps[:, i // 2, (i % 2) * T:(i % 2) * T + T], ACT.Sigmoid,
                                          bias=vec("w0")[:, i:i + 1]))
            order.join()
            act.nop().then_inc(sig_ready, 1)
            act.wait_ge(al_done, 1)
            for i in range(WT):
                order.mark(act.activation(gate_a[:, i, :], ps[:, 2 + i // 2, (i % 2) * T:(i % 2) * T + T],
                                          ACT.Sigmoid, bias=vec("a0")[:, i:i + 1]))
            order.join()
            act.nop().then_inc(ga_ready, 1)
            act.wait_ge(kksum_done, 1)
            act.activation(knorm, ps[:, 6:8, :].rearrange("p b (a n) -> p (b a) n", a=2), ACT.Sqrt)\
                .then_inc(knorm_ready, 1)
            act.wait_ge(gv_stats, 1)
            act.activation(bn2[:, :, 1], bn2[:, :, 1], ACT.Sqrt, bias=eps_col).then_inc(gv_root, 1)
            for c in range(NC):
                act.wait_ge(rows_done, c + 1)
                act.activation(v_tok[:, c, :], ps[:, c, :], ACT.Copy).then_inc(rows_copied, 1)
            act.wait_ge(cs_ready, 1)
            act.activation(e_dec, csc, ACT.Exp, scale=-K_DECAY).then_inc(exps_ready, 1)
            act.activation(e_prev, csm, ACT.Exp, scale=-K_DECAY).then_inc(exps_ready, 1)
            act.activation(e_inv, csc, ACT.Exp, scale=K_DECAY).then_inc(exps_ready, 1)
            act.wait_ge(half_ready, 1)
            act.activation(state_scale, state_scale, ACT.Exp, scale=-K_DECAY).then_inc(scale_ready, 1)
            for n in range(2):
                act.wait_ge(rows_done, 3 + n)
                act.activation(bk_tok[:, n, :], ps[:, 2 + n, :], ACT.Copy).then_inc(rows_copied, 1)
            for n in range(4, 4 * (LEVELS - 1)):
                act.wait_ge(tt_done, n - 3)
                act.activation(inv_t[:, n % 4, :, :].rearrange("p a n -> p (a n)"), ps[:, 2 + 2 * (n % 3), :],
                               ACT.Copy).then_inc(t_copied, 1)
            for c in range(NC):
                act.wait_ge(rhs_done, c + 1)
                act.activation(rhs_tok, ps[:, 0, :], ACT.Copy).then_inc(rhs_ready, 1)
                act.wait_ge(sa_done, c + 1)
                act.activation(sa_tok, ps[:, 1, :], ACT.Copy).then_inc(sa_ready, 1)
            act.wait_ge(gn_root, 1)
            order.then(act.activation(y_sq, y_cols, ACT.Square))
            act.nop().then_inc(ysum_in, 1)
            act.wait_ge(ysum_done, 2)
            order.then(act.activation(y_sq, ps[:, 4:6, :].rearrange("p b (a n) -> p (b a) n", a=2), ACT.Sqrt,
                                      scale=1.0 / HD, bias=gn_eps_col))
            act.nop().then_inc(gn_root, 1)
            act_post(act, order, 0)

        def dve_mix0(dve, order):
            dve.wait_ge(s_init, 32)
            dve.wait_ge(s_x, 16)
            dve_norm(dve, order, 0, vec("g_mix0"))
            for job in (0, 2, 4, 6):
                dve.wait_ge(in_done, job + 1)
                dve.tensor_copy(praw[:, 2 * job:2 * job + 2, :],
                                ps[:, job % 4, :].rearrange("p (a n) -> p a n", a=2)).then_inc(in_dve, 1)
            dve.wait_ge(in_act, 3)
            dve.wait_ge(in_dve, 4)
            def mix(lo, hi, signal):
                order.mark(dve.tensor_tensor(pm[:, lo:hi, 1:T], praw[:, lo:hi, 0:T - 1], praw[:, lo:hi, 1:T],
                                             ALU.subtract))
                order.then(dve.tensor_scalar(pm[:, lo:hi, 0], praw[:, lo:hi, 0], -1.0, None, ALU.mult))
                for i in range(lo, hi):
                    ins = dve.scalar_tensor_tensor(pm[:, i, :], pm[:, i, :], vec("mu")[:, i:i + 1],
                                                   praw[:, i, :], ALU.mult, ALU.add)
                    if signal is None:
                        order.mark(ins)
                    else:
                        ins.then_inc(signal, 1)
            mix(12, 14, lora_mixed)
            mix(4, 8, None)
            mix(0, 4, None)
            mix(8, 12, None)
            order.join()
            dve.nop().then_inc(mixed, 1)
            dve.wait_ge(in_done, 11)
            k_cols, r_cols = pm[:, 4:8, :], pm[:, 0:4, :]
            order.then(dve.tensor_tensor(kk, k_cols, along(vec("k_k"), T), ALU.mult))
            dve.tensor_tensor(kp, kk, kk, ALU.mult).then_inc(kksq_ready, 1)
            dve.wait_ge(s_b2, 16 * 6)
            dve.wait_ge(in_act, 7)
            dve.tensor_tensor(ws_t, ws_t, across(const("le"), WT), ALU.mult).then_inc(ws_ready, 1)
            for c in range(NC):
                for g in range(WT):
                    order.mark(dve.bn_stats(bn6[:, c * WT + g, :], v_rows[:, c, g * P:(g + 1) * P]))
            order.join()
            for i in range(NC * WT):
                order.mark(dve.bn_aggr(bn2[:, i, :], bn6[:, i, :]))
            order.join()
            dve.nop().then_inc(gv_stats, 1)
            dve.wait_ge(sig_ready, 1)
            for i in range(WT):
                for c in range(NC):
                    s = slice(c * P, (c + 1) * P)
                    order.mark(dve.tensor_tensor_scan(cs[:, i, s], const("one")[:, 0:1].broadcast_to([P, P]),
                                                      sig_w[:, i, s], 0.0, ALU.mult, ALU.add))
            order.join()
            cs4 = cs.rearrange("p i (c n) -> p i c n", c=NC)
            order.then(dve.tensor_scalar(half_sum, cs4[:, :, :, P - 1], 0.5, None, ALU.mult))
            for c in range(NC):
                order.mark(dve.tensor_tensor(csc.rearrange("p i (c n) -> p i c n", c=NC)[:, :, c, :],
                                             cs4[:, :, c, :], along(half_sum[:, :, c], P), ALU.subtract))
            order.join()
            dve.tensor_tensor(csm, csc, sig_w, ALU.subtract).then_inc(cs_ready, 1)
            dve.tensor_tensor(state_scale, half_sum[:, :, 0], half_sum[:, :, 1], ALU.add).then_inc(half_ready, 1)
            dve.wait_ge(gv_root, 1)
            order.then(dve.reciprocal(bn2[:, :, 1], bn2[:, :, 1]))
            for c in range(NC):
                for g in range(WT):
                    v = v_rows[:, c, g * P:(g + 1) * P]
                    i = c * WT + g
                    order.mark(dve.tensor_scalar(v, v, bn2[:, i, 0:1], bn2[:, i, 1:2], ALU.subtract, ALU.mult))
            order.join()
            order.then(dve.tensor_tensor(v_rows, v_rows, across(gln[:, 0, :], NC), ALU.mult))
            dve.tensor_tensor(v_rows, v_rows, across(gln[:, 1, :], NC), ALU.add).then_inc(gv_ready, 1)
            dve.wait_ge(knorm_ready, 1)
            order.then(dve.tensor_scalar(knorm, knorm, 1e-12, None, ALU.max))
            order.then(dve.reciprocal(knorm, knorm))
            order.then(dve.tensor_tensor(kk, kk, knorm, ALU.mult))
            dve.wait_ge(ga_ready, 1)
            for i in range(WT):
                order.mark(dve.tensor_scalar(knorm[:, i, :], gate_a[:, i, :], -1.0, vec("k_a")[:, i:i + 1],
                                             ALU.add, ALU.mult))
            order.join()
            order.then(dve.scalar_tensor_tensor(kp, knorm, 1.0, k_cols, ALU.add, ALU.mult))
            order.then(dve.tensor_tensor(bonus_in, r_cols, kp, ALU.mult))
            dve.tensor_tensor(bonus_in, bonus_in, along(vec("r_k"), T), ALU.mult).then_inc(bonus_ready, 1)
            dve.wait_ge(exps_ready, 3)
            def by_chunk(x):
                return x.rearrange("p i (c n) -> p i c n", c=NC)
            order.mark(dve.scalar_tensor_tensor(ar[:, :, :, 0, :], by_chunk(kk), -1.0, by_chunk(e_prev),
                                                ALU.mult, ALU.mult))
            order.mark(dve.tensor_tensor(ar[:, :, :, 1, :], by_chunk(r_cols), by_chunk(e_dec), ALU.mult))
            order.mark(dve.tensor_tensor(kt, kp, e_inv, ALU.mult))
            order.then(dve.tensor_tensor(bt, kk, gate_a, ALU.mult))
            order.then(dve.tensor_tensor(bt, bt, e_inv, ALU.mult))
            dve.nop().then_inc(ab_ready, 1)
            for c in range(NC):
                dve.wait_ge(gs_done, c + 1)
                dve.tensor_tensor(y8[:, WT:KT, c * P:(c + 1) * P], u_cols[:, :, c * P:(c + 1) * P],
                                  ps[:, 4 + c, :].rearrange("p (g n) -> p g n", g=WT), ALU.mult)\
                    .then_inc(yb_ready, 1)
            for m in range(NH * NC):
                dve.wait_ge(mat_zero, m + 1)
                dve.wait_ge(mat_done, m + 1)
                for n in range(2):
                    ins = dve.copy_predicated(mats[:, m, 2 * n:2 * n + 2, :].rearrange("p a n -> p (a n)"),
                                              mask_ar, ps[:, m % 8, n * 2 * P:(n + 1) * 2 * P])
                    if n == 0:
                        order.mark(ins)
                    else:
                        ins.then_inc(mat_ready, 1)
            order.join()
            id4 = across(ident, 4)
            for i in range(4 * LEVELS + 1):
                if i < 4 * LEVELS:
                    lev, q = divmod(i, 4)
                    dve.wait_ge(u_done, i + 1)
                    u = ps[:, i % 2, :].rearrange("p (a n) -> p a n", a=4)
                    if lev == 0:
                        order.mark(dve.tensor_tensor(inv_tt[:, q], inv_m[:, q], id4, ALU.add))
                        order.join()
                        dve.tensor_tensor(inv_t[:, q], u, id4, ALU.add).then_inc(v_ready, 1)
                    else:
                        if lev > 1:
                            dve.wait_ge(tt_done, i - 7)
                        dve.tensor_tensor(inv_v[:, q], u, id4, ALU.add).then_inc(v_ready, 1)
                n = i - 1
                if n >= 4:
                    dve.wait_ge(tt_done, n - 3)
                    dve.tensor_copy(inv_tt[:, n % 4].rearrange("p a n -> p (a n)"), ps[:, 3 + 2 * (n % 3), :])\
                        .then_inc(tt_copied, 1)
            order.then(dve.memset(state, 0.0))
            dve.wait_ge(st_done, 1)
            dve.wait_ge(scale_ready, 1)
            for n in range(2):
                lo = slice(n * HD, (n + 1) * HD)
                dve.tensor_tensor(state[lo, :, n, :], ps[lo, 2, 0:WT * HD].rearrange("p (a n) -> p a n", a=WT),
                                  along(state_scale[lo], HD), ALU.mult).then_inc(st_ready, 1)
            dve.wait_ge(yk_done, 2)
            for c in range(NC):
                order.mark(dve.tensor_copy(y_cols[:, :, c * P:(c + 1) * P],
                                           ps[:, 4 + c, :].rearrange("p (a n) -> p a n", a=WT)))
            order.join()
            dve.nop().then_inc(ysum_in, 1)
            dve.wait_ge(ysum_done, 1)
            def bank2(b):
                return ps[:, b:b + 2, :].rearrange("p b (a n) -> p (b a) n", a=2)
            order.then(dve.scalar_tensor_tensor(y_cols, bank2(6), -1.0 / HD, y_cols, ALU.mult, ALU.add))
            dve.nop().then_inc(gn_root, 1)
            dve.wait_ge(bg_done, 1)
            order.then(dve.tensor_tensor(bonus_in, bank2(0), pm[:, 8:12, :], ALU.mult))
            dve.wait_ge(gn_root, 2)
            order.then(dve.reciprocal(y_sq, y_sq))
            order.then(dve.tensor_tensor(y_cols, y_cols, y_sq, ALU.mult))
            for i in range(WT):
                order.mark(dve.tensor_scalar(y_cols[:, i, :], y_cols[:, i, :], vec("ln_w")[:, i:i + 1],
                                             vec("ln_b")[:, i:i + 1], ALU.mult, ALU.add))
            order.join()
            order.then(dve.tensor_tensor(y_cols, y_cols, bonus_in, ALU.add))
            dve.tensor_tensor(y8[:, 0:WT, :], bank2(2), y_cols, ALU.mult).then_inc(ya_ready, 1)
            dve_post(dve, order, 0)

        def pool_mix0(pool, order):
            pool.wait_ge(gs_done, 2)
            pool.dma_start(gain_rows[:, :], t["gain_mix0"]).then_inc(s_gain, 16)
            pool.wait_ge(ab_ready, 1)
            for m in range(NH * NC):
                pool.memset(mats[:, m, :, :], 0.0).then_inc(mat_zero, 1)
            pool.wait_ge(mat_ready, NH * NC)
            for i in range(4 * LEVELS):
                lev, q = divmod(i, 4)
                if lev:
                    pool.wait_ge(u_done, i - 3)
                    if lev == 1:
                        pool.wait_ge(v_ready, i - 3)
                pool.tensor_tensor(inv_m[:, q], mats[:, 4 * q:4 * q + 4, 0, :], across(inv_mask[:, lev, :], 4),
                                   ALU.mult).then_inc(m_ready, 1)

        def ffn_products(pe, f):
            for g in range(2):
                for j in range(KT):
                    last = pe.matmul(ps[:, f % 2, g * T:(g + 1) * T], f_w[f % 4][0][:, g, j, :], xn[:, j, :],
                                     start=j == 0, stop=j == KT - 1)
            last.then_inc(f_prod, 1)

        def ffn_down(pe, f, first=False, final=False):
            for c in range(NC):
                for h in range(2):
                    last = pe.matmul(ps[:, 4 + 2 * c + h, :], f_act[f % 2][:, c * P:(c + 1) * P],
                                     f_w[f % 4][1][:, h * NB:(h + 1) * NB], start=first, stop=final)
                if final:
                    last.then_inc(y_done, 1)
            if not final:
                last.then_inc(f_free, 1)

        def pe_ffn(pe):
            pe_norm(pe, 1)
            pe.wait_ge(xn_ready, 8)
            for f in range(2):
                pe.wait_ge(f_loaded[f], 48)
                ffn_products(pe, f)
            pe.wait_ge(f_act_ready, 1)
            ffn_down(pe, 0, first=True)
            with pe.Fori(0, (FT - 2) // 4) as g:
                for f in range(2, 6):
                    pe.wait_ge(f_loaded[f % 4], g * 48 + 48 * (1 + f // 4))
                    ffn_products(pe, f)
                    pe.wait_ge(f_act_ready, g * 4 + f)
                    ffn_down(pe, f - 1)
            pe.wait_ge(f_act_ready, FT)
            ffn_down(pe, FT - 1, final=True)

        def act_ffn(act, order):
            act_norm(act, order, 1)

            def silu(b):
                act.activation(f_silu[b], ps[:, b, 0:T], ACT.Silu).then_inc(f_silu_ready, 1)
            for b in range(2):
                act.wait_ge(f_prod, b + 1)
                silu(b)
            with act.Fori(0, FT // 2 - 1) as g:
                for b in range(2):
                    act.wait_ge(f_prod, g * 2 + (b + 3))
                    act.wait_ge(f_act_ready, g * 2 + (b + 1))
                    silu(b)
            act_post(act, order, 1)

        def dve_ffn(dve, order):
            dve_norm(dve, order, 1, vec("g_ffn0"))

            def times_up(b):
                dve.tensor_tensor(f_act[b], f_silu[b], ps[:, b, T:2 * T], ALU.mult).then_inc(f_act_ready, 1)
            for b in range(2):
                dve.wait_ge(f_silu_ready, b + 1)
                times_up(b)
            with dve.Fori(0, FT // 2 - 1) as g:
                for b in range(2):
                    dve.wait_ge(f_silu_ready, g * 2 + (b + 3))
                    dve.wait_ge(f_free, g * 2 + (b + 1))
                    times_up(b)
            dve_post(dve, order, 1)

        def sp_ffn(sp):
            sp.wait_ge(ya_ready, 1)
            gate_d = t["l0_ffn_w_gate"].rearrange("(k p) n -> p k n", p=P)
            up_d = t["l0_ffn_w_up"].rearrange("(k p) n -> p k n", p=P)
            down_d = t["l0_ffn_w_down"]

            def load(b, f):
                sp.dma_start(f_w[b][0][:, 0, :, :], gate_d[:, :, bass.ds(f * P, P)]).then_inc(f_loaded[b], 16)
                sp.dma_start(f_w[b][0][:, 1, :, :], up_d[:, :, bass.ds(f * P, P)]).then_inc(f_loaded[b], 16)
                sp.dma_start(f_w[b][1], down_d[bass.ds(f * P, P), :]).then_inc(f_loaded[b], 16)
            for f in range(4):
                load(f, f)
            for f in range(4, 6):
                sp.wait_ge(f_free, f - 3)
                load(f % 4, f)
            with sp.Fori(0, (FT - 6) // 4) as g:
                for f in range(6, 10):
                    sp.wait_ge(f_free, g * 4 + (f - 3))
                    load(f % 4, g * 4 + f)

        TWO_PI = (6.28125, 1.9350051879882812e-3, 3.0199159819567529e-7)
        MAGIC = 1.5 * 2.0 ** 23
        PI_LOW = 3.14159250

        def act_angles(act):
            act.wait_ge(s_init, 32)
            act.activation(s5_dt, vec("log_dt"), ACT.Exp).then_inc(ang_ready, 1)
            act.wait_ge(ang_reduced, 1)
            act.activation(s5_mag, s5_mag, ACT.Exp).then_inc(rot_ready, 1)
            act.activation(rot_s[:, :, :], turns[:, :, :], ACT.Sin).then_inc(rot_ready, 1)
            act.activation(rot_c[:, :, :], angle[:, :, :], ACT.Sin, scale=-1.0, bias=const("eps")[:, 2:3])\
                .then_inc(rot_ready, 1)

        def dve_angles(dve, order):
            dve.wait_ge(s_init, 32)
            dve.wait_ge(ang_ready, 1)
            order.mark(dve.tensor_tensor(s5_mag, vec("a_re"), s5_dt, ALU.mult))
            order.then(dve.tensor_tensor(angle[:, 0, :], vec("a_im"), s5_dt, ALU.mult))
            for k in range(1, LEVELS + 1):
                order.mark(dve.tensor_scalar(angle[:, k, :], angle[:, 0, :], float(2 ** k), None, ALU.mult))
            order.join()
            order.then(dve.tensor_scalar(turns[:, :, :], angle[:, :, :], 1.0 / (2 * math.pi), MAGIC,
                                         ALU.mult, ALU.add))
            order.then(dve.tensor_scalar(turns[:, :, :], turns[:, :, :], MAGIC, None, ALU.subtract))
            for part in TWO_PI:
                order.then(dve.scalar_tensor_tensor(angle[:, :, :], turns[:, :, :], -part, angle[:, :, :],
                                                    ALU.mult, ALU.add))
            order.then(dve.tensor_scalar(turns[:, :, :], angle[:, :, :], PI_LOW, -PI_LOW, ALU.min, ALU.max))
            dve.scalar_tensor_tensor(angle[:, :, :], turns[:, :, :], -1.0, turns[:, :, :],
                                     ALU.mult, ALU.max).then_inc(ang_reduced, 1)
            dve.wait_ge(rot_ready, 3)
            lr, li = vec("a_re"), vec("a_im")
            order.mark(dve.tensor_tensor(s5_nr, s5_mag, rot_c[:, 0, :], ALU.mult))
            order.mark(dve.tensor_tensor(s5_ni, s5_mag, rot_s[:, 0, :], ALU.mult))
            order.mark(dve.tensor_tensor(f_re, lr, lr, ALU.mult))
            order.then(dve.tensor_tensor(f_im, li, li, ALU.mult))
            order.mark(dve.tensor_scalar(s5_nr, s5_nr, -1.0, None, ALU.add))
            order.then(dve.tensor_tensor(s5_den, f_re, f_im, ALU.add))
            order.mark(dve.reciprocal(s5_den, s5_den))
            order.mark(dve.tensor_tensor(f_re, s5_nr, lr, ALU.mult))
            order.mark(dve.tensor_tensor(f_im, s5_ni, lr, ALU.mult))
            order.join()
            order.mark(dve.tensor_tensor(s5_ni, s5_ni, li, ALU.mult))
            order.then(dve.tensor_tensor(s5_nr, s5_nr, li, ALU.mult))
            order.mark(dve.tensor_tensor(f_re, f_re, s5_ni, ALU.add))
            order.then(dve.tensor_tensor(f_im, f_im, s5_nr, ALU.subtract))
            order.mark(dve.tensor_tensor(f_re, f_re, s5_den, ALU.mult))
            order.then(dve.tensor_tensor(f_im, f_im, s5_den, ALU.mult))

        def pool_rotations(pool, order):
            pool.wait_ge(ya_ready, 1)
            pool.wait_ge(rot_ready, 3)
            order.mark(pool.memset(cos_t[:, :, 0:1], 1.0))
            order.then(pool.memset(sin_t[:, :, 0:1], 0.0))
            for k in range(LEVELS + 1):
                m = 2 ** k
                lo, hi = slice(0, m), slice(m, 2 * m)
                c, s = along(rot_c[:, k, :], m), along(rot_s[:, k, :], m)
                t1, t2 = (x[:, 0:S5_TILES * m].rearrange("p (j n) -> p j n", j=S5_TILES) for x in rot_tmp)
                order.mark(pool.tensor_tensor(t1, cos_t[:, :, lo], c, ALU.mult))
                order.then(pool.tensor_tensor(t2, sin_t[:, :, lo], s, ALU.mult))
                order.then(pool.tensor_tensor(cos_t[:, :, hi], t1, t2, ALU.subtract))
                order.mark(pool.tensor_tensor(t1, cos_t[:, :, lo], s, ALU.mult))
                order.then(pool.tensor_tensor(t2, sin_t[:, :, lo], c, ALU.mult))
                order.then(pool.tensor_tensor(sin_t[:, :, hi], t1, t2, ALU.add))
            pool.nop().then_inc(rot_table, 1)

        def sp_mix1(sp):
            w = t["l1_w_in"].rearrange("(k p) n -> p k n", p=P)
            for s in range(4):
                if s == 0:
                    sp.wait_ge(y_done, 2)
                sp.dma_start(slot_tiles(s), w[:, :, s * NB:(s + 1) * NB]).then_inc(loaded[s], 16)
            sp.wait_ge(y_done, 4)
            sp.dma_start(b_in, t["s5_b"].rearrange("a p j n -> p a j n")).then_inc(s5_loaded, 16)
            sp.dma_start(c_in, t["s5_c"].rearrange("a p j n -> p a j n")).then_inc(s5_loaded, 16)
            w = t["l1_w_out"].rearrange("(k p) n -> p k n", p=P)
            sp.wait_ge(dt_done, 1)
            sp.dma_start(glu_w, t["l1_s5_glu_w"].rearrange("(k p) n -> p k n", p=P)).then_inc(glu_loaded, 16)
            for s in range(2):
                sp.dma_start(slot_tiles(s), w[:, :, s * NB:(s + 1) * NB]).then_inc(loaded[s], 16)

        def pe_mix1(pe):
            pe_norm(pe, 2)
            pe.wait_ge(xn_ready, 12)

            def in_job(job):
                if job >= 4:
                    pe.wait_ge(p1_ready, job - 3)
                for i in (2 * job, 2 * job + 1):
                    s = i // 4
                    pe.wait_ge(loaded[s], 48 if s < 2 else 32)
                    w = slot_tiles(s)
                    for j in range(KT):
                        last = pe.matmul(ps[:, 4 + job % 4, (i % 2) * T:(i % 2) * T + T],
                                         w[:, j, (i % 4) * P:(i % 4) * P + P], xn[:, j, :],
                                         start=j == 0, stop=j == KT - 1)
                last.then_inc(p1_done, 1)

            def bu(g):
                if g:
                    pe.wait_ge(v_done, g)
                for q in range(4):
                    for n in range(2):
                        last = pe.matmul(ps[:, q, n * T:(n + 1) * T], b_in[32 * q:32 * q + 32, n, g, :],
                                         p1[32 * q:32 * q + 32, g, :], start=True, stop=True)
                last.then_inc(bu_done, 1)

            def s5_y(g):
                pe.wait_ge(c_ready, 1)
                pe.wait_ge(q_done, g + 1)
                for q in range(4):
                    o = ps[32 * q:32 * q + 32, 4 + g // 2, (g % 2) * T:(g % 2) * T + T]
                    pe.matmul(o, c_out[:, 0, 4 * g + q, :], q_re[:, q, :], start=True, stop=False)
                    last = pe.matmul(o, c_out[:, 1, 4 * g + q, :], q_im[:, q, :], start=False, stop=True)
                last.then_inc(y5_done, 1)

            in_job(0)
            in_job(1)
            pe.wait_ge(p1_ready, 2)
            pe.wait_ge(s5_loaded, 32)
            bu(0)
            for job in range(2, 8):
                in_job(job)
            pe.wait_ge(p1_ready, 5)
            pe.wait_ge(s_small, 32)
            for c in range(NC):
                for j in range(KT):
                    last = pe.matmul(ps[:, 4, c * NH:(c + 1) * NH], xn[:, j, c * P:(c + 1) * P],
                                     w_small[:, 0, j, :], start=j == 0, stop=j == KT - 1)
            last.then_inc(dt_done, 1)
            bu(1)
            pe.wait_ge(p1_ready, 8)
            pe.wait_ge(xc_ready, 2)
            for c in range(NC):
                for i in range(WT):
                    last = pe.transpose(ps[:, 6 + c, i * P:(i + 1) * P], xc[:, i, c * P:(c + 1) * P], ident)
                last.then_inc(jobs, 1)
            pe.wait_ge(ssd_dve, 1)
            for g in range(2):
                last = pe.transpose(ps[:, 6, g * P:(g + 1) * P], xc[:, WT + g, 0:P], ident)
            last.then_inc(jobs, 1)
            for n in range(4):
                c, g = divmod(n, 2)
                pe.wait_ge(seg_ready, c + 1)
                if n == 0:
                    pe.wait_ge(ssd_dve, 2)
                else:
                    pe.wait_ge(ssd_act, n)
                for h in range(4):
                    last = pe.matmul(ps[:, 7 - n % 2, h * P:(h + 1) * P], seg_in[:, c, 4 * g + h, :], const("le"),
                                     start=True, stop=True)
                last.then_inc(jobs, 1)
            pe.wait_ge(ssd_act, 4)
            for c in range(NC):
                for g in range(2):
                    s = slice(c * P, (c + 1) * P)
                    last = pe.matmul(ps[:, 7, (2 * c + g) * P:(2 * c + g + 1) * P], xc[:, WT + g, s],
                                     xc[:, WT + 2 + g, s], start=True, stop=True)
            last.then_inc(jobs, 1)
            pe.wait_ge(ssd_act, 5)
            last = pe.matmul(ps[:, 6, 0:NH], const("gt"), adt[:, 0:NH], start=True, stop=True)
            last.then_inc(jobs, 1)
            s5_y(0)
            bu(2)
            s5_y(1)
            bu(3)
            pe.wait_ge(seg_ready, 3)
            pe.wait_ge(ssd_dve, 3)
            pe.wait_ge(ssd_act, 6)
            for g in range(2):
                for h in range(4):
                    last = pe.matmul(ps[:, 7 - g, h * P:(h + 1) * P], acs_in[:, 4 * g + h, :], const("le"),
                                     start=True, stop=True)
                last.then_inc(jobs, 1)
            pe.wait_ge(ssd_act, 7)
            pe.wait_ge(xdec_ready, 1)
            for g in range(2):
                last = pe.matmul(ps[:, 7, g * T:(g + 1) * T], b_rows[:, g * P:(g + 1) * P],
                                 xdec[:, g * T:(g + 1) * T], start=True, stop=True)
            last.then_inc(jobs, 1)
            s5_y(2)
            s5_y(3)
            pe.wait_ge(mats1, 4)
            pe.wait_ge(ssd_act, 9)
            pe.wait_ge(ce_ready, 1)
            for c in range(NC):
                for h in range(NH):
                    o = ps[HD * (h % 2):HD * (h % 2) + HD, 6 + c, (h // 2) * P:(h // 2 + 1) * P]
                    last = pe.matmul(o, xdt[:, c, h * HD:(h + 1) * HD], lmat[:, c, h, :],
                                     start=True, stop=c == 0)
                    if c:
                        last = pe.matmul(o, st_rows[:, h * HD:(h + 1) * HD], ce[:, h, :],
                                         start=False, stop=True)
                last.then_inc(ssd_y, 1)
            pe.wait_ge(gy_ready, 1)
            pe.wait_ge(v_done, 4)
            pe.wait_ge(glu_loaded, 16)
            for i in range(WT):
                for j in range(WT):
                    last = pe.matmul(ps[:, i // 2, (i % 2) * T:(i % 2) * T + T], glu_w[:, j, i * P:(i + 1) * P],
                                     y5[:, j, :], start=j == 0, stop=j == WT - 1)
            last.then_inc(glu_done, 1)
            pe.wait_ge(yz_ready, 1)
            for g in range(2):
                for j in range(2):
                    last = pe.matmul(ps[:, 2, g * T:(g + 1) * T], const("one"), yz_sq[:, 2 * g + j, :],
                                     start=j == 0, stop=j == 1)
            last.then_inc(yz_sum, 1)
            pe.wait_ge(yc_ready, 1)
            pe.wait_ge(yd_ready, WT)
            for s in range(2):
                pe.wait_ge(loaded[s], 64)
            pe_out(pe, 2, 64)

        def act_mix1(act, order):
            act_norm(act, order, 2)

            def copy_job(job, func):
                act.wait_ge(p1_done, job + 1)
                act.activation(p1[:, 2 * job:2 * job + 2, :],
                               ps[:, 4 + job % 4, :].rearrange("p (a n) -> p a n", a=2), func).then_inc(p1_ready, 1)
            act.wait_ge(rot_table, 1)
            for job in range(8):
                copy_job(job, ACT.Silu if job in (2, 3) else ACT.Copy)
            act.activation(a_neg, vec2(("dt_bias", "a_log")), ACT.Exp).then_inc(sp2, 1)
            act.wait_ge(sp1, 1)
            act.activation(sp_e, sp_w, ACT.Exp, scale=-1.0).then_inc(sp2, 1)
            act.wait_ge(sp1, 2)
            act.activation(sp_l, sp_w, ACT.Ln).then_inc(sp2, 1)
            for n in range(2):
                act.wait_ge(conv_done, 4 * n + 4)
                act.activation(xc[:, 4 * n:4 * n + 4, :], xc[:, 4 * n:4 * n + 4, :], ACT.Silu).then_inc(xc_ready, 1)
            act.wait_ge(jobs, 3)
            act.activation(b_rows, ps[:, 6, 0:2 * P], ACT.Copy).then_inc(ssd_act, 1)
            for n in range(4):
                c, g = divmod(n, 2)
                act.wait_ge(jobs, 4 + n)
                act.activation(lmat[:, c, 4 * g:4 * g + 4, :],
                               ps[:, 7 - n % 2, :].rearrange("p (a n) -> p a n", a=4), ACT.Exp).then_inc(ssd_act, 1)
            act.wait_ge(jobs, 9)
            act.activation(dec_s[:, 0:NH], ps[:, 6, 0:NH], ACT.Exp).then_inc(ssd_act, 1)
            for g in range(2):
                act.wait_ge(jobs, 10 + g)
                act.activation(ce[:, 4 * g:4 * g + 4, :], ps[:, 7 - g, :].rearrange("p (a n) -> p a n", a=4),
                               ACT.Exp).then_inc(ssd_act, 1)
            act.wait_ge(jobs, 12)
            act.activation(st_rows, ps[:, 7, :], ACT.Copy).then_inc(ssd_act, 1)
            act.wait_ge(y5_in, WT)
            act.activation(y5, y5, ACT.Gelu_apprx_tanh).then_inc(gy_ready, 1)
            act.wait_ge(glu_done, 1)
            for i in range(WT):
                act.activation(tmp1[:, i, :], ps[:, i // 2, (i % 2) * T:(i % 2) * T + T], ACT.Sigmoid,
                               bias=vec("glu_b")[:, i:i + 1]).then_inc(glu_sig, 1)
            act.wait_ge(yz_sum, 1)
            act.activation(yz_sq[:, 0:2, :], ps[:, 2, :].rearrange("p (a n) -> p a n", a=2), ACT.Sqrt,
                           scale=1.0 / (2 * P), bias=eps_col).then_inc(yz_root, 1)
            act_post(act, order, 2)

        def vec2(names):
            a, b = VEC_AT[names[0]][0], VEC_AT[names[1]][0] + NH
            return vecs[:, a:b]

        def dve_mix1(dve, order):
            dve_norm(dve, order, 2, vec("g_mix1"))
            dve.wait_ge(s5_loaded, 32)
            cr, ci, orr, oi = c_in[:, 0], c_in[:, 1], c_out[:, 0], c_out[:, 1]
            fr, fi = along(f_re, 32), along(f_im, 32)
            t1 = tmp1.rearrange("p a n -> p (a n)")[:, 0:S5_TILES * 32].rearrange("p (j n) -> p j n", n=32)
            order.mark(dve.tensor_tensor(orr, cr, fr, ALU.mult))
            order.then(dve.tensor_tensor(t1, ci, fi, ALU.mult))
            order.then(dve.tensor_tensor(orr, orr, t1, ALU.subtract))
            order.mark(dve.tensor_tensor(oi, cr, fi, ALU.mult))
            order.then(dve.tensor_tensor(t1, ci, fr, ALU.mult))
            dve.scalar_tensor_tensor(oi, oi, -1.0, t1, ALU.mult, ALU.subtract).then_inc(c_ready, 1)
            dve.wait_ge(c_ready, 1)

            def s5_group(g):
                js = slice(4 * g, 4 * g + 4)
                c, s = cos_t[:, js, :], sin_t[:, js, :]
                dve.wait_ge(bu_done, g + 1)
                b_re, b_im = ps[:, 0:4, 0:T], ps[:, 0:4, T:2 * T]
                order.mark(dve.tensor_tensor(v_re, b_re, c, ALU.mult))
                order.mark(dve.tensor_tensor(tmp1, b_im, s, ALU.mult))
                order.mark(dve.tensor_tensor(v_im, b_im, c, ALU.mult))
                dve.tensor_tensor(tmp2, b_re, s, ALU.mult).then_inc(v_done, 1)
                order.join()
                dve.wait_ge(v_done, g + 1)
                order.mark(dve.tensor_tensor(v_re, v_re, tmp1, ALU.add))
                order.then(dve.tensor_tensor(v_im, v_im, tmp2, ALU.subtract))
                for q in range(4):
                    mag = s5_mag[:, 4 * g + q:4 * g + q + 1].broadcast_to([P, T])
                    order.mark(dve.tensor_tensor_scan(z_re[:, q, :], mag, v_re[:, q, :], 0.0, ALU.mult, ALU.add))
                    order.mark(dve.tensor_tensor_scan(z_im[:, q, :], mag, v_im[:, q, :], 0.0, ALU.mult, ALU.add))
                order.join()
                if g:
                    dve.wait_ge(y5_done, g)
                order.mark(dve.tensor_tensor(q_re, z_re, c, ALU.mult))
                order.mark(dve.tensor_tensor(tmp1, z_im, s, ALU.mult))
                order.mark(dve.tensor_tensor(q_im, z_im, c, ALU.mult))
                order.then(dve.tensor_tensor(tmp2, z_re, s, ALU.mult))
                order.mark(dve.tensor_tensor(q_re, q_re, tmp1, ALU.subtract))
                dve.tensor_tensor(q_im, q_im, tmp2, ALU.add).then_inc(q_done, 1)
                order.join()
                dve.wait_ge(q_done, g + 1)

            dve.wait_ge(rot_table, 1)
            s5_group(0)
            taps = vec("conv_w").rearrange("p (j i) -> p j i", j=4)
            for i in range(KT):
                dve.wait_ge(p1_ready, 5 + i // 2)
                x = p1[:, 8 + i, :]
                order.mark(dve.tensor_scalar(xc[:, i, :], x, taps[:, 3, i:i + 1], vec("conv_b")[:, i:i + 1],
                                             ALU.mult, ALU.add))
            order.join()
            for back in (1, 2, 3):
                for i in range(KT):
                    x = p1[:, 8 + i, :]
                    ins = dve.scalar_tensor_tensor(xc[:, i, back:], x[:, 0:T - back], taps[:, 3 - back, i:i + 1],
                                                   xc[:, i, back:], ALU.mult, ALU.add)
                    if back < 3:
                        order.mark(ins)
                    else:
                        ins.then_inc(conv_done, 1)
                order.join()
            dve.wait_ge(dt_done, 1)
            order.then(dve.tensor_tensor(dt_v.rearrange("p (c h) -> p c h", c=NC),
                                         ps[:, 4, 0:NC * NH].rearrange("p (c h) -> p c h", c=NC),
                                         across(vec("dt_bias"), NC), ALU.add))
            dve.scalar_tensor_tensor(sp_w, dt_v, -1.0, dt_v, ALU.mult, ALU.max).then_inc(sp1, 1)
            order.then(dve.tensor_scalar(dt_v, dt_v, 0.0, None, ALU.max))
            dve.wait_ge(sp2, 2)
            dve.tensor_scalar(sp_w, sp_e, 1.0, None, ALU.add).then_inc(sp1, 1)
            dve.wait_ge(sp1, 2)
            order.then(dve.tensor_scalar(sp_m, sp_w, 1.0, None, ALU.is_equal))
            order.then(dve.scalar_tensor_tensor(adt, sp_w, -1.0, sp_m, ALU.add, ALU.add))
            order.then(dve.reciprocal(adt, adt))
            dve.wait_ge(sp2, 3)
            order.then(dve.tensor_tensor(sp_l, sp_l, sp_m, ALU.add))
            order.then(dve.tensor_tensor(sp_l, sp_l, adt, ALU.mult))
            order.then(dve.tensor_tensor(sp_l, sp_l, sp_e, ALU.mult))
            order.then(dve.tensor_tensor(dt_v, dt_v, sp_l, ALU.add))
            dve.scalar_tensor_tensor(adt.rearrange("p (c h) -> p c h", c=NC),
                                     dt_v.rearrange("p (c h) -> p c h", c=NC), -1.0,
                                     across(a_neg[:, NH:2 * NH], NC), ALU.mult, ALU.mult).then_inc(dt_ready, 1)
            for c in range(NC):
                dve.wait_ge(jobs, c + 1)
                dve.tensor_tensor(xdt[:, c, :].rearrange("p (h n) -> p h n", h=NH),
                                  ps[:, 6 + c, :].rearrange("p (h n) -> p h n", h=NH),
                                  along(dt_v[:, c * NH:(c + 1) * NH], HD), ALU.mult).then_inc(ssd_dve, 1)
            s5_group(1)
            dve.wait_ge(jobs, 8)
            dve.tensor_tensor(cb.rearrange("p c g n -> p (c g) n"),
                              ps[:, 7, :].rearrange("p (a n) -> p a n", a=4), across(const("le"), 4), ALU.mult)\
                .then_inc(ssd_dve, 1)
            dve.wait_ge(ssd_act, 6)
            dve.tensor_tensor(xdec.rearrange("p (h n) -> p h n", h=NH),
                              xdt[:, 0, :].rearrange("p (h n) -> p h n", h=NH),
                              along(dec_s[:, 0:NH], HD), ALU.mult).then_inc(xdec_ready, 1)
            s5_group(2)
            dve.wait_ge(ssd_dve, 3)
            for n in range(4):
                c, g = divmod(n, 2)
                m = lmat[:, c, 4 * g:4 * g + 4, :]
                dve.tensor_tensor(m, m, across(cb[:, c, g, :], 4), ALU.mult).then_inc(mats1, 1)
            s5_group(3)
            dve.wait_ge(ssd_act, 8)
            for g in range(2):
                m = ce[:, 4 * g:4 * g + 4, :]
                order.mark(dve.tensor_tensor(m, m, across(xc[:, WT + 2 + g, P:T], 4), ALU.mult))
            order.join()
            dve.nop().then_inc(ce_ready, 1)
            dve.wait_ge(y5_done, 4)
            for i in range(WT):
                dve.scalar_tensor_tensor(y5[:, i, :], p1[:, i, :], vec("s5_d")[:, i:i + 1],
                                         ps[:, 4 + i // 2, (i % 2) * T:(i % 2) * T + T],
                                         ALU.mult, ALU.add).then_inc(y5_in, 1)
            dve.wait_ge(ssd_y, 2)
            for i in range(WT):
                order.mark(dve.scalar_tensor_tensor(
                    yz[:, i, :].rearrange("p (c n) -> p c n", c=NC),
                    xc[:, i, :].rearrange("p (c n) -> p c n", c=NC), vec("m2_d")[:, i:i + 1],
                    ps[:, 6:8, i * P:(i + 1) * P], ALU.mult, ALU.add))
            order.join()
            order.then(dve.tensor_tensor(yz, yz, p1[:, 4:8, :], ALU.mult))
            dve.tensor_tensor(yz_sq, yz, yz, ALU.mult).then_inc(yz_ready, 1)
            dve.wait_ge(glu_sig, WT)
            dve.tensor_tensor(y8[:, 0:WT, :], y5, tmp1, ALU.mult).then_inc(yc_ready, 1)
            dve.wait_ge(yz_root, 1)
            order.then(dve.reciprocal(yz_sq[:, 0:2, :], yz_sq[:, 0:2, :]))
            for i in range(WT):
                dve.scalar_tensor_tensor(y8[:, WT + i, :], yz[:, i, :], vec("m2_norm")[:, i:i + 1],
                                         yz_sq[:, i // 2, :], ALU.mult, ALU.mult).then_inc(yd_ready, 1)
            dve_post(dve, order, 2)

        def pool_mix1(pool, order):
            pool.wait_ge(x_ready, 4)
            pool.dma_start(gain_rows[:, :], t["gain_mix1"]).then_inc(s_gain, 16)
            pool.wait_ge(dt_ready, 1)
            for c in range(NC):
                pool.tensor_tensor(seg_in[:, c, :, :], across(const("gt"), NH),
                                   along(adt[:, c * NH:(c + 1) * NH], P), ALU.mult).then_inc(seg_ready, 1)
            pool.wait_ge(jobs, 7)
            pool.tensor_tensor(acs_in, across(const("one"), NH), along(adt[:, NH:2 * NH], P), ALU.mult)\
                .then_inc(seg_ready, 1)

        STEPS = []
        for u in range(UNITS):
            STEPS += [("gate", u, 0), ("gate", u, 1), ("up", u, 0), ("up", u, 1)]
            STEPS += [("down", u - 1, 0), ("down", u - 1, 1)] if u else []
        STEPS += [("down", UNITS - 1, 0), ("down", UNITS - 1, 1)]
        N_STEPS = len(STEPS)
        assert N_STEPS % HALVES == 0 and N_STEPS % 3 == 0
        AT = {step: n for n, step in enumerate(STEPS)}
        GATED = [AT["gate", u, 1] for u in range(UNITS)]
        UPPED = [AT["up", u, 1] for u in range(UNITS)]
        DOWNED = [AT["down", u, 1] for u in range(UNITS)]
        LAST = UNITS - 1
        TURN_LAST = AT["down", LAST - 1, 0]

        def raw_of(n):
            i = 1 + (n + 3) % HALVES
            return i - 1, ring_flat[:, i * HALF:(i + 1) * HALF]

        def loads_before(n, item):
            return item * (16 * N_STEPS // HALVES) + (16 * N_STEPS // HALVES * (n // N_STEPS)
                                                      + 16 * (n % N_STEPS // HALVES + 1))

        def passes(engine, body):
            with engine.Fori(0, NE) as e:
                body(e)
            engine.wait_ge(plan_ready, 1)
            n_over = engine.value_load(plan[0:1, 0:1], min_val=0, max_val=MAX_OVER)
            with engine.If(n_over > 0):
                with engine.Fori(0, n_over) as j:
                    body(j + NE)
            return n_over

        def sp_moe(sp):
            gate_d = t["l1_moe_w_gate"].rearrange("e (k p) n -> p (e k) n", p=P)
            up_d = t["l1_moe_w_up"].rearrange("e (k p) n -> p (e k) n", p=P)
            down_d = t["l1_moe_w_down"].rearrange("e f d -> (e f) d")

            def load(n, e):
                kind, u, half = STEPS[n]
                i, raw = raw_of(n)
                if kind == "down":
                    dst = raw.rearrange("p (k d) -> p k d", k=2)
                    src = down_d[bass.ds(e * FE + u * NB, NB), :].rearrange("(p k) d -> p k d", k=4)
                    src = src[:, 2 * half:2 * half + 2, :]
                else:
                    dst = raw.rearrange("p (k n) -> p k n", k=4)
                    src = (gate_d if kind == "gate" else up_d)[:, bass.ds(e * KT + 4 * half, 4),
                                                               u * NB:(u + 1) * NB]
                sp.dma_start(dst, src).then_inc(e_loaded[i], 16)

            sp.wait_ge(yc_ready, 1)
            sp.wait_ge(yd_ready, WT)
            for n in range(N_STEPS):
                if n == 4:
                    sp.wait_ge(y_done, 6)
                if n >= HALVES:
                    sp.wait_ge(lo_ready, n - HALVES + 1)
                load(n, 0)

            def body(item, e):
                for n in range(N_STEPS):
                    sp.wait_ge(lo_ready, item * N_STEPS + (n - HALVES + 1))
                    load(n, e)
            with sp.Fori(1, NE) as e:
                body(e, e)
            sp.wait_ge(plan_ready, 1)
            n_over = sp.value_load(plan[0:1, 0:1], min_val=0, max_val=MAX_OVER)
            with sp.If(n_over > 0):
                with sp.Fori(0, n_over) as j:
                    body(j + NE, sp.value_load(plan[0:1, bass.ds(j + 1, 1)], min_val=0, max_val=NE - 1))
            for n in range(3):
                sp.wait_ge(lo_ready, n_over * N_STEPS + (NE * N_STEPS + n - HALVES + 1))
                load(n, 0)
            sp.wait_ge(x_ready, 8)
            sp.dma_start(out.rearrange("(c p) d -> p c d", p=P), x_rows[:, :, :]).then_inc(out_done, 16)

        def pe_moe(pe):
            pe_norm(pe, 3)
            pe.wait_ge(xn_ready, 16)
            for c in range(NC):
                for j in range(KT):
                    last = pe.matmul(ps[:, 4, c * NE:(c + 1) * NE], xn[:, j, c * P:(c + 1) * P],
                                     w_small[:, 1, j, :], start=j == 0, stop=j == KT - 1)
            last.then_inc(logits_done, 1)
            pe.wait_ge(sel_ready, 1)
            for n, terms in enumerate(((("lt", 0),), (("one", 0), ("lt", 1)), (("one", 0), ("one", 1)))):
                for i, (name, c) in enumerate(terms):
                    last = pe.matmul(ps[:, 5, n * NE:(n + 1) * NE], const(name), sel[:, c, :],
                                     start=i == 0, stop=i == len(terms) - 1)
            last.then_inc(ranks_done, 1)

            def gather(q, bank):
                for k in range(4):
                    f = (4 * q + k) * P
                    for c in range(NC):
                        last = pe.matmul(ps[:, bank, k * P:(k + 1) * P], xs[:, c, f:f + P], perm[:, c, :],
                                         start=c == 0, stop=c == NC - 1)
                last.then_inc(gather_done, 1)

            def scatter(c, bank):
                for h in range(2):
                    pe.matmul(ps[:, bank + h, :], perm_t[:, c, :], e_y[:, h, :],
                              start=True, stop=True).then_inc(comb_done, 1)

            def turn(u, item):
                pe.wait_ge(h_ready, item * UNITS + (u + 1))
                for k in range(4):
                    last = pe.transpose(ps[:, u % 2, k * P:(k + 1) * P],
                                        e_h[u % 2].rearrange("s (f k) -> s k f", k=4)[:, k, :], ident)
                last.then_inc(t_done, 1)

            def product(kind, u, half, item):
                n = AT[kind, u, half]
                if kind == "down":
                    pe.wait_ge(ht_lo, item * UNITS + (u + 1))
                pe.wait_ge(lo_ready, item * N_STEPS + (n + 1))
                w = split[:, n % 3, :, :]
                if kind == "down":
                    w = w.rearrange("p a (k d) -> p a k d", k=2)
                    for k in range(2):
                        for a, b in ((0, 0), (0, 1), (1, 0)):
                            for h in range(2):
                                last = pe.matmul(ps[:, 6 + h, :], ht_parts[:, u % 2, a, 2 * half + k, :],
                                                 w[:, b, k, h * NB:(h + 1) * NB],
                                                 start=u == half == k == a == b == 0,
                                                 stop=u == LAST and half == k == 1 and a == 1)
                else:
                    w = w.rearrange("p a (k n) -> p a k n", k=4)
                    for j in range(4):
                        for a, b in ((0, 0), (0, 1), (1, 0)):
                            last = pe.matmul(ps[:, 2 + 2 * (u % 2) + (kind == "up"), :],
                                             xg_parts[:, a, 4 * half + j, :], w[:, b, j, :],
                                             start=half == j == a == b == 0,
                                             stop=half == 1 and j == 3 and a == 1)
                last.then_inc(part_done, 1)

            pe.wait_ge(perm_ready, 4)
            for q in range(2):
                gather(q, 1 - q)

            def body(item):
                pe.wait_ge(xg_lo, item + 1)
                for u in range(UNITS):
                    if u == 1:
                        pe.wait_ge(comb_added, item * 4 + 2)
                    for half in range(2):
                        product("gate", u, half, item)
                    if u == 0:
                        pe.wait_ge(ey_ready, item * 2 + 2)
                        pe.wait_ge(pgt_copied, item + 1)
                        scatter(0, 4)
                    if u == 1:
                        pe.wait_ge(comb_added, item * 4 + 4)
                    if u == 4:
                        pe.wait_ge(pgt_copied, item + 2)
                    if u == 6:
                        pe.wait_ge(xg_ready, item * 2 + 3)
                    if u:
                        turn(u - 1, item)
                    for half in range(2):
                        product("up", u, half, item)
                    if u == 0:
                        scatter(1, 0)
                    if u == 3:
                        for c in range(NC):
                            last = pe.transpose(ps[:, 1, c * P:(c + 1) * P], perm_gate[:, c, :], ident)
                        last.then_inc(pgt_done, 1)
                    if u == 5:
                        pe.wait_ge(perm_ready, item * 4 + 8)
                        gather(0, 1)
                    if 0 < u:
                        product("down", u - 1, 0, item)
                        if u == LAST:
                            pe.wait_ge(xg_ready, item * 2 + 4)
                            turn(LAST, item)
                        product("down", u - 1, 1, item)
                    if u == 5:
                        gather(1, 0)
                for half in range(2):
                    product("down", LAST, half, item)
            n_over = passes(pe, body)
            pe.wait_ge(ey_ready, n_over * 2 + (NE * 2 + 2))
            scatter(0, 4)
            scatter(1, 0)

        def act_moe(act, order):
            def high(n, item):
                i, raw = raw_of(n % N_STEPS)
                act.wait_ge(e_loaded[i], loads_before(n, item))
                act.activation(split[:, n % 3, 0, :], raw, ACT.Copy).then_inc(hi_ready, 1)

            act_norm(act, order, 3)
            for n in range(3):
                high(n, 0)
            act.wait_ge(router_max, 1)
            for c in range(NC):
                act.activation(e_exp[:, c, :], logits[:, c, :], ACT.Exp, bias=top[:, c:c + 1]).then_inc(router_exp, 1)

            def xg_high(passes_before):
                act.wait_ge(xg_ready, passes_before * 2 + 2)
                act.activation(xg_parts[:, 0, :, :], xg, ACT.Copy).then_inc(xg_hi, 1)

            def silu(u):
                act.activation(e_silu[u % 2], ps[:, 2 + 2 * (u % 2), :], ACT.Silu).then_inc(silu_ready, 1)

            def ht_high(u, item):
                act.wait_ge(t_done, item * UNITS + (u + 1))
                act.activation(ht_parts[:, u % 2, 0, :, :], ps[:, u % 2, :].rearrange("p (k n) -> p k n", k=4),
                               ACT.Copy).then_inc(ht_hi, 1)
            xg_high(0)

            def body(item):
                for n in range(N_STEPS):
                    if n == TURN_LAST:
                        ht_high(LAST, item)
                    act.wait_ge(part_done, item * N_STEPS + (n + 1))
                    high(n + 3, item)
                    for u in range(UNITS):
                        if n == GATED[u]:
                            silu(u)
                            if u:
                                ht_high(u - 1, item)
                    if n == UPPED[3]:
                        act.wait_ge(pgt_done, item + 1)
                        act.activation(perm_t, ps[:, 1, 0:NC * P].rearrange("p (c n) -> p c n", c=NC), ACT.Copy)\
                            .then_inc(pgt_copied, 1)
                    if n == UPPED[LAST]:
                        xg_high(item + 1)
                for h in range(2):
                    act.activation(e_y[:, h, :], ps[:, 6 + h, :], ACT.Copy).then_inc(ey_ready, 1)
            passes(act, body)
            act.wait_ge(moe_ready, 1)
            for c in range(NC):
                order.mark(act.activation(xs[:, c, :], moe[:, c, :], ACT.Square, accum_out=sumsq[:, c:c + 1]))
            order.join()
            act.activation(root, sumsq, ACT.Sqrt, scale=1.0 / D, bias=eps_col).then_inc(out_root, 1)

        def dve_moe(dve, order):
            def low(n, item):
                _, raw = raw_of(n % N_STEPS)
                dve.wait_ge(hi_ready, item * N_STEPS + (n + 1))
                dve.tensor_tensor(split[:, n % 3, 1, :], raw, split[:, n % 3, 0, :].bitcast(F32),
                                  ALU.subtract).then_inc(lo_ready, 1)

            dve_norm(dve, order, 3, vec("g_ffn1"))
            for n in range(2):
                low(n, 0)
            dve.wait_ge(logits_done, 1)
            order.then(dve.tensor_copy(logits, ps[:, 4, 0:NC * NE].rearrange("p (c e) -> p c e", c=NC)))
            order.then(dve.tensor_reduce(top, logits, AX.X, ALU.max))
            dve.tensor_scalar(top, top, -1.0, None, ALU.mult).then_inc(router_max, 1)
            lower = const("lower8").rearrange("p (a b) -> p a b", a=NE)
            for c in range(NC):
                other, own = across(logits[:, c, :], NE), along(logits[:, c, :], NE)
                order.mark(dve.tensor_tensor(cmp1[:, c], other, own, ALU.is_gt))
                order.mark(dve.tensor_tensor(cmp2[:, c], other, own, ALU.is_equal))
            order.join()
            for c in range(NC):
                order.mark(dve.tensor_tensor(cmp2[:, c], cmp2[:, c], lower, ALU.mult))
            order.join()
            for c in range(NC):
                order.mark(dve.tensor_tensor(cmp1[:, c], cmp1[:, c], cmp2[:, c], ALU.add))
            order.join()
            for c in range(NC):
                order.mark(dve.tensor_reduce(beaten[:, c, :], cmp1[:, c], AX.X, ALU.add))
            order.join()
            dve.tensor_scalar(sel, beaten, 2.0, None, ALU.is_lt).then_inc(sel_ready, 1)
            dve.wait_ge(router_exp, 2)
            dve.wait_ge(sel_ready, 1)
            order.then(dve.tensor_tensor(e_exp, e_exp, sel, ALU.mult))
            order.then(dve.tensor_reduce(den, e_exp, AX.X, ALU.add))
            order.then(dve.reciprocal(den, den))
            order.mark(dve.tensor_tensor(gate_all[:, :, 0:NE], e_exp, along(den, NE), ALU.mult))
            dve.wait_ge(ranks_done, 1)
            order.then(dve.scalar_tensor_tensor(rank_all[:, :, 0:NE],
                                                ps[:, 5, 0:NC * NE].rearrange("p (c e) -> p c e", c=NC), 1.0,
                                                sel, ALU.add, ALU.mult))
            order.then(dve.tensor_scalar(rank_all[:, :, 0:NE], rank_all[:, :, 0:NE], -1.0, None, ALU.add))

            def make_perm(item):
                for c in range(NC):
                    rank, gate = (x[:, c, bass.ds(item, 1)] for x in (rank_all, gate_all))
                    dve.tensor_scalar(perm[:, c, :], const("iota"), rank, None, ALU.is_equal).then_inc(perm_ready, 1)
                    dve.tensor_scalar(perm_gate[:, c, :], const("iota"), rank, gate, ALU.is_equal,
                                      ALU.mult).then_inc(perm_ready, 1)

            def make_xg(q, item):
                dve.wait_ge(gather_done, item * 2 + (q + 1))
                dve.tensor_tensor(xg[:, 4 * q:4 * q + 4, :], ps[:, 1 - q, :].rearrange("p (k n) -> p k n", k=4),
                                  along(vec("g_ffn1")[:, 4 * q:4 * q + 4], P), ALU.mult).then_inc(xg_ready, 1)

            def xg_low(item):
                dve.wait_ge(xg_hi, item + 1)
                dve.tensor_tensor(xg_parts[:, 1, :, :], xg, xg_parts[:, 0, :, :].bitcast(F32),
                                  ALU.subtract).then_inc(xg_lo, 1)
            make_perm(0)
            low(2, 0)
            for q in range(2):
                make_xg(q, 0)
            order.then(dve.tensor_copy(counts, ps[:, 5, NC * NE:(NC + 1) * NE]))
            order.mark(dve.memset(moe, 0.0))
            order.mark(dve.memset(rank_all[:, :, NE:], 0.0))
            order.mark(dve.memset(gate_all[:, :, NE:], 0.0))
            order.then(dve.tensor_scalar(over, counts, float(P), None, ALU.is_gt))
            xg_low(0)
            order.then(dve.tensor_tensor_scan(over_sum, const("one")[:, 0:NE], over, 0.0, ALU.mult, ALU.add))
            order.mark(dve.tensor_copy(plan_f[:, 0:1], over_sum[:, NE - 1:NE]))
            for j in range(MAX_OVER):
                order.then(dve.scalar_tensor_tensor(pick, over_sum, float(j + 1), over, ALU.is_equal, ALU.mult))
                order.mark(dve.tensor_tensor(counts, pick, const("iota")[:, 0:NE], ALU.mult))
                order.then(dve.scalar_tensor_tensor(chosen, rank_all[:, :, 0:NE], 1.0 - P, across(pick, NC),
                                                    ALU.add, ALU.mult))
                order.mark(dve.tensor_reduce(plan_f[:, j + 1:j + 2], counts, AX.X, ALU.add))
                order.then(dve.tensor_reduce(rank_all[:, :, NE + j], chosen, AX.X, ALU.add))
                order.then(dve.tensor_tensor(chosen, gate_all[:, :, 0:NE], across(pick, NC), ALU.mult))
                order.then(dve.tensor_reduce(gate_all[:, :, NE + j], chosen, AX.X, ALU.add))
            order.mark(dve.tensor_scalar(rank_all[:, :, NE:], rank_all[:, :, NE:], -1.0, None, ALU.add))
            order.join()
            dve.tensor_copy(plan, plan_f).then_inc(plan_ready, 1)

            def ht_low(u, item):
                dve.wait_ge(ht_hi, item * UNITS + (u + 1))
                dve.tensor_tensor(ht_parts[:, u % 2, 1, :, :], ps[:, u % 2, :].rearrange("p (k n) -> p k n", k=4),
                                  ht_parts[:, u % 2, 0, :, :].bitcast(F32), ALU.subtract).then_inc(ht_lo, 1)

            def add_rows(n, bank, before):
                m = moe[:, n // 2, (n % 2) * NB:(n % 2 + 1) * NB]
                dve.wait_ge(comb_done, before * 4 + (n + 1))
                dve.tensor_tensor(m, m, ps[:, bank, :], ALU.add).then_inc(comb_added, 1)

            def body(item):
                for n in range(N_STEPS):
                    if n == TURN_LAST:
                        ht_low(LAST, item)
                    low(n + 3, item)
                    if n in (1, 3):
                        for h in range(2):
                            add_rows(n - 1 + h, (4 if n == 1 else 0) + h, item)
                    for u in range(UNITS):
                        if n == GATED[u] and u:
                            ht_low(u - 1, item)
                        if n == UPPED[u]:
                            dve.wait_ge(part_done, item * N_STEPS + (n + 1))
                            dve.wait_ge(silu_ready, item * UNITS + (u + 1))
                            dve.tensor_tensor(e_h[u % 2], e_silu[u % 2], ps[:, 3 + 2 * (u % 2), :], ALU.mult)\
                                .then_inc(h_ready, 1)
                    if n == UPPED[4]:
                        dve.wait_ge(pgt_done, item + 1)
                        make_perm(item + 1)
                    if n == UPPED[5]:
                        make_xg(0, item + 1)
                    if n == DOWNED[4]:
                        make_xg(1, item + 1)
                    if n == DOWNED[5]:
                        xg_low(item + 1)
            n_over = passes(dve, body)
            for n in range(4):
                add_rows(n, (4, 5, 0, 1)[n], n_over + NE)
            dve.wait_ge(comb_added, n_over * 4 + 4 * NE + 4)
            dve.nop().then_inc(moe_ready, 1)
            dve.wait_ge(out_root, 4)
            order.then(dve.reciprocal(rstd, root))
            dve.wait_ge(s_gain, 64)
            for c in range(NC):
                order.mark(dve.scalar_tensor_tensor(xs[:, c, :], moe[:, c, :], rstd[:, c:c + 1], gain_rows[:, :],
                                                    ALU.mult, ALU.mult))
            order.join()
            for c in range(NC):
                dve.tensor_tensor(x_rows[:, c, :], x_rows[:, c, :], xs[:, c, :], ALU.add).then_inc(x_ready, 1)

        def pool_moe(pool, order):
            pool.wait_ge(x_ready, 6)
            pool.dma_start(gain_rows[:, :], t["gain_ffn1"]).then_inc(s_gain, 16)
            pool.memset(e_y, 0.0).then_inc(ey_ready, 2)
            pool.memset(perm_t, 0.0).then_inc(pgt_copied, 1)

        @block.sync
        def _(sp):
            sp.dma_start(x_rows[:, :, :], t["x"].rearrange("(c p) d -> p c d", p=P)).then_inc(s_x, 16)
            w = t["l0_w_in"].rearrange("(k p) n -> p k n", p=P)
            for s in range(6):
                n = min(NB, EVEN_IN - s * NB)
                sp.dma_start(slot_tiles(s, n), w[:, :, s * NB:s * NB + n]).then_inc(loaded[s], 16)
            w = t["l0_w_out"].rearrange("(k p) n -> p k n", p=P)
            sp.wait_ge(in_done, 11)
            for s in range(2):
                sp.dma_start(slot_tiles(s), w[:, :, s * NB:(s + 1) * NB]).then_inc(loaded[s], 16)
            if stop != "mix0":
                sp_ffn(sp)
            if stop not in ("mix0", "ffn0"):
                sp_mix1(sp)
            if stop is None:
                sp_moe(sp)
            else:
                if stop == "mix1":
                    sp.wait_ge(x_ready, 6)
                    sp.dma_start(dbg, y8).then_inc(dbg_sem, 16)
                    sp.wait_ge(dbg_sem, 16)
                if stop == "mix0":
                    sp.wait_ge(x_ready, 2)
                    sp.dma_start(dbg, y8).then_inc(dbg_sem, 16)
                    sp.wait_ge(dbg_sem, 16)
                elif stop == "ffn0":
                    sp.wait_ge(x_ready, 4)
                sp.dma_start(out.rearrange("(c p) d -> p c d", p=P), x_rows[:, :, :]).then_inc(out_done, 16)
            sp.wait_ge(out_done, 16)

        @block.gpsimd
        def _(pool):
            order = Order(pool, o_pool)
            pool_mix0(pool, order)
            if stop != "mix0":
                pool.wait_ge(x_ready, 2)
                pool.dma_start(gain_rows[:, :], t["gain_ffn0"]).then_inc(s_gain, 16)
                pool_rotations(pool, order)
            if stop not in ("mix0", "ffn0"):
                pool_mix1(pool, order)
            if stop is None:
                pool_moe(pool, order)

        @block.scalar
        def _(act):
            order = Order(act, o_act)
            act.dma_start(consts[:, :], t["consts"]).then_inc(s_init, 16)
            act.dma_start(vecs[:, :], t["vecs"]).then_inc(s_init, 16)
            for dst, name in ((inv_mask, "inv_mask"), (lora_wa, "lora_wa"), (lora_g, "l0_rwkv_g2"),
                              (gln, "gmlp_ln"), (ws_t, "ws_t")):
                act.dma_start(dst, t[name]).then_inc(s_b2, 16)
            act.dma_start(w_small[:, 0], t["w_dt"]).then_inc(s_small, 16)
            act.dma_start(w_small[:, 1], t["router"]).then_inc(s_small, 16)
            act.dma_start(bs_row[0:1, :], t["bs_row"]).then_inc(s_b2, 16)
            act_angles(act)
            act_mix0(act, order)
            if stop != "mix0":
                act_ffn(act, order)
            if stop not in ("mix0", "ffn0"):
                act_mix1(act, order)
            if stop is None:
                act_moe(act, order)

        @block.vector
        def _(dve):
            order = Order(dve, o_dve)
            dve_angles(dve, order)
            dve_mix0(dve, order)
            if stop != "mix0":
                dve_ffn(dve, order)
            if stop not in ("mix0", "ffn0"):
                dve_mix1(dve, order)
            if stop is None:
                dve_moe(dve, order)

        @block.tensor
        def _(pe):
            pe_mix0(pe)
            if stop != "mix0":
                pe_ffn(pe)
            if stop not in ("mix0", "ffn0"):
                pe_mix1(pe)
            if stop is None:
                pe_moe(pe)


def layout(inputs):
    import numpy as np

    a = {k: np.asarray(v) for k, v in inputs.items()}
    f32 = np.float32

    def cols(v):
        return np.ascontiguousarray(np.reshape(v, (-1, P)).T)

    i = np.arange(P)
    s, u = i[:, None], i[None, :]
    c = {"ident": s == u, "le": s <= u, "lt": s < u, "gt": s > u, "blk": s // HD == u // HD,
         "iota": np.broadcast_to(u, (P, P)), "one": np.ones((P, P)),
         "lower8": np.broadcast_to(np.tri(NE, NE, -1).reshape(1, -1), (P, NE * NE)),
         "eps": np.broadcast_to(np.array([[EPS, GN_EPS, math.pi / 2]]), (P, 3))}
    masks = [(s // (2 * m) == u // (2 * m)) & (s % (2 * m) < m) & (u % (2 * m) >= m)
             for m in (2 ** e for e in range(LEVELS))]
    state_p = lambda v: np.ascontiguousarray(v.reshape(S5_TILES, P).T)
    per_state = lambda v: np.repeat(v, 64, axis=0)
    v = {"mu": cols(a["l0_rwkv_mu"]), "w0": cols(a["l0_rwkv_w0"]), "a0": cols(a["l0_rwkv_a0"]),
         "k_k": cols(a["l0_rwkv_k_k"]), "k_a": cols(a["l0_rwkv_k_a"]), "r_k": cols(a["l0_rwkv_r_k"]),
         "ln_w": cols(a["l0_rwkv_ln_w"]), "ln_b": cols(a["l0_rwkv_ln_b"]),
         "g_mix0": cols(a["l0_norm_pre_mix"]), "g_ffn0": cols(a["l0_norm_pre_ffn"]),
         "g_mix1": cols(a["l1_norm_pre_mix"]), "g_ffn1": cols(a["l1_norm_pre_ffn"]),
         "a_re": state_p(a["l1_s5_a_re"]), "a_im": state_p(a["l1_s5_a_im"]),
         "log_dt": state_p(per_state(a["l1_s5_log_dt"])), "s5_d": cols(a["l1_s5_d"]),
         "glu_b": cols(a["l1_s5_glu_b"]),
         "conv_w": np.concatenate([cols(w) for w in a["l1_m2_conv_w"]], axis=1),
         "conv_b": cols(a["l1_m2_conv_b"]), "m2_d": cols(per_state(a["l1_m2_d"])),
         "m2_norm": cols(a["l1_m2_norm_w"]),
         "dt_bias": np.broadcast_to(a["l1_m2_dt_bias"][None, :], (P, NH)),
         "a_log": np.broadcast_to(a["l1_m2_a_log"][None, :], (P, NH))}
    rows = lambda w: np.ascontiguousarray(np.broadcast_to(w[None, :], (P, D)))
    b_t = np.zeros((2, P, 4, P), f32)
    c_t = np.zeros((2, P, S5_TILES, 32), f32)
    for n, (b, cc) in enumerate((("l1_s5_b_re", "l1_s5_c_re"), ("l1_s5_b_im", "l1_s5_c_im"))):
        for g in range(2 * S5_TILES):
            j, half = divmod(g, 2)
            ch = 32 * (j % 4) + 16 * half
            b_t[n, ch:ch + 16, j // 4, 64 * half:64 * half + 64] = a[b][g].T
            c_t[n, 64 * half:64 * half + 64, j, 16 * half:16 * half + 16] = a[cc][g].T
    t = {
        "x": a["x"][0],
        "consts": np.concatenate([c[n] for n, _ in CONSTS], axis=1).astype(f32),
        "vecs": np.concatenate([v[n] for n, _ in VECS], axis=1),
        "inv_mask": np.stack(masks, axis=1).astype(f32),
        "lora_wa": np.concatenate([a["l0_rwkv_w2"], a["l0_rwkv_a2"]], axis=0),
        "l0_rwkv_g2": a["l0_rwkv_g2"],
        "gmlp_ln": np.ascontiguousarray(np.broadcast_to(
            np.stack([a["l0_gmlp_ln_w"].reshape(-1), a["l0_gmlp_ln_b"].reshape(-1)])[None], (P, 2, WID))),
        "ws_t": np.ascontiguousarray(a["l0_gmlp_ws"].transpose(2, 0, 1)),
        "bs_row": a["l0_gmlp_bs"].reshape(1, -1),
        "gain_mix0": rows(a["l0_norm_post_mix"]), "gain_ffn0": rows(a["l0_norm_post_ffn"]),
        "gain_mix1": rows(a["l1_norm_post_mix"]), "gain_ffn1": rows(a["l1_norm_post_ffn"]),
        "w_dt": np.ascontiguousarray(a["l1_w_in"][:, ODD_MAIN:].reshape(KT, P, NE).transpose(1, 0, 2)),
        "router": np.ascontiguousarray(a["l1_moe_router"].reshape(KT, P, NE).transpose(1, 0, 2)),
        "s5_b": b_t, "s5_c": c_t,
    }
    for name in ("l0_w_in", "l0_w_out", "l0_ffn_w_gate", "l0_ffn_w_up", "l0_ffn_w_down", "l1_w_in",
                 "l1_s5_glu_w", "l1_w_out", "l1_moe_w_gate", "l1_moe_w_up", "l1_moe_w_down"):
        t[name] = a[name]
    return {k: np.ascontiguousarray(x) for k, x in t.items()}


def kernel(**inputs):
    from concourse import bacc
    from concourse.bass_utils import run_bass_kernel_spmd

    nc = bacc.Bacc("TRN2", target_bir_lowering=False, num_devices=1)
    arrays = layout(inputs)
    aps = {n: nc.dram_tensor(f"{n}_dram", a.shape, mybir.dt.from_np(a.dtype), kind="ExternalInput").ap()
           for n, a in arrays.items()}
    out = nc.dram_tensor("out_dram", (T, D), F32, kind="ExternalOutput").ap()
    trunk(nc, aps, out)
    r = run_bass_kernel_spmd(nc, [{f"{n}_dram": a for n, a in arrays.items()}], core_ids=[0])
    return r.results[0]["out_dram"].reshape(1, T, D)
```

```python
import math
from contextlib import ExitStack

import concourse.bass as bass
from concourse import mybir

F32 = mybir.dt.float32
I32 = mybir.dt.int32
F32R = mybir.dt.float32r
ALU = mybir.AluOpType
ACT = mybir.ActivationFunctionType
AX = mybir.AxisListType

P = 128
T = 256
NC = T // P
D = 1024
KT = D // P
EPS = 1e-6
NB = 512

WID = D // 2
WT = WID // P
HD = 64
NH = WID // HD
A_IN = 3 * WID + 64 + 64 + 128
A_TILES = A_IN // P
EVEN_IN = A_IN + 2 * WID
GN_EPS = 64e-5
LEVELS = 7
K_DECAY = math.exp(-0.5)

S5_TILES = 16
D_XBC = 1024
ODD_MAIN = 2048
FFN = 2816
FT = FFN // P
NE = 8
FE = 3584
UNITS = FE // NB
MAX_OVER = 3
PASSES = NE + MAX_OVER

SLOT = 4096
SLOTS = 7
HALF = SLOT // 2
HALVES = 7

VECS = [("mu", A_TILES), ("w0", WT), ("a0", WT), ("k_k", WT), ("k_a", WT), ("r_k", WT),
        ("ln_w", WT), ("ln_b", WT), ("g_mix0", KT), ("g_ffn0", KT), ("g_mix1", KT), ("g_ffn1", KT),
        ("a_re", S5_TILES), ("a_im", S5_TILES), ("log_dt", S5_TILES), ("s5_d", WT), ("glu_b", WT),
        ("conv_w", 4 * KT), ("conv_b", KT), ("m2_d", WT), ("m2_norm", WT),
        ("dt_bias", NH), ("a_log", NH)]
VEC_AT = {}
_at = 0
for _n, _w in VECS:
    VEC_AT[_n] = (_at, _w)
    _at += _w
N_VEC = _at

CONSTS = [("ident", P), ("lt", P), ("le", P), ("gt", P), ("blk", P), ("iota", P), ("lower8", NE * NE),
          ("one", P), ("eps", 3)]
CONST_AT = {}
_at = 0
for _n, _w in CONSTS:
    CONST_AT[_n] = (_at, _w)
    _at += _w
N_CONST = _at


class Region:

    def __init__(self, ap):
        self.ap, self.at = ap, 0

    def take(self, *shape):
        n = math.prod(shape)
        got = self.ap[:, self.at:self.at + n]
        assert self.at + n <= self.ap.shape[1], (self.at, n)
        self.at += n
        if len(shape) == 1:
            return got
        names = "abcde"[:len(shape)]
        spec = f"p ({' '.join(names)}) -> p {' '.join(names)}"
        return got.rearrange(spec, **dict(zip(names[1:], shape[1:])))


class Order:

    def __init__(self, engine, sem):
        self.engine, self.sem, self.n = engine, sem, 0

    def then(self, ins):
        self.mark(ins)
        self.join()

    def mark(self, ins):
        ins.then_inc(self.sem, 1)
        self.n += 1

    def join(self):
        self.engine.wait_ge(self.sem, self.n)


def along(vec, n):
    return vec.rearrange("p (k o) -> p k o", o=1).broadcast_to([vec.shape[0], vec.shape[1], n])


def across(mat, k):
    return mat.rearrange("p (o n) -> p o n", o=1).broadcast_to([mat.shape[0], k, mat.shape[1]])


def trunk(nc, t, out):
    ctx = ExitStack()
    with ctx:
        def sb(name, *shape):
            return ctx.enter_context(nc.sbuf_tensor(name, [P, *shape], F32))

        def sem(name):
            return ctx.enter_context(nc.semaphore(name))

        consts = sb("consts", N_CONST)
        vecs = sb("vecs", N_VEC)
        x_rows = sb("x_rows", NC, D)
        xn = sb("xn", KT, T)
        gain_rows = sb("gain_rows", D)
        w_small = sb("w_small", 2, KT, NE)
        stats = sb("stats", 16)
        with ExitStack() as first:
            work_a = first.enter_context(nc.sbuf_tensor("work_a", [P, 9216], F32))
            tables = first.enter_context(nc.sbuf_tensor("tables", [P, 8192], F32))
            ring = first.enter_context(nc.sbuf_tensor("ring", [P, SLOTS, SLOT], F32))

        def parts(name, *shape):
            return ctx.enter_context(nc.sbuf_tensor(name, [P, *shape], F32R))
        with ExitStack() as second:
            second.enter_context(nc.sbuf_tensor("split0_front", [P, 9216 + 8192 + 3 * SLOT], F32))
            split_0 = second.enter_context(nc.sbuf_tensor("split_0", [P, 3, 2, HALF], F32R))
        sb("work_front", 5120)
        act_parts = parts("act_parts", 2, 2, 2, T)
        sb("work_back", 2048)
        xn_parts_0 = parts("xn_parts_0", 2, KT, T)
        sb("tables_back", 2048)
        ht_parts = parts("ht_parts", 2, 2, 4, P)
        xg_parts = parts("xg_parts", 2, KT, P)
        sb("ring_front", 5 * HALF)
        xn_parts = parts("xn_parts", 2, KT, T)
        split = parts("split", 3, 2, HALF)
        ps = ctx.enter_context(nc.psum_tensor("ps", [P, 8, NB], F32))
        ring_flat = ring[:, :, :].rearrange("p s n -> p (s n)")

        def const(name):
            a, w = CONST_AT[name]
            return consts[:, a:a + w]

        def vec(name):
            a, w = VEC_AT[name]
            return vecs[:, a:a + w]

        ident = const("ident")
        sumsq, root, rstd = stats[:, 0:2], stats[:, 2:4], stats[:, 4:6]

        def slot_tiles(s, n=NB, k=KT):
            return ring[:, s, 0:k * n].rearrange("p (k n) -> p k n", k=k)

        a0 = Region(work_a[:, :])
        praw = a0.take(A_TILES, T)
        pm = a0.take(A_TILES, T)
        u_cols = a0.take(WT, T)
        v_rows = a0.take(NC, WID)
        a0b = Region(work_a[:, 0:A_TILES * T])
        sig_w, cs, csc = a0b.take(WT, T), a0b.take(WT, T), a0b.take(WT, T)
        y8 = work_a[:, 0:KT * T].rearrange("p (k n) -> p k n", k=KT)
        xs = work_a[:, 2 * A_TILES * T:2 * A_TILES * T + NC * D].rearrange("p (c n) -> p c n", c=NC)
        b1 = Region(ring_flat[:, 2 * SLOT:6 * SLOT])
        early = Region(b1.take(8 * WT * T))
        csm, e_dec, e_prev, e_inv = (early.take(WT, T) for _ in range(4))
        gate_a, kk, kp, knorm = (early.take(WT, T) for _ in range(4))
        mats = ring_flat[:, 2 * SLOT:4 * SLOT].rearrange("p (m j n) -> p m j n", m=NH * NC, j=4)
        ar = b1.take(WT, NC, 2, P)
        bt, kt = b1.take(WT, T), b1.take(WT, T)
        v_tok = b1.take(NC, WID)
        bk_tok = b1.take(2, WID)
        bonus_in = b1.take(WT, T)
        rhs_tok, sa_tok = b1.take(WID), b1.take(WID)
        y_cols = ar.rearrange("p a b c d -> p (a b c d)")[:, 0:WT * T].rearrange("p (a n) -> p a n", a=WT)
        y_sq = ar.rearrange("p a b c d -> p (a b c d)")[:, WT * T:].rearrange("p (a n) -> p a n", a=WT)
        b2 = Region(ring[:, 6, :])
        inv_mask = b2.take(LEVELS, P)
        lora_wa, lora_g = b2.take(WID), b2.take(WID)
        gln = b2.take(2, WID)
        ws_t = b2.take(WT, P)
        state = b2.take(WT, 2, HD)
        half_sum = b2.take(WT, NC)
        state_scale = b2.take(WT)
        bn6 = b2.take(NC * WT, 6)
        bn2 = b2.take(NC * WT, 2)
        k_norm, y_std = b2.take(NC * NH), b2.take(NC * NH)
        bs_row = gain_rows[:, 0:WID]
        tb = Region(tables[:, :])
        inv_t, inv_tt, inv_v, inv_m = (tb.take(4, 4, P) for _ in range(4))
        gate = inv_m.rearrange("p a b n -> p (a b n)")[:, 0:WT * T].rearrange("p (a n) -> p a n", a=WT)
        bk_head = tables[:, 4096:8192].rearrange("p (h m i n) -> p h m i n", h=2, m=2, i=WT)

        f_h = [work_a[:, b * NB:(b + 1) * NB].rearrange("p (i n) -> p i n", i=2) for b in range(2)]

        angle = sb("angle", LEVELS + 1, S5_TILES)
        turns = sb("turns", LEVELS + 1, S5_TILES)
        rot_c, rot_s = sb("rot_c", LEVELS + 1, S5_TILES), sb("rot_s", LEVELS + 1, S5_TILES)
        s5v = sb("s5v", 7, S5_TILES)
        s5_dt, s5_mag, f_re, f_im, s5_den, s5_nr, s5_ni = (s5v[:, i, :] for i in range(7))
        cos_t = tables[:, 0:S5_TILES * T].rearrange("p (j n) -> p j n", j=S5_TILES)
        sin_t = tables[:, S5_TILES * T:].rearrange("p (j n) -> p j n", j=S5_TILES)
        rot_tmp = [work_a[:, 1024 + i * 2048:3072 + i * 2048] for i in range(2)]
        a1 = Region(work_a[:, :])
        p1 = a1.take(2 * KT, T)
        xc = a1.take(KT, T)
        ce = a1.take(NH, P)
        yz = xs[:, 0, :].rearrange("p (i n) -> p i n", i=WT)
        yz_sq = xs[:, 1, :].rearrange("p (i n) -> p i n", i=WT)
        xdec = p1[:, 8:10, :].rearrange("p a n -> p (a n)")
        st_rows = p1[:, 10:12, :].rearrange("p a n -> p (a n)")
        c1 = Region(ring_flat[:, 4 * SLOT:])
        b_in, c_in, c_out = c1.take(2, 4, P), c1.take(2, S5_TILES, 32), c1.take(2, S5_TILES, 32)
        tmp1, tmp2 = c1.take(4, T), c1.take(4, T)
        z_bufs = [(c1.take(4, T), c1.take(4, T)) for _ in range(2)]
        z_re_cos, z_im_cos = c1.take(4, T), c1.take(4, T)
        c_minus = c_in[:, 0]
        y5 = c1.take(WT, T)
        glu_w = ring[:, 2, 0:2048].rearrange("p (k n) -> p k n", k=WT)
        d1 = Region(ring_flat[:, 2 * SLOT + 2048:4 * SLOT])
        seg_in = d1.take(NC, NH, P)
        lmat = d1.take(NC, NH, P)
        cb = d1.take(NC, 2, P)
        xdt = d1.take(NC, WID)
        b_rows = d1.take(2 * P)
        acs_in = seg_in[:, 0, :, :]
        ssd = d1.take(8, NC * NH)
        dt_v, sp_e, sp_w, sp_l, adt, dec_s, a_neg, sp_m = (ssd[:, i, :] for i in range(8))

        e1 = Region(work_a[:, 0:2 * A_TILES * T])
        xg = e1.take(KT, P)
        perm, perm_gate = e1.take(NC, P), e1.take(NC, P)
        perm_t = e1.take(NC, P)
        e_silu, e_h = [e1.take(NB) for _ in range(2)], [e1.take(NB) for _ in range(2)]
        e_y = e1.take(2, NB)
        g1 = Region(tables[:, 0:8192 - 2048])
        moe = g1.take(NC, D)
        logits, beaten, sel, e_exp = (g1.take(NC, NE) for _ in range(4))
        cmp1, cmp2 = g1.take(NC, NE, NE), g1.take(NC, NE, NE)
        top, den = g1.take(NC), g1.take(NC)
        rank_all, gate_all = g1.take(NC, PASSES + 1), g1.take(NC, PASSES + 1)
        chosen = g1.take(NC, NE)
        counts, over, over_sum, pick = (g1.take(NE) for _ in range(4))
        plan_f = g1.take(1 + MAX_OVER)
        plan = g1.take(1 + MAX_OVER).bitcast(I32)

        s_init = sem("params_loaded")
        s_x = [sem(f"x_chunk{c}_loaded") for c in range(NC)]
        s_b2 = sem("small_params_loaded")
        s_gain = sem("gain_rows_loaded")
        loaded = [sem(f"out_weights{i}_loaded") for i in range(2)]
        x_ready = sem("x_rows_ready")
        rms_ready = sem("norm_root_ready")
        scaled = sem("norm_rows_scaled")
        norm_t = sem("norm_transposed")
        xn_ready = sem("xn_ready")
        y_done = sem("out_product_done")
        out_root = sem("post_norm_root_ready")
        o_act, o_dve, o_pool = sem("act_order"), sem("dve_order"), sem("pool_order")
        in_done = sem("in_product_done")
        in_hi, in_lo = sem("in_high_part_ready"), sem("in_low_part_ready")
        in_dve, in_act = sem("in_copied_by_dve"), sem("in_copied_by_act")
        lora_mixed, mixed = sem("loras_mixed"), sem("p_mixed")
        lora_act = sem("loras_activated")
        wl_done, al_done = sem("w_lora_done"), sem("a_lora_done")
        sig_ready, ga_ready = sem("sig_w_ready"), sem("gate_a_ready")
        kksq_ready, kksum_done, knorm_ready = sem("kk_squared"), sem("kk_summed"), sem("kk_norm_ready")
        cs_ready, exps_ready = sem("decay_sums_ready"), sem("decays_ready")
        half_ready, scale_ready = sem("state_exponent_ready"), sem("state_scale_ready")
        ab_ready, bonus_ready = sem("abrk_ready"), sem("bonus_in_ready")
        kp_used, r_ready = sem("k_used_by_bonus"), sem("decayed_r_ready")
        gate_copied = sem("rwkv_gate_copied")
        wide_ready = sem("head_factors_widened")
        inv_ready, spread_done = sem("head_factors_ready"), sem("head_factors_spread")
        bk_zero, b_head, k_head = sem("bk_head_zeroed"), sem("b_by_head_ready"), sem("k_by_head_ready")
        rows_done, rows_copied = sem("vbk_transposed"), sem("vbk_rows_ready")
        mat_zero, mat_done, mat_ready = sem("mat_zeroed"), sem("mat_done"), sem("mat_ready")
        m_ready, u_done, v_ready = sem("inv_m_ready"), sem("inv_u_done"), sem("inv_v_ready")
        tt_done, t_copied, tt_copied = sem("inv_t_done"), sem("inv_t_copied"), sem("inv_tt_copied")
        rhs_done, rhs_ready = sem("rhs_done"), sem("rhs_ready")
        sa_done, sa_ready = sem("sa_done"), sem("sa_ready")
        yk_done, st_done, st_ready = sem("rwkv_y_done"), sem("state_done"), sem("state_ready")
        ysum_in, ysum_done, gn_root = sem("group_norm_in"), sem("group_norm_summed"), sem("group_norm_root")
        bg_done = sem("bonus_and_gate_done")
        ya_ready, yb_ready = sem("ya_ready"), sem("yb_ready")
        gv_ready, ws_ready, gs_done = sem("gmlp_v_ready"), sem("spatial_weights_ready"), sem("spatial_done")
        gv_root = sem("gmlp_root_ready")
        gv_stats = sem("gmlp_stats_ready")
        half_loaded = [sem(f"half_slot{i}_loaded") for i in range(8)]
        xp_hi, xp_lo = sem("xn_high_part_ready"), sem("xn_low_part_ready")
        f_hi, f_lo, f_done = sem("ffn_high_part_ready"), sem("ffn_low_part_ready"), sem("ffn_step_done")
        f_silu_ready, f_h_ready = sem("ffn_silu_ready"), sem("ffn_h_ready")
        fh_hi, fh_lo = sem("ffn_h_high_part_ready"), sem("ffn_h_low_part_ready")
        ang_ready, ang_reduced, rot_ready = sem("dt_ready"), sem("angles_reduced"), sem("rotations_ready")
        rot_table = sem("rotation_tables_ready")
        s5_loaded = sem("s5_maps_and_glu_loaded")
        p1_done, p1_ready, dt_done = sem("in1_product_done"), sem("in1_copied"), sem("dt_product_done")
        bu_done, v_done, q_done, y5_done = sem("s5_bu_done"), sem("s5_bu_used"), sem("s5_x_ready"), sem("s5_y_done")
        c_ready, z_ready = sem("s5_output_map_ready"), sem("s5_recurrence_ready")
        last_re = sem("s5_last_real_part_turned_back")
        conv_done, xc_ready = sem("conv_done"), sem("xbc_ready")
        sp1, sp2, dt_ready = sem("softplus_in"), sem("softplus_exp"), sem("dt_and_a_ready")
        seg_ready, jobs = sem("segment_weights_ready"), sem("ssd_products_done")
        ssd_act, ssd_dve = sem("ssd_copied_by_act"), sem("ssd_copied_by_dve")
        xdec_ready, mats1 = sem("xdec_ready"), sem("ssd_matrices_ready")
        ce_ready, ssd_y = sem("ce_ready"), sem("ssd_y_done")
        yz_ready, yz_sum, yz_root = sem("ssd_gated_ready"), sem("ssd_gated_summed"), sem("ssd_gated_root")
        y5_in, gy_ready, glu_done, glu_sig = sem("s5_y_ready"), sem("s5_gelu_ready"), sem("glu_done"), sem("glu_sigmoid")
        yc_ready, yd_ready = sem("yc_ready"), sem("yd_ready")
        logits_done, router_max, router_exp = sem("logits_done"), sem("router_max"), sem("router_exp")
        sel_ready, ranks_done, plan_ready = sem("selection_ready"), sem("ranks_done"), sem("plan_ready")
        hi_ready, lo_ready = sem("expert_high_part_ready"), sem("expert_low_part_ready")
        part_done = sem("expert_half_used")
        perm_ready, gather_done, xg_ready = sem("perm_parts_ready"), sem("gather_done"), sem("xg_ready")
        xg_hi, xg_lo = sem("xg_high_part_ready"), sem("xg_low_part_ready")
        pgt_done, pgt_copied = sem("perm_transposed"), sem("perm_t_ready")
        silu_ready, h_ready = sem("expert_silu_ready"), sem("expert_h_ready")
        t_done, ht_hi, ht_lo = sem("expert_h_transposed"), sem("expert_ht_high_ready"), sem("expert_ht_low_ready")
        ey_ready = sem("expert_y_ready")
        comb_done, comb_added = sem("scatter_done"), sem("scatter_added")
        moe_ready = sem("moe_sum_ready")
        out_done = sem("output_written")

        block = ctx.enter_context(nc.Block())

        def act_norm(act, order, k):
            for c in range(NC):
                if k == 0:
                    act.wait_ge(s_x[c], 16)
                else:
                    act.wait_ge(x_ready, 2 * k - 1 + c)
                order.mark(act.activation(xs[:, c, :], x_rows[:, c, :], ACT.Square,
                                          accum_out=sumsq[:, c:c + 1]))
            order.join()
            if k == 0:
                act.wait_ge(s_init, 32)
            act.activation(root, sumsq, ACT.Sqrt, scale=1.0 / D, bias=eps_col).then_inc(rms_ready, 1)

        def dve_norm(dve, order, k, gain, between=None):
            dve.wait_ge(rms_ready, k + 1)
            order.then(dve.reciprocal(rstd, root))
            for c in range(NC):
                dve.tensor_scalar(xs[:, c, :], x_rows[:, c, :], rstd[:, c:c + 1], None,
                                  ALU.mult).then_inc(scaled, 1)
            if between:
                between()
            for c in range(NC):
                for q in range(2):
                    i = 2 * c + q
                    dve.wait_ge(norm_t, 4 * k + i + 1)
                    dve.tensor_tensor(xn[:, 4 * q:4 * q + 4, c * P:(c + 1) * P],
                                      ps[:, i, :].rearrange("p (k n) -> p k n", k=4),
                                      along(gain[:, 4 * q:4 * q + 4], P), ALU.mult).then_inc(xn_ready, 1)

        def act_xn_high(act, k, dst):
            for c in range(NC):
                for q in range(2):
                    act.wait_ge(xn_ready, 4 * k + 2 * c + q + 1)
                    act.activation(dst[:, 0, 4 * q:4 * q + 4, c * P:(c + 1) * P],
                                   xn[:, 4 * q:4 * q + 4, c * P:(c + 1) * P], ACT.Copy).then_inc(xp_hi, 1)

        def dve_xn_low(dve, k, dst):
            for c in range(NC):
                for q in range(2):
                    dve.wait_ge(xp_hi, 4 * k + 2 * c + q + 1)
                    ks, ts = slice(4 * q, 4 * q + 4), slice(c * P, (c + 1) * P)
                    dve.tensor_tensor(dst[:, 1, ks, ts], xn[:, ks, ts], dst[:, 0, ks, ts].bitcast(F32),
                                      ALU.subtract).then_inc(xp_lo, 1)

        def pe_norm(pe, k):
            for c in range(NC):
                pe.wait_ge(scaled, 2 * k + c + 1)
                for q in range(2):
                    for j in range(4):
                        f = (4 * q + j) * P
                        last = pe.transpose(ps[:, 2 * c + q, j * P:(j + 1) * P], xs[:, c, f:f + P], ident)
                    last.then_inc(norm_t, 1)

        def pe_out(pe, first, mixer, products=range(16)):
            for n in products:
                bank, i = divmod(n, WT)
                c, h = divmod(bank, 2)
                j = mixer * WT + i
                last = pe.matmul(ps[:, 4 + bank, :], y8[:, j, c * P:(c + 1) * P], slot_tiles(h)[:, j, :],
                                 start=first and i == 0, stop=not first and i == WT - 1)
                if not first and h == 1 and i == WT - 1:
                    last.then_inc(y_done, 1)

        def act_post(act, order, k, banks=True):
            for c in range(NC):
                act.wait_ge(y_done, 2 * k + c + 1)
                order.mark(act.activation(xs[:, c, :].rearrange("p (a n) -> p a n", a=2),
                                          ps[:, 4 + 2 * c:6 + 2 * c, :], ACT.Square,
                                          accum_out=sumsq[:, c:c + 1]))
            order.join()
            act.activation(root, sumsq, ACT.Sqrt, scale=1.0 / D, bias=eps_col).then_inc(out_root, 1)

        def dve_post(dve, order, k):
            dve.wait_ge(out_root, k + 1)
            order.then(dve.reciprocal(rstd, root))
            dve.wait_ge(s_gain, 16 * (k + 1))
            for c in range(NC):
                order.then(dve.scalar_tensor_tensor(
                    xs[:, c, :].rearrange("p (a n) -> p a n", a=2), ps[:, 4 + 2 * c:6 + 2 * c, :],
                    rstd[:, c:c + 1], gain_rows[:, :].rearrange("p (a n) -> p a n", a=2), ALU.mult, ALU.mult))
                dve.tensor_tensor(x_rows[:, c, :], x_rows[:, c, :], xs[:, c, :], ALU.add).then_inc(x_ready, 1)

        eps_col = const("eps")[:, 0:1]
        gn_eps_col = const("eps")[:, 1:2]
        mask_ar = consts[:, CONST_AT["lt"][0]:CONST_AT["lt"][0] + 2 * P].bitcast(I32)

        TERMS = ((0, 0), (0, 1), (1, 0))
        RAW = 6
        IN_STEPS = EVEN_IN // T

        def half_slot(i):
            return ring_flat[:, i * HALF:(i + 1) * HALF]

        def in_high(act, n):
            act.wait_ge(half_loaded[n % RAW], 16 * (n // RAW + 1))
            act.activation(split_0[:, n % 3, 0, :], half_slot(n % RAW), ACT.Copy).then_inc(in_hi, 1)

        def in_low(dve, n):
            dve.wait_ge(in_hi, n + 1)
            dve.tensor_tensor(split_0[:, n % 3, 1, :], half_slot(n % RAW), split_0[:, n % 3, 0, :].bitcast(F32),
                              ALU.subtract).then_inc(in_lo, 1)

        def flat(x):
            return x.rearrange("p a n -> p (a n)")

        def widen(act, src, dst, count):
            act.wait_ge(inv_ready, count)
            act.activation(flat(dst).rearrange("p (h n) -> p h n", n=HD), along(src, HD), ACT.Copy)\
                .then_inc(wide_ready, 1)

        def head_rows(pe, src, bank):
            for c in range(NC):
                for i in range(WT):
                    at = c * NH + 2 * i
                    last = pe.matmul(ps[:, bank, at:at + 2], src[:, i, c * P:(c + 1) * P],
                                     const("blk").rearrange("p (h n) -> p h n", h=2)[:, :, 0],
                                     start=True, stop=True)
            return last

        def spread(pe, rows, bank):
            for i in range(WT):
                for c in range(NC):
                    last = pe.matmul(ps[:, bank + i // 2, (i % 2) * T + c * P:(i % 2) * T + (c + 1) * P],
                                     rows[:, c * WID + i * P:c * WID + (i + 1) * P], ident, start=True, stop=True)
            return last

        def pe_mix0(pe):
            pe.wait_ge(s_init, 32)
            pe_norm(pe, 0)
            pe.wait_ge(xp_lo, 4)
            for n in range(IN_STEPS):
                pe.wait_ge(in_lo, n + 1)
                w = split_0[:, n % 3, :, :].rearrange("p a (k n) -> p a k n", k=KT)
                if n < 9:
                    if n >= 4:
                        pe.wait_ge(in_act if n % 2 else in_dve, n // 2 - 1)
                    for i in range(2):
                        for j in range(KT):
                            for a, b in TERMS:
                                last = pe.matmul(ps[:, n % 4, i * T:(i + 1) * T], w[:, b, j, i * P:(i + 1) * P],
                                                 xn_parts_0[:, a, j, :],
                                                 start=j == a == b == 0, stop=j == KT - 1 and a == 1)
                else:
                    h = n - 9
                    for c in range(NC):
                        for j in range(KT):
                            for a, b in TERMS:
                                last = pe.matmul(ps[:, 4 + c, h * T:(h + 1) * T],
                                                 xn_parts_0[:, a, j, c * P:(c + 1) * P], w[:, b, j, :],
                                                 start=j == a == b == 0, stop=j == KT - 1 and a == 1)
                last.then_inc(in_done, 1)
            pe.wait_ge(s_b2, 16 * 8)
            pe.wait_ge(lora_act, 1)
            pe.wait_ge(in_act, 5)
            pe.wait_ge(in_dve, 4)
            for i in range(WT):
                last = pe.matmul(ps[:, i // 2, (i % 2) * T:(i % 2) * T + T], lora_wa[0:64, i * P:(i + 1) * P],
                                 pm[0:64, 12, :], start=True, stop=True)
            last.then_inc(wl_done, 1)
            for i in range(WT):
                last = pe.matmul(ps[:, 2 + i // 2, (i % 2) * T:(i % 2) * T + T],
                                 lora_wa[64:128, i * P:(i + 1) * P], pm[64:128, 12, :], start=True, stop=True)
            last.then_inc(al_done, 1)
            pe.wait_ge(kksq_ready, 1)
            head_rows(pe, kp, 6).then_inc(kksum_done, 1)
            pe.wait_ge(sig_ready, 1)
            pe.wait_ge(mixed, 1)
            for c in range(NC):
                for i in range(WT):
                    last = pe.transpose(ps[:, c, i * P:(i + 1) * P], pm[:, 8 + i, c * P:(c + 1) * P], ident)
                last.then_inc(rows_done, 1)
            pe.wait_ge(wide_ready, 1)
            spread(pe, flat(knorm), 6).then_inc(spread_done, 1)
            pe.wait_ge(ws_ready, 1)
            pe.wait_ge(gv_ready, 1)
            for c in range(NC):
                for g in range(WT):
                    o = ps[:, 4 + c, g * P:(g + 1) * P]
                    pe.matmul(o, v_rows[:, c, g * P:(g + 1) * P], ws_t[:, g, :], start=True, stop=False)
                    last = pe.matmul(o, const("one")[0:1, :], bs_row[0:1, g * P:(g + 1) * P],
                                     start=False, stop=True)
                last.then_inc(gs_done, 1)
            pe.wait_ge(ab_ready, 1)
            pe.wait_ge(ga_ready, 1)
            for n, src in enumerate((bt, kt)):
                for i in range(WT):
                    last = pe.transpose(ps[:, 2 + n, i * P:(i + 1) * P], src[:, i, 0:P], ident)
                last.then_inc(rows_done, 1)
            pe.wait_ge(b_head, 2)
            pe.wait_ge(k_head, 2)
            pe.wait_ge(r_ready, 1)
            for m in range(NH * NC):
                h, c = divmod(m, NC)
                if m == 2:
                    pe.wait_ge(rows_copied, 4)
                if m == 4:
                    pe.wait_ge(yb_ready, 2)
                if m >= 8:
                    pe.wait_ge(mat_ready, m - 7)
                for n in range(2):
                    last = pe.matmul(ps[:, m % 8, n * 2 * P:(n + 1) * 2 * P],
                                     bk_head[:, h % 2, n, h // 2, c * P:(c + 1) * P],
                                     ar[:, h // 2, c, :, :].rearrange("p a n -> p (a n)"),
                                     start=True, stop=True)
                last.then_inc(mat_done, 1)
            pe.wait_ge(mat_ready, NH * NC)
            for i in range(4 * LEVELS + 1):
                if i < 4 * LEVELS:
                    lev, q = divmod(i, 4)
                    pe.wait_ge(m_ready, i + 1)
                    if i >= 2:
                        pe.wait_ge(v_ready, i - 1)
                    if lev > 1:
                        pe.wait_ge(t_copied, i - 7)
                    elif lev == 1:
                        pe.wait_ge(v_ready, i - 3)
                    for j in range(4):
                        o = ps[:, i % 2, j * P:(j + 1) * P]
                        if lev == 0:
                            last = pe.transpose(o, inv_m[:, q, j, :], ident)
                        else:
                            last = pe.matmul(o, inv_m[:, q, j, :], inv_t[:, q, j, :], start=True, stop=True)
                    last.then_inc(u_done, 1)
                n = i - 1
                if n >= 4:
                    lev, q = divmod(n, 4)
                    pe.wait_ge(v_ready, n + 1)
                    if lev > 1:
                        pe.wait_ge(tt_copied, n - 7)
                    b = 2 + 2 * (n % 3)
                    if n >= 7:
                        pe.wait_ge(tt_copied, n - 6)
                        pe.wait_ge(t_copied, min(n - 6, 20))
                    for j in range(4):
                        if lev < LEVELS - 1:
                            pe.matmul(ps[:, b, j * P:(j + 1) * P], inv_tt[:, q, j, :], inv_v[:, q, j, :],
                                      start=True, stop=True)
                        last = pe.matmul(ps[:, b + 1, j * P:(j + 1) * P], inv_v[:, q, j, :],
                                         inv_tt[:, q, j, :], start=True, stop=True)
                    last.then_inc(tt_done, 1)
            pe.wait_ge(tt_copied, 24)
            def head_sums(src, b):
                for i in range(WT):
                    last = pe.matmul(ps[:, b + i // 2, (i % 2) * T:(i % 2) * T + T], const("blk"), src[:, i, :],
                                     start=True, stop=True)
                return last
            for c in range(NC):
                if c:
                    pe.wait_ge(st_ready, 2)
                for h in range(NH):
                    if c and h % 2 == 0:
                        pe.matmul(ps[:, 0, h * HD:(h + 2) * HD], ar[:, h // 2, c, 0, :],
                                  state[:, h // 2, :, :].rearrange("p a n -> p (a n)"), start=True, stop=False)
                    last = pe.matmul(ps[:, 0, h * HD:(h + 1) * HD], mats[:, 2 * h + c, 2, :],
                                     v_tok[:, c, h * HD:(h + 1) * HD], start=c == 0, stop=c == 0 or h % 2 == 1)
                last.then_inc(rhs_done, 1)
                if c == 0:
                    for i in range(WT):
                        last = pe.matmul(ps[:, 6 + i // 2, (i % 2) * T:(i % 2) * T + T],
                                         lora_g[:, i * P:(i + 1) * P], pm[:, 13, :], start=True, stop=True)
                    last.then_inc(bg_done, 1)
                else:
                    pe.wait_ge(bonus_ready, 1)
                    head_sums(bonus_in, 2).then_inc(bg_done, 1)
                pe.wait_ge(rhs_ready, c + 1)
                for h in range(NH):
                    m = 2 * h + c
                    last = pe.matmul(ps[:, 1, h * HD:(h + 1) * HD], inv_tt[:, m // 4, m % 4, :],
                                     rhs_tok[:, h * HD:(h + 1) * HD], start=True, stop=True)
                last.then_inc(sa_done, 1)
                pe.wait_ge(sa_ready, c + 1)
                if c == 0:
                    for h in range(NH):
                        lo, o = HD * (h % 2), ps[HD * (h % 2):HD * (h % 2) + HD, 2, (h // 2) * HD:(h // 2 + 1) * HD]
                        hs = slice(h * HD, (h + 1) * HD)
                        pe.matmul(o, bk_tok[:, 0, hs], sa_tok[:, hs], start=True, stop=False)
                        last = pe.matmul(o, bk_tok[:, 1, hs], v_tok[:, 0, hs], start=False, stop=True)
                    last.then_inc(st_done, 1)
                for h in range(NH):
                    lo, m = HD * (h % 2), 2 * h + c
                    if c and h % 2 == 0:
                        pe.matmul(ps[:, 4 + c, (h // 2) * P:(h // 2 + 1) * P],
                                  state[:, h // 2, :, :].rearrange("p a n -> p (a n)"),
                                  ar[:, h // 2, c, 1, :], start=True, stop=False)
                    o = ps[lo:lo + HD, 4 + c, (h // 2) * P:(h // 2 + 1) * P]
                    hs = slice(h * HD, (h + 1) * HD)
                    pe.matmul(o, sa_tok[:, hs], mats[:, m, 1, :], start=c == 0, stop=False)
                    last = pe.matmul(o, v_tok[:, c, hs], mats[:, m, 3, :], start=False, stop=True)
                last.then_inc(yk_done, 1)
            pe.wait_ge(ysum_in, 1)
            head_sums(y_cols, 0).then_inc(ysum_done, 1)
            for i in range(2):
                pe.wait_ge(loaded[i], 16)
            pe.wait_ge(gate_copied, 1)
            pe_out(pe, True, 1, range(0, 3))
            pe.wait_ge(ysum_in, 2)
            head_rows(pe, y_sq, 0).then_inc(ysum_done, 1)
            pe_out(pe, True, 1, range(3, 6))
            pe.wait_ge(wide_ready, 2)
            spread(pe, flat(y_sq), 2).then_inc(spread_done, 1)
            pe_out(pe, True, 1, range(6, 16))
            pe.wait_ge(ya_ready, 1)
            pe_out(pe, False, 0)

        def act_mix0(act, order):
            act.wait_ge(bk_zero, 1)
            order.then(act.activation(y_std[:, 0:1], k_norm[:, 0:1], ACT.Sqrt))
            act_norm(act, order, 0)
            in_high(act, 0)
            act_xn_high(act, 0, xn_parts_0)
            in_high(act, 1)
            in_high(act, 2)
            for n in range(IN_STEPS):
                act.wait_ge(in_done, n + 1)
                if n + 3 < IN_STEPS:
                    in_high(act, n + 3)
                if n == 3:
                    act_angles(act)
                bank = ps[:, n % 4, :].rearrange("p (a n) -> p a n", a=2)
                if n in (1, 3, 5):
                    act.activation(praw[:, 2 * n:2 * n + 2, :], bank, ACT.Copy).then_inc(in_act, 1)
                if n in (7, 8):
                    act.activation(u_cols[:, 2 * n - 14:2 * n - 12, :], bank, ACT.Gelu_apprx_tanh)\
                        .then_inc(in_act, 1)
                if n == 9:
                    act.wait_ge(lora_mixed, 2)
                    order.mark(act.activation(pm[:, 13, :], pm[:, 13, :], ACT.Sigmoid))
                    order.mark(act.activation(pm[0:64, 12, :], pm[0:64, 12, :], ACT.Tanh))
                    order.join()
                    act.nop().then_inc(lora_act, 1)
            for c in range(NC):
                act.activation(v_rows[:, c, :], ps[:, 4 + c, :], ACT.Gelu_apprx_tanh).then_inc(in_act, 1)
            act.wait_ge(wl_done, 1)
            act.wait_ge(mixed, 1)
            for i in range(WT):
                order.mark(act.activation(sig_w[:, i, :], ps[:, i // 2, (i % 2) * T:(i % 2) * T + T], ACT.Sigmoid,
                                          bias=vec("w0")[:, i:i + 1]))
            order.join()
            act.nop().then_inc(sig_ready, 1)
            act.wait_ge(al_done, 1)
            for i in range(WT):
                order.mark(act.activation(gate_a[:, i, :], ps[:, 2 + i // 2, (i % 2) * T:(i % 2) * T + T],
                                          ACT.Sigmoid, bias=vec("a0")[:, i:i + 1]))
            order.join()
            act.nop().then_inc(ga_ready, 1)
            act.wait_ge(kksum_done, 1)
            act.activation(k_norm, ps[:, 6, 0:NC * NH], ACT.Sqrt).then_inc(knorm_ready, 1)
            act.wait_ge(gv_stats, 1)
            act.activation(bn2[:, :, 1], bn2[:, :, 1], ACT.Sqrt, bias=eps_col).then_inc(gv_root, 1)
            widen(act, k_norm, knorm, 1)
            for c in range(NC):
                act.wait_ge(rows_done, c + 1)
                act.activation(v_tok[:, c, :], ps[:, c, :], ACT.Copy).then_inc(rows_copied, 1)
            act.wait_ge(cs_ready, 1)
            act.activation(e_dec, csc, ACT.Exp, scale=-K_DECAY).then_inc(exps_ready, 1)
            act.activation(e_prev, csm, ACT.Exp, scale=-K_DECAY).then_inc(exps_ready, 1)
            act.activation(e_inv, csc, ACT.Exp, scale=K_DECAY).then_inc(exps_ready, 1)
            act.wait_ge(half_ready, 1)
            act.activation(state_scale, state_scale, ACT.Exp, scale=-K_DECAY).then_inc(scale_ready, 1)
            act.wait_ge(ab_ready, 1)
            act.wait_ge(bk_zero, 2)
            for n in range(2):
                lo = slice(n * HD, (n + 1) * HD)
                act.activation(bk_head[lo, n, 0, :, :], bt[lo], ACT.Copy).then_inc(b_head, 1)
            for n in range(2):
                act.wait_ge(rows_done, 3 + n)
                act.activation(bk_tok[:, n, :], ps[:, 2 + n, :], ACT.Copy).then_inc(rows_copied, 1)
            for n in range(4, 4 * (LEVELS - 1)):
                act.wait_ge(tt_done, n - 3)
                act.activation(inv_t[:, n % 4, :, :].rearrange("p a n -> p (a n)"), ps[:, 2 + 2 * (n % 3), :],
                               ACT.Copy).then_inc(t_copied, 1)
            for c in range(NC):
                act.wait_ge(rhs_done, c + 1)
                act.activation(rhs_tok, ps[:, 0, :], ACT.Copy).then_inc(rhs_ready, 1)
                if c == 0:
                    act.wait_ge(bg_done, 1)
                    act.activation(gate, ps[:, 6:8, :].rearrange("p b (a n) -> p (b a) n", a=2), ACT.Copy)\
                        .then_inc(gate_copied, 1)
                act.wait_ge(sa_done, c + 1)
                act.activation(sa_tok, ps[:, 1, :], ACT.Copy).then_inc(sa_ready, 1)
            act.wait_ge(gn_root, 1)
            order.then(act.activation(y_sq, y_cols, ACT.Square))
            act.nop().then_inc(ysum_in, 1)
            act.wait_ge(ysum_done, 2)
            order.then(act.activation(y_std, ps[:, 0, 0:NC * NH], ACT.Sqrt, scale=1.0 / HD, bias=gn_eps_col))
            act.nop().then_inc(gn_root, 1)
            widen(act, y_std, y_sq, 2)
            act.wait_ge(ya_ready, 1)
            for n in range(2):
                f_high(act, n, 0)
            act_post(act, order, 0)

        def dve_mix0(dve, order):
            dve.wait_ge(s_init, 32)
            for c in range(NC):
                dve.wait_ge(s_x[c], 16)
            dve_norm(dve, order, 0, vec("g_mix0"), lambda: in_low(dve, 0))
            dve_xn_low(dve, 0, xn_parts_0)
            for n in range(1, 3):
                in_low(dve, n)
            for n in range(8):
                if n % 2 == 0:
                    dve.wait_ge(in_done, n + 1)
                    dve.tensor_copy(praw[:, 2 * n:2 * n + 2, :],
                                    ps[:, n % 4, :].rearrange("p (a n) -> p a n", a=2)).then_inc(in_dve, 1)
                in_low(dve, n + 3)
                if n == 3:
                    dve_angles(dve, order)
            dve.wait_ge(in_act, 3)
            dve.wait_ge(in_dve, 4)
            def mix(lo, hi, signal):
                order.mark(dve.tensor_tensor(pm[:, lo:hi, 1:T], praw[:, lo:hi, 0:T - 1], praw[:, lo:hi, 1:T],
                                             ALU.subtract))
                order.then(dve.tensor_scalar(pm[:, lo:hi, 0], praw[:, lo:hi, 0], -1.0, None, ALU.mult))
                for i in range(lo, hi):
                    ins = dve.scalar_tensor_tensor(pm[:, i, :], pm[:, i, :], vec("mu")[:, i:i + 1],
                                                   praw[:, i, :], ALU.mult, ALU.add)
                    if signal is None:
                        order.mark(ins)
                    else:
                        ins.then_inc(signal, 1)
            mix(12, 14, lora_mixed)
            mix(4, 8, None)
            mix(0, 4, None)
            mix(8, 12, None)
            order.join()
            dve.nop().then_inc(mixed, 1)
            dve.wait_ge(in_done, 11)
            k_cols, r_cols = pm[:, 4:8, :], pm[:, 0:4, :]
            order.then(dve.tensor_tensor(kk, k_cols, along(vec("k_k"), T), ALU.mult))
            dve.tensor_tensor(kp, kk, kk, ALU.mult).then_inc(kksq_ready, 1)
            dve.wait_ge(s_b2, 16 * 8)
            dve.wait_ge(in_act, 7)
            dve.tensor_tensor(ws_t, ws_t, across(const("le"), WT), ALU.mult).then_inc(ws_ready, 1)
            for c in range(NC):
                for g in range(WT):
                    order.mark(dve.bn_stats(bn6[:, c * WT + g, :], v_rows[:, c, g * P:(g + 1) * P]))
            order.join()
            for i in range(NC * WT):
                order.mark(dve.bn_aggr(bn2[:, i, :], bn6[:, i, :]))
            order.join()
            dve.nop().then_inc(gv_stats, 1)
            dve.wait_ge(sig_ready, 1)
            for i in range(WT):
                for c in range(NC):
                    s = slice(c * P, (c + 1) * P)
                    order.mark(dve.tensor_tensor_scan(cs[:, i, s], const("one")[:, 0:1].broadcast_to([P, P]),
                                                      sig_w[:, i, s], 0.0, ALU.mult, ALU.add))
            order.join()
            cs4 = cs.rearrange("p i (c n) -> p i c n", c=NC)
            order.then(dve.tensor_scalar(half_sum, cs4[:, :, :, P - 1], 0.5, None, ALU.mult))
            for c in range(NC):
                order.mark(dve.tensor_tensor(csc.rearrange("p i (c n) -> p i c n", c=NC)[:, :, c, :],
                                             cs4[:, :, c, :], along(half_sum[:, :, c], P), ALU.subtract))
            order.join()
            dve.tensor_tensor(csm, csc, sig_w, ALU.subtract).then_inc(cs_ready, 1)
            dve.tensor_tensor(state_scale, half_sum[:, :, 0], half_sum[:, :, 1], ALU.add).then_inc(half_ready, 1)
            dve.wait_ge(knorm_ready, 1)
            order.then(dve.tensor_scalar(k_norm, k_norm, 1e-12, None, ALU.max))
            dve.reciprocal(k_norm, k_norm).then_inc(inv_ready, 1)
            dve.wait_ge(gv_root, 1)
            order.then(dve.reciprocal(bn2[:, :, 1], bn2[:, :, 1]))
            for c in range(NC):
                for g in range(WT):
                    v = v_rows[:, c, g * P:(g + 1) * P]
                    i = c * WT + g
                    order.mark(dve.tensor_scalar(v, v, bn2[:, i, 0:1], bn2[:, i, 1:2], ALU.subtract, ALU.mult))
            order.join()
            order.then(dve.tensor_tensor(v_rows, v_rows, across(gln[:, 0, :], NC), ALU.mult))
            dve.tensor_tensor(v_rows, v_rows, across(gln[:, 1, :], NC), ALU.add).then_inc(gv_ready, 1)
            dve.wait_ge(spread_done, 1)
            order.then(dve.tensor_tensor(kk, kk, ps[:, 6:8, :].rearrange("p b (a n) -> p (b a) n", a=2), ALU.mult))
            dve.wait_ge(ga_ready, 1)
            for i in range(WT):
                order.mark(dve.tensor_scalar(knorm[:, i, :], gate_a[:, i, :], -1.0, vec("k_a")[:, i:i + 1],
                                             ALU.add, ALU.mult))
            order.join()
            order.then(dve.scalar_tensor_tensor(kp, knorm, 1.0, k_cols, ALU.add, ALU.mult))
            dve.wait_ge(exps_ready, 3)
            def by_chunk(x):
                return x.rearrange("p i (c n) -> p i c n", c=NC)
            order.mark(dve.scalar_tensor_tensor(ar[:, :, :, 0, :], by_chunk(kk), -1.0, by_chunk(e_prev),
                                                ALU.mult, ALU.mult))
            order.mark(dve.tensor_tensor(kt, kp, e_inv, ALU.mult))
            order.then(dve.tensor_tensor(bt, kk, gate_a, ALU.mult))
            order.then(dve.tensor_tensor(bt, bt, e_inv, ALU.mult))
            dve.nop().then_inc(ab_ready, 1)
            dve.wait_ge(bk_zero, 2)
            for n in range(2):
                lo = slice(n * HD, (n + 1) * HD)
                dve.tensor_copy(bk_head[lo, n, 1, :, :], kt[lo]).then_inc(k_head, 1)
            dve.tensor_tensor(bonus_in, r_cols, kp, ALU.mult).then_inc(kp_used, 1)
            dve.wait_ge(kp_used, 1)
            dve.tensor_tensor(bonus_in, bonus_in, along(vec("r_k"), T), ALU.mult).then_inc(bonus_ready, 1)
            for c in range(NC):
                dve.wait_ge(gs_done, c + 1)
                dve.tensor_tensor(y8[:, WT:KT, c * P:(c + 1) * P], u_cols[:, :, c * P:(c + 1) * P],
                                  ps[:, 4 + c, :].rearrange("p (g n) -> p g n", g=WT), ALU.mult)\
                    .then_inc(yb_ready, 1)
            for m in range(NH * NC):
                dve.wait_ge(mat_zero, m + 1)
                dve.wait_ge(mat_done, m + 1)
                for n in range(2):
                    ins = dve.copy_predicated(mats[:, m, 2 * n:2 * n + 2, :].rearrange("p a n -> p (a n)"),
                                              mask_ar, ps[:, m % 8, n * 2 * P:(n + 1) * 2 * P])
                    if n == 0:
                        order.mark(ins)
                    else:
                        ins.then_inc(mat_ready, 1)
            order.join()
            id4 = across(ident, 4)
            for i in range(4 * LEVELS + 1):
                if i < 4 * LEVELS:
                    lev, q = divmod(i, 4)
                    dve.wait_ge(u_done, i + 1)
                    u = ps[:, i % 2, :].rearrange("p (a n) -> p a n", a=4)
                    if lev == 0:
                        order.mark(dve.tensor_tensor(inv_tt[:, q], inv_m[:, q], id4, ALU.add))
                        order.join()
                        dve.tensor_tensor(inv_t[:, q], u, id4, ALU.add).then_inc(v_ready, 1)
                    else:
                        if lev > 1:
                            dve.wait_ge(tt_done, i - 7)
                        dve.tensor_tensor(inv_v[:, q], u, id4, ALU.add).then_inc(v_ready, 1)
                n = i - 1
                if n >= 4:
                    dve.wait_ge(tt_done, n - 3)
                    dve.tensor_copy(inv_tt[:, n % 4].rearrange("p a n -> p (a n)"), ps[:, 3 + 2 * (n % 3), :])\
                        .then_inc(tt_copied, 1)
            order.then(dve.memset(state, 0.0))
            dve.wait_ge(st_done, 1)
            dve.wait_ge(scale_ready, 1)
            for n in range(2):
                lo = slice(n * HD, (n + 1) * HD)
                dve.tensor_tensor(state[lo, :, n, :], ps[lo, 2, 0:WT * HD].rearrange("p (a n) -> p a n", a=WT),
                                  along(state_scale[lo], HD), ALU.mult).then_inc(st_ready, 1)
            dve.wait_ge(yk_done, 2)
            for c in range(NC):
                order.mark(dve.tensor_copy(y_cols[:, :, c * P:(c + 1) * P],
                                           ps[:, 4 + c, :].rearrange("p (a n) -> p a n", a=WT)))
            order.join()
            dve.nop().then_inc(ysum_in, 1)
            dve.wait_ge(ysum_done, 1)
            def bank2(b):
                return ps[:, b:b + 2, :].rearrange("p b (a n) -> p (b a) n", a=2)
            order.then(dve.scalar_tensor_tensor(y_cols, bank2(0), -1.0 / HD, y_cols, ALU.mult, ALU.add))
            dve.nop().then_inc(gn_root, 1)
            dve.wait_ge(bg_done, 2)
            order.then(dve.tensor_tensor(bonus_in, bank2(2), pm[:, 8:12, :], ALU.mult))
            dve.wait_ge(gn_root, 2)
            dve.reciprocal(y_std, y_std).then_inc(inv_ready, 1)
            dve.wait_ge(spread_done, 2)
            order.then(dve.tensor_tensor(y_cols, y_cols, bank2(2), ALU.mult))
            for i in range(WT):
                order.mark(dve.tensor_scalar(y_cols[:, i, :], y_cols[:, i, :], vec("ln_w")[:, i:i + 1],
                                             vec("ln_b")[:, i:i + 1], ALU.mult, ALU.add))
            order.join()
            order.then(dve.tensor_tensor(y_cols, y_cols, bonus_in, ALU.add))
            dve.wait_ge(gate_copied, 1)
            dve.tensor_tensor(y8[:, 0:WT, :], gate, y_cols, ALU.mult).then_inc(ya_ready, 1)
            for n in range(2):
                f_low(dve, n, 0)
            dve_post(dve, order, 0)

        def pool_mix0(pool, order):
            pool.memset(k_norm, 0.0).then_inc(bk_zero, 1)
            pool.memset(tables[:, 4096:8192], 0.0).then_inc(bk_zero, 1)
            pool.wait_ge(mixed, 1)
            pool.wait_ge(exps_ready, 1)
            by_chunk = lambda x: x.rearrange("p i (c n) -> p i c n", c=NC)
            pool.tensor_tensor(ar[:, :, :, 1, :], by_chunk(pm[:, 0:4, :]), by_chunk(e_dec), ALU.mult)\
                .then_inc(r_ready, 1)
            pool.wait_ge(gs_done, 2)
            pool.dma_start(gain_rows[:, :], t["gain_mix0"]).then_inc(s_gain, 16)
            pool.wait_ge(ab_ready, 1)
            pool.wait_ge(r_ready, 1)
            for m in range(NH * NC):
                if m == 12:
                    pool.wait_ge(kp_used, 1)
                pool.memset(mats[:, m, :, :], 0.0).then_inc(mat_zero, 1)
            pool.wait_ge(mat_ready, NH * NC)
            for i in range(4 * LEVELS):
                lev, q = divmod(i, 4)
                if lev:
                    pool.wait_ge(u_done, i - 3)
                    if lev == 1:
                        pool.wait_ge(v_ready, i - 3)
                pool.tensor_tensor(inv_m[:, q], mats[:, 4 * q:4 * q + 4, 0, :], across(inv_mask[:, lev, :], 4),
                                   ALU.mult).then_inc(m_ready, 1)

        PAIRS = FT // 2
        F_STEPS = 3 * PAIRS
        F_LOOPS = (F_STEPS - 9) // 6

        def f_step(n):
            if n < 2:
                return ("gate", "up")[n], 0
            if n == F_STEPS - 1:
                return "down", PAIRS - 1
            return (("up", n // 3), ("down", (n - 4) // 3), ("gate", (n + 1) // 3))[n % 3]

        def f_half(n):
            i = (n + 4) % RAW
            return i, half_slot(i)

        def f_loads(n, r=0):
            before = sum(m % RAW == f_half(n)[0] for m in range(IN_STEPS))
            return r * 16 + 16 * (before + n // RAW + 1)

        def f_high(act, n, r):
            i, raw = f_half(n)
            act.wait_ge(half_loaded[i], f_loads(n, r))
            act.activation(split[:, n % 3, 0, :], raw, ACT.Copy).then_inc(f_hi, 1)

        def f_low(dve, n, r):
            dve.wait_ge(f_hi, r * 6 + (n + 1))
            dve.tensor_tensor(split[:, n % 3, 1, :], f_half(n)[1], split[:, n % 3, 0, :].bitcast(F32),
                              ALU.subtract).then_inc(f_lo, 1)

        def f_steps(engine, first, body):
            with engine.Fori(0, F_LOOPS) as r:
                for n in range(first, first + 6):
                    body(n, r)
            for n in range(first + 6 * F_LOOPS, F_STEPS):
                body(n, 0)

        def pe_ffn(pe):
            pe_norm(pe, 1)
            pe.wait_ge(xp_lo, 8)

            def step(n, r):
                kind, p = f_step(n)
                if kind == "down":
                    pe.wait_ge(fh_lo, r * 2 + (p + 1))
                pe.wait_ge(f_lo, r * 6 + (n + 1))
                w = split[:, n % 3, :, :]
                if kind == "down":
                    w = w.rearrange("p a (i d) -> p a i d", i=2)
                    for i in range(2):
                        for c in range(NC):
                            for a, b in TERMS:
                                for h in range(2):
                                    last = pe.matmul(ps[:, 4 + 2 * c + h, :],
                                                     act_parts[:, p % 2, a, i, c * P:(c + 1) * P],
                                                     w[:, b, i, h * NB:(h + 1) * NB],
                                                     start=n == 4 and i == a == b == 0,
                                                     stop=n == F_STEPS - 1 and i == a == 1)
                            if n == F_STEPS - 1 and i == 1:
                                last.then_inc(y_done, 1)
                else:
                    w = w.rearrange("p a (k n) -> p a k n", k=KT)
                    for i in range(2):
                        for j in range(KT):
                            for a, b in TERMS:
                                last = pe.matmul(ps[:, 2 * (p % 2) + (kind == "up"), i * T:(i + 1) * T],
                                                 w[:, b, j, i * P:(i + 1) * P], xn_parts[:, a, j, :],
                                                 start=j == a == b == 0, stop=j == KT - 1 and a == 1)
                if n < F_STEPS - 1:
                    last.then_inc(f_done, 1)
            for n in range(6):
                step(n, 0)
            f_steps(pe, 6, step)

        def act_ffn(act, order):
            act_norm(act, order, 1)

            act_xn_high(act, 1, xn_parts)
            f_high(act, 2, 0)

            def after(n, r):
                kind, p = f_step(n)
                act.wait_ge(f_done, r * 6 + (n + 1))
                if n + 3 < F_STEPS:
                    f_high(act, n + 3, r)
                if kind == "gate":
                    act.activation(f_h[p % 2], ps[:, 2 * (p % 2), :].rearrange("p (i n) -> p i n", i=2),
                                   ACT.Silu).then_inc(f_silu_ready, 1)
                if kind == "up":
                    act.wait_ge(f_h_ready, r * 2 + (p + 1))
                    act.activation(act_parts[:, p % 2, 0, :, :], f_h[p % 2], ACT.Copy).then_inc(fh_hi, 1)
            with_last(act, after)
            act_post(act, order, 1)

        def with_last(engine, after):
            for n in range(2):
                after(n, 0)
            with engine.Fori(0, F_LOOPS) as r:
                for n in range(2, 8):
                    after(n, r)
            for n in range(2 + 6 * F_LOOPS, F_STEPS - 1):
                after(n, 0)

        def dve_ffn(dve, order):
            dve_norm(dve, order, 1, vec("g_ffn0"))

            dve_xn_low(dve, 1, xn_parts)
            f_low(dve, 2, 0)

            def after(n, r):
                kind, p = f_step(n)
                b = p % 2
                if kind == "up":
                    dve.wait_ge(f_silu_ready, r * 2 + (p + 1))
                    dve.wait_ge(f_done, r * 6 + (n + 1))
                    dve.tensor_tensor(f_h[b], f_h[b], ps[:, 2 * b + 1, :].rearrange("p (i n) -> p i n", i=2),
                                      ALU.mult).then_inc(f_h_ready, 1)
                if n + 3 < F_STEPS:
                    f_low(dve, n + 3, r)
                if kind == "up":
                    dve.wait_ge(fh_hi, r * 2 + (p + 1))
                    dve.tensor_tensor(act_parts[:, b, 1, :, :], f_h[b], act_parts[:, b, 0, :, :].bitcast(F32),
                                      ALU.subtract).then_inc(fh_lo, 1)
            with_last(dve, after)
            dve_post(dve, order, 1)

        def sp_ffn(sp):
            sp.wait_ge(ya_ready, 1)
            gate_d = t["l0_ffn_w_gate"].rearrange("(k p) n -> p k n", p=P)
            up_d = t["l0_ffn_w_up"].rearrange("(k p) n -> p k n", p=P)
            down_d = t["l0_ffn_w_down"]

            def load(n, r):
                kind, p = f_step(n)
                i, raw = f_half(n)
                if n == 2:
                    sp.wait_ge(y_done, 2)
                if n >= RAW:
                    sp.wait_ge(f_lo, r * 6 + (n - RAW + 1))
                rows = bass.ds(r * (4 * P) + p * 2 * P, 2 * P)
                if kind == "down":
                    src = down_d[rows, :].rearrange("(i p) d -> p i d", i=2)
                else:
                    src = (gate_d if kind == "gate" else up_d)[:, :, rows]
                sp.dma_start(raw.rearrange("p (a n) -> p a n", a=src.shape[1]), src).then_inc(half_loaded[i], 16)
            for n in range(6):
                load(n, 0)
            f_steps(sp, 6, load)

        TWO_PI = (6.28125, 1.9350051879882812e-3, 3.0199159819567529e-7)
        MAGIC = 1.5 * 2.0 ** 23
        PI_LOW = 3.14159250

        def act_angles(act):
            act.wait_ge(s_init, 32)
            act.activation(s5_dt, vec("log_dt"), ACT.Exp).then_inc(ang_ready, 1)
            act.wait_ge(ang_reduced, 1)
            act.activation(s5_mag, s5_mag, ACT.Exp).then_inc(rot_ready, 1)
            act.activation(rot_s[:, :, :], turns[:, :, :], ACT.Sin).then_inc(rot_ready, 1)
            act.activation(rot_c[:, :, :], angle[:, :, :], ACT.Sin, scale=-1.0, bias=const("eps")[:, 2:3])\
                .then_inc(rot_ready, 1)

        def dve_angles(dve, order):
            dve.wait_ge(s_init, 32)
            dve.wait_ge(ang_ready, 1)
            order.mark(dve.tensor_tensor(s5_mag, vec("a_re"), s5_dt, ALU.mult))
            order.then(dve.tensor_tensor(angle[:, 0, :], vec("a_im"), s5_dt, ALU.mult))
            for k in range(1, LEVELS + 1):
                order.mark(dve.tensor_scalar(angle[:, k, :], angle[:, 0, :], float(2 ** k), None, ALU.mult))
            order.join()
            order.then(dve.tensor_scalar(turns[:, :, :], angle[:, :, :], 1.0 / (2 * math.pi), MAGIC,
                                         ALU.mult, ALU.add))
            order.then(dve.tensor_scalar(turns[:, :, :], turns[:, :, :], MAGIC, None, ALU.subtract))
            for part in TWO_PI:
                order.then(dve.scalar_tensor_tensor(angle[:, :, :], turns[:, :, :], -part, angle[:, :, :],
                                                    ALU.mult, ALU.add))
            order.then(dve.tensor_scalar(turns[:, :, :], angle[:, :, :], PI_LOW, -PI_LOW, ALU.min, ALU.max))
            dve.scalar_tensor_tensor(angle[:, :, :], turns[:, :, :], -1.0, turns[:, :, :],
                                     ALU.mult, ALU.max).then_inc(ang_reduced, 1)
            dve.wait_ge(rot_ready, 3)
            lr, li = vec("a_re"), vec("a_im")
            order.mark(dve.tensor_tensor(s5_nr, s5_mag, rot_c[:, 0, :], ALU.mult))
            order.mark(dve.tensor_tensor(s5_ni, s5_mag, rot_s[:, 0, :], ALU.mult))
            order.mark(dve.tensor_tensor(f_re, lr, lr, ALU.mult))
            order.then(dve.tensor_tensor(f_im, li, li, ALU.mult))
            order.mark(dve.tensor_scalar(s5_nr, s5_nr, -1.0, None, ALU.add))
            order.then(dve.tensor_tensor(s5_den, f_re, f_im, ALU.add))
            order.mark(dve.reciprocal(s5_den, s5_den))
            order.mark(dve.tensor_tensor(f_re, s5_nr, lr, ALU.mult))
            order.mark(dve.tensor_tensor(f_im, s5_ni, lr, ALU.mult))
            order.join()
            order.mark(dve.tensor_tensor(s5_ni, s5_ni, li, ALU.mult))
            order.then(dve.tensor_tensor(s5_nr, s5_nr, li, ALU.mult))
            order.mark(dve.tensor_tensor(f_re, f_re, s5_ni, ALU.add))
            order.then(dve.tensor_tensor(f_im, f_im, s5_nr, ALU.subtract))
            order.mark(dve.tensor_tensor(f_re, f_re, s5_den, ALU.mult))
            order.then(dve.tensor_tensor(f_im, f_im, s5_den, ALU.mult))

        def pool_rotations(pool, order):
            pool.wait_ge(ya_ready, 1)
            pool.wait_ge(rot_ready, 3)
            order.mark(pool.memset(cos_t[:, :, 0:1], 1.0))
            order.then(pool.memset(sin_t[:, :, 0:1], 0.0))
            for k in range(LEVELS + 1):
                m = 2 ** k
                lo, hi = slice(0, m), slice(m, 2 * m)
                c, s = along(rot_c[:, k, :], m), along(rot_s[:, k, :], m)
                t1, t2 = (x[:, 0:S5_TILES * m].rearrange("p (j n) -> p j n", j=S5_TILES) for x in rot_tmp)
                order.mark(pool.tensor_tensor(t1, cos_t[:, :, lo], c, ALU.mult))
                order.then(pool.tensor_tensor(t2, sin_t[:, :, lo], s, ALU.mult))
                order.then(pool.tensor_tensor(cos_t[:, :, hi], t1, t2, ALU.subtract))
                order.mark(pool.tensor_tensor(t1, cos_t[:, :, lo], s, ALU.mult))
                order.then(pool.tensor_tensor(t2, sin_t[:, :, lo], c, ALU.mult))
                order.then(pool.tensor_tensor(sin_t[:, :, hi], t1, t2, ALU.add))
            pool.nop().then_inc(rot_table, 1)

        def in1_half(job):
            i = f_half(F_STEPS + job)[0] if job < 6 else job
            return i, half_slot(i).rearrange("p (k n) -> p k n", k=KT)

        def sp_mix1(sp):
            w = t["l1_w_in"].rearrange("(k p) n -> p k n", p=P)
            for job in range(8):
                i, half = in1_half(job)
                if job < 6:
                    sp.wait_ge(f_lo, F_STEPS + job - RAW + 1)
                else:
                    sp.wait_ge(f_done, F_STEPS - 2)
                sp.dma_start(half, w[:, :, job * T:(job + 1) * T]).then_inc(half_loaded[i], 16)
            sp.wait_ge(y_done, 4)
            sp.dma_start(b_in, t["s5_b"].rearrange("a p j n -> p a j n")).then_inc(s5_loaded, 16)
            sp.dma_start(c_in, t["s5_c"].rearrange("a p j n -> p a j n")).then_inc(s5_loaded, 16)
            w = t["l1_w_out"].rearrange("(k p) n -> p k n", p=P)
            sp.wait_ge(dt_done, 1)
            sp.dma_start(glu_w, t["l1_s5_glu_w"].rearrange("(k p) n -> p k n", p=P)).then_inc(s5_loaded, 16)
            for s in range(2):
                sp.dma_start(slot_tiles(s), w[:, :, s * NB:(s + 1) * NB]).then_inc(loaded[s], 16)

        def pe_mix1(pe):
            pe_norm(pe, 2)
            pe.wait_ge(xn_ready, 12)

            def in_job(job):
                if job >= 4:
                    pe.wait_ge(p1_ready, job - 3)
                for i in (2 * job, 2 * job + 1):
                    n, w = in1_half(job)
                    pe.wait_ge(half_loaded[n], f_loads(F_STEPS + job) if job < 6 else 16)
                    for j in range(KT):
                        last = pe.matmul(ps[:, 4 + job % 4, (i % 2) * T:(i % 2) * T + T],
                                         w[:, j, (i % 2) * P:(i % 2) * P + P], xn[:, j, :],
                                         start=j == 0, stop=j == KT - 1)
                last.then_inc(p1_done, 1)

            def bu(g):
                if g:
                    pe.wait_ge(v_done, g)
                for q in range(4):
                    for n in range(2):
                        last = pe.matmul(ps[:, q, n * T:(n + 1) * T], b_in[32 * q:32 * q + 32, n, g, :],
                                         p1[32 * q:32 * q + 32, g, :], start=True, stop=True)
                last.then_inc(bu_done, 1)

            def s5_y(g):
                pe.wait_ge(c_ready, 2)
                pe.wait_ge(q_done, g + 1)
                if g == 3:
                    pe.wait_ge(last_re, 1)
                for q in range(4):
                    o = ps[32 * q:32 * q + 32, 4 + g // 2, (g % 2) * T:(g % 2) * T + T]
                    z_re_sin, z_im_sin = z_bufs[g % 2]
                    terms = ((c_out[:, 0], z_re_cos), (c_minus, z_im_sin), (c_out[:, 1], z_im_cos),
                             (c_out[:, 1], z_re_sin))
                    for n, (c_map, part) in enumerate(terms):
                        last = pe.matmul(o, c_map[:, 4 * g + q, :], part[:, q, :], start=n == 0, stop=n == 3)
                last.then_inc(y5_done, 1)

            in_job(0)
            in_job(1)
            pe.wait_ge(p1_ready, 2)
            pe.wait_ge(s5_loaded, 32)
            bu(0)
            for job in range(2, 8):
                in_job(job)
                if job == 4:
                    bu(1)
            pe.wait_ge(p1_ready, 5)
            s5_y(0)
            pe.wait_ge(p1_ready, 6)
            pe.wait_ge(s_b2, 16 * 8)
            for c in range(NC):
                for j in range(KT):
                    last = pe.matmul(ps[:, 5, c * NH:(c + 1) * NH], xn[:, j, c * P:(c + 1) * P],
                                     w_small[:, 0, j, :], start=j == 0, stop=j == KT - 1)
            last.then_inc(dt_done, 1)
            bu(2)
            pe.wait_ge(p1_ready, 8)
            pe.wait_ge(xc_ready, 2)
            for c in range(NC):
                for i in range(WT):
                    last = pe.transpose(ps[:, 6 + c, i * P:(i + 1) * P], xc[:, i, c * P:(c + 1) * P], ident)
                last.then_inc(jobs, 1)
            pe.wait_ge(ssd_dve, 1)
            for g in range(2):
                last = pe.transpose(ps[:, 6, g * P:(g + 1) * P], xc[:, WT + g, 0:P], ident)
            last.then_inc(jobs, 1)
            for n in range(4):
                c, g = divmod(n, 2)
                pe.wait_ge(seg_ready, c + 1)
                if n == 0:
                    pe.wait_ge(ssd_dve, 2)
                else:
                    pe.wait_ge(ssd_act, n)
                for h in range(4):
                    last = pe.matmul(ps[:, 7 - n % 2, h * P:(h + 1) * P], seg_in[:, c, 4 * g + h, :], const("le"),
                                     start=True, stop=True)
                last.then_inc(jobs, 1)
            pe.wait_ge(ssd_act, 4)
            for c in range(NC):
                for g in range(2):
                    s = slice(c * P, (c + 1) * P)
                    last = pe.matmul(ps[:, 7, (2 * c + g) * P:(2 * c + g + 1) * P], xc[:, WT + g, s],
                                     xc[:, WT + 2 + g, s], start=True, stop=True)
            last.then_inc(jobs, 1)
            pe.wait_ge(ssd_act, 5)
            last = pe.matmul(ps[:, 6, 0:NH], const("gt"), adt[:, 0:NH], start=True, stop=True)
            last.then_inc(jobs, 1)
            s5_y(1)
            bu(3)
            pe.wait_ge(seg_ready, 3)
            pe.wait_ge(ssd_dve, 3)
            pe.wait_ge(ssd_act, 6)
            for g in range(2):
                for h in range(4):
                    last = pe.matmul(ps[:, 7 - g, h * P:(h + 1) * P], acs_in[:, 4 * g + h, :], const("le"),
                                     start=True, stop=True)
                last.then_inc(jobs, 1)
            pe.wait_ge(ssd_act, 7)
            pe.wait_ge(xdec_ready, 1)
            for g in range(2):
                last = pe.matmul(ps[:, 7, g * T:(g + 1) * T], b_rows[:, g * P:(g + 1) * P],
                                 xdec[:, g * T:(g + 1) * T], start=True, stop=True)
            last.then_inc(jobs, 1)
            s5_y(2)
            pe.wait_ge(mats1, 4)
            pe.wait_ge(ssd_act, 9)
            for c in range(NC):
                if c:
                    pe.wait_ge(ce_ready, 1)
                for h in range(NH):
                    o = ps[HD * (h % 2):HD * (h % 2) + HD, 6 + c, (h // 2) * P:(h // 2 + 1) * P]
                    last = pe.matmul(o, xdt[:, c, h * HD:(h + 1) * HD], lmat[:, c, h, :],
                                     start=True, stop=c == 0)
                    if c:
                        last = pe.matmul(o, st_rows[:, h * HD:(h + 1) * HD], ce[:, h, :],
                                         start=False, stop=True)
                last.then_inc(ssd_y, 1)
            s5_y(3)
            pe.wait_ge(gy_ready, 1)
            pe.wait_ge(v_done, 4)
            pe.wait_ge(s5_loaded, 48)
            for i in range(WT):
                for j in range(WT):
                    last = pe.matmul(ps[:, i // 2, (i % 2) * T:(i % 2) * T + T], glu_w[:, j, i * P:(i + 1) * P],
                                     y5[:, j, :], start=j == 0, stop=j == WT - 1)
            last.then_inc(glu_done, 1)
            pe.wait_ge(yz_ready, 1)
            for g in range(2):
                for j in range(2):
                    last = pe.matmul(ps[:, 2, g * T:(g + 1) * T], const("one"), yz_sq[:, 2 * g + j, :],
                                     start=j == 0, stop=j == 1)
            last.then_inc(yz_sum, 1)
            pe.wait_ge(yc_ready, 1)
            for s in range(2):
                pe.wait_ge(loaded[s], 32)
            pe_out(pe, True, 0)
            pe.wait_ge(yd_ready, WT)
            pe_out(pe, False, 1)

        def act_mix1(act, order):
            act_norm(act, order, 2)

            def copy_job(job, func):
                act.wait_ge(p1_done, job + 1)
                act.activation(p1[:, 2 * job:2 * job + 2, :],
                               ps[:, 4 + job % 4, :].rearrange("p (a n) -> p a n", a=2), func).then_inc(p1_ready, 1)
            act.wait_ge(rot_table, 1)
            for job in range(8):
                copy_job(job, ACT.Silu if job in (2, 3) else ACT.Copy)
            act.activation(a_neg, vec2(("dt_bias", "a_log")), ACT.Exp).then_inc(sp2, 1)
            act.wait_ge(sp1, 1)
            act.activation(sp_e, sp_w, ACT.Exp, scale=-1.0).then_inc(sp2, 1)
            act.wait_ge(sp1, 2)
            act.activation(sp_l, sp_w, ACT.Ln).then_inc(sp2, 1)
            for n in range(2):
                act.wait_ge(conv_done, 4 * n + 4)
                act.activation(xc[:, 4 * n:4 * n + 4, :], xc[:, 4 * n:4 * n + 4, :], ACT.Silu).then_inc(xc_ready, 1)
            act.wait_ge(jobs, 3)
            act.activation(b_rows, ps[:, 6, 0:2 * P], ACT.Copy).then_inc(ssd_act, 1)
            for n in range(4):
                c, g = divmod(n, 2)
                act.wait_ge(jobs, 4 + n)
                act.activation(lmat[:, c, 4 * g:4 * g + 4, :],
                               ps[:, 7 - n % 2, :].rearrange("p (a n) -> p a n", a=4), ACT.Exp).then_inc(ssd_act, 1)
            act.wait_ge(jobs, 9)
            act.activation(dec_s[:, 0:NH], ps[:, 6, 0:NH], ACT.Exp).then_inc(ssd_act, 1)
            for g in range(2):
                act.wait_ge(jobs, 10 + g)
                act.activation(ce[:, 4 * g:4 * g + 4, :], ps[:, 7 - g, :].rearrange("p (a n) -> p a n", a=4),
                               ACT.Exp).then_inc(ssd_act, 1)
            act.wait_ge(jobs, 12)
            act.activation(st_rows, ps[:, 7, :], ACT.Copy).then_inc(ssd_act, 1)
            act.wait_ge(y5_in, WT)
            act.activation(y5, y5, ACT.Gelu_apprx_tanh).then_inc(gy_ready, 1)
            act.wait_ge(glu_done, 1)
            for i in range(WT):
                act.activation(tmp1[:, i, :], ps[:, i // 2, (i % 2) * T:(i % 2) * T + T], ACT.Sigmoid,
                               bias=vec("glu_b")[:, i:i + 1]).then_inc(glu_sig, 1)
            act.wait_ge(yz_sum, 1)
            act.activation(yz_sq[:, 0:2, :], ps[:, 2, :].rearrange("p (a n) -> p a n", a=2), ACT.Sqrt,
                           scale=1.0 / (2 * P), bias=eps_col).then_inc(yz_root, 1)
            act.wait_ge(yc_ready, 1)
            for n in range(3):
                e_high(act, n, 0)
            act_post(act, order, 2)

        def vec2(names):
            a, b = VEC_AT[names[0]][0], VEC_AT[names[1]][0] + NH
            return vecs[:, a:b]

        def dve_mix1(dve, order):
            dve_norm(dve, order, 2, vec("g_mix1"))
            dve.wait_ge(s5_loaded, 32)
            cr, ci, orr, oi = c_in[:, 0], c_in[:, 1], c_out[:, 0], c_out[:, 1]
            fr, fi = along(f_re, 32), along(f_im, 32)
            t1 = tmp1.rearrange("p a n -> p (a n)")[:, 0:S5_TILES * 32].rearrange("p (j n) -> p j n", n=32)
            order.mark(dve.tensor_tensor(orr, cr, fr, ALU.mult))
            order.then(dve.tensor_tensor(t1, ci, fi, ALU.mult))
            order.then(dve.tensor_tensor(orr, orr, t1, ALU.subtract))
            order.mark(dve.tensor_tensor(oi, cr, fi, ALU.mult))
            order.then(dve.tensor_tensor(t1, ci, fr, ALU.mult))
            dve.scalar_tensor_tensor(oi, oi, -1.0, t1, ALU.mult, ALU.subtract).then_inc(c_ready, 1)
            dve.wait_ge(c_ready, 1)
            dve.tensor_scalar(c_minus, orr, -1.0, None, ALU.mult).then_inc(c_ready, 1)

            def scale_c():
                dve.wait_ge(ssd_act, 8)
                for g in range(2):
                    m = ce[:, 4 * g:4 * g + 4, :]
                    order.mark(dve.tensor_tensor(m, m, across(xc[:, WT + 2 + g, P:T], 4), ALU.mult))
                order.join()
                dve.nop().then_inc(ce_ready, 1)

            def s5_group(g):
                js = slice(4 * g, 4 * g + 4)
                c, s = cos_t[:, js, :], sin_t[:, js, :]
                z_re, z_im = z_bufs[g % 2]
                dve.wait_ge(bu_done, g + 1)
                if g > 1:
                    dve.wait_ge(y5_done, g - 1)
                b_re, b_im = ps[:, 0:4, 0:T], ps[:, 0:4, T:2 * T]
                order.mark(dve.tensor_tensor(z_re, b_re, c, ALU.mult))
                order.mark(dve.tensor_tensor(tmp1, b_im, s, ALU.mult))
                order.mark(dve.tensor_tensor(z_im, b_im, c, ALU.mult))
                dve.tensor_tensor(tmp2, b_re, s, ALU.mult).then_inc(v_done, 1)
                order.join()
                dve.wait_ge(v_done, g + 1)
                order.mark(dve.tensor_tensor(z_re, z_re, tmp1, ALU.add))
                order.then(dve.tensor_tensor(z_im, z_im, tmp2, ALU.subtract))
                for q in range(4):
                    mag = s5_mag[:, 4 * g + q:4 * g + q + 1].broadcast_to([P, T])
                    for z in (z_re, z_im):
                        order.mark(dve.tensor_tensor_scan(z[:, q, :], mag, z[:, q, :], 0.0, ALU.mult, ALU.add))
                order.join()
                dve.nop().then_inc(z_ready, 1)
                if g == 3:
                    scale_c()
                    dve.wait_ge(y5_done, g)
                    order.then(dve.tensor_tensor(z_re_cos, z_re, c, ALU.mult))
                    dve.tensor_tensor(z_re, z_re, s, ALU.mult).then_inc(last_re, 1)

            dve.wait_ge(rot_table, 1)
            s5_group(0)
            s5_group(1)
            def dt_start():
                dve.wait_ge(dt_done, 1)
                order.then(dve.tensor_tensor(dt_v.rearrange("p (c h) -> p c h", c=NC),
                                             ps[:, 5, 0:NC * NH].rearrange("p (c h) -> p c h", c=NC),
                                             across(vec("dt_bias"), NC), ALU.add))
                dve.scalar_tensor_tensor(sp_w, dt_v, -1.0, dt_v, ALU.mult, ALU.max).then_inc(sp1, 1)
                order.then(dve.tensor_scalar(dt_v, dt_v, 0.0, None, ALU.max))

            def dt_middle():
                dve.wait_ge(sp2, 2)
                dve.tensor_scalar(sp_w, sp_e, 1.0, None, ALU.add).then_inc(sp1, 1)
                dve.wait_ge(sp1, 2)
                order.then(dve.tensor_scalar(sp_m, sp_w, 1.0, None, ALU.is_equal))
                order.then(dve.scalar_tensor_tensor(adt, sp_w, -1.0, sp_m, ALU.add, ALU.add))
                order.then(dve.reciprocal(adt, adt))

            def dt_end():
                dve.wait_ge(sp2, 3)
                order.then(dve.tensor_tensor(sp_l, sp_l, sp_m, ALU.add))
                order.then(dve.tensor_tensor(sp_l, sp_l, adt, ALU.mult))
                order.then(dve.tensor_tensor(sp_l, sp_l, sp_e, ALU.mult))
                order.then(dve.tensor_tensor(dt_v, dt_v, sp_l, ALU.add))
                dve.scalar_tensor_tensor(adt.rearrange("p (c h) -> p c h", c=NC),
                                         dt_v.rearrange("p (c h) -> p c h", c=NC), -1.0,
                                         across(a_neg[:, NH:2 * NH], NC), ALU.mult, ALU.mult).then_inc(dt_ready, 1)

            taps = vec("conv_w").rearrange("p (j i) -> p j i", j=4)
            for i in range(KT):
                dve.wait_ge(p1_ready, 5 + i // 2)
                x = p1[:, 8 + i, :]
                order.mark(dve.tensor_scalar(xc[:, i, :], x, taps[:, 3, i:i + 1], vec("conv_b")[:, i:i + 1],
                                             ALU.mult, ALU.add))
            order.join()
            for back in (1, 2, 3):
                for i in range(KT):
                    x = p1[:, 8 + i, :]
                    ins = dve.scalar_tensor_tensor(xc[:, i, back:], x[:, 0:T - back], taps[:, 3 - back, i:i + 1],
                                                   xc[:, i, back:], ALU.mult, ALU.add)
                    if back < 3:
                        order.mark(ins)
                    else:
                        ins.then_inc(conv_done, 1)
                order.join()
                if back == 1:
                    dt_start()
                elif back == 2:
                    dt_middle()
            dt_end()
            for c in range(NC):
                dve.wait_ge(jobs, c + 1)
                dve.tensor_tensor(xdt[:, c, :].rearrange("p (h n) -> p h n", h=NH),
                                  ps[:, 6 + c, :].rearrange("p (h n) -> p h n", h=NH),
                                  along(dt_v[:, c * NH:(c + 1) * NH], HD), ALU.mult).then_inc(ssd_dve, 1)
            s5_group(2)
            dve.wait_ge(jobs, 8)
            dve.tensor_tensor(cb.rearrange("p c g n -> p (c g) n"),
                              ps[:, 7, :].rearrange("p (a n) -> p a n", a=4), across(const("le"), 4), ALU.mult)\
                .then_inc(ssd_dve, 1)
            dve.wait_ge(ssd_act, 6)
            dve.tensor_tensor(xdec.rearrange("p (h n) -> p h n", h=NH),
                              xdt[:, 0, :].rearrange("p (h n) -> p h n", h=NH),
                              along(dec_s[:, 0:NH], HD), ALU.mult).then_inc(xdec_ready, 1)
            dve.wait_ge(ssd_dve, 3)
            for n in range(4):
                c, g = divmod(n, 2)
                m = lmat[:, c, 4 * g:4 * g + 4, :]
                dve.tensor_tensor(m, m, across(cb[:, c, g, :], 4), ALU.mult).then_inc(mats1, 1)
            s5_group(3)
            dve.wait_ge(y5_done, 4)
            for i in range(WT):
                dve.scalar_tensor_tensor(y5[:, i, :], p1[:, i, :], vec("s5_d")[:, i:i + 1],
                                         ps[:, 4 + i // 2, (i % 2) * T:(i % 2) * T + T],
                                         ALU.mult, ALU.add).then_inc(y5_in, 1)
            dve.wait_ge(ssd_y, 2)
            for i in range(WT):
                order.mark(dve.scalar_tensor_tensor(
                    yz[:, i, :].rearrange("p (c n) -> p c n", c=NC),
                    xc[:, i, :].rearrange("p (c n) -> p c n", c=NC), vec("m2_d")[:, i:i + 1],
                    ps[:, 6:8, i * P:(i + 1) * P], ALU.mult, ALU.add))
            order.join()
            order.then(dve.tensor_tensor(yz, yz, p1[:, 4:8, :], ALU.mult))
            dve.tensor_tensor(yz_sq, yz, yz, ALU.mult).then_inc(yz_ready, 1)
            dve.wait_ge(glu_sig, WT)
            dve.tensor_tensor(y8[:, 0:WT, :], y5, tmp1, ALU.mult).then_inc(yc_ready, 1)
            dve.wait_ge(yz_root, 1)
            order.then(dve.reciprocal(yz_sq[:, 0:2, :], yz_sq[:, 0:2, :]))
            for i in range(WT):
                dve.scalar_tensor_tensor(y8[:, WT + i, :], yz[:, i, :], vec("m2_norm")[:, i:i + 1],
                                         yz_sq[:, i // 2, :], ALU.mult, ALU.mult).then_inc(yd_ready, 1)
            for n in range(3):
                e_low(dve, n, 0)
            dve_post(dve, order, 2)

        def pool_mix1(pool, order):
            pool.wait_ge(x_ready, 4)
            pool.dma_start(gain_rows[:, :], t["gain_mix1"]).then_inc(s_gain, 16)
            def s5_back(g):
                c, sn = cos_t[:, 4 * g:4 * g + 4, :], sin_t[:, 4 * g:4 * g + 4, :]
                z_re, z_im = z_bufs[g % 2]
                pool.wait_ge(z_ready, g + 1)
                if g:
                    pool.wait_ge(y5_done, g)
                if g < 3:
                    order.mark(pool.tensor_tensor(z_re_cos, z_re, c, ALU.mult))
                order.mark(pool.tensor_tensor(z_im_cos, z_im, c, ALU.mult))
                order.join()
                if g < 3:
                    order.mark(pool.tensor_tensor(z_re, z_re, sn, ALU.mult))
                order.mark(pool.tensor_tensor(z_im, z_im, sn, ALU.mult))
                order.join()
                pool.nop().then_inc(q_done, 1)
            s5_back(0)
            s5_back(1)
            pool.wait_ge(dt_ready, 1)
            for c in range(NC):
                pool.tensor_tensor(seg_in[:, c, :, :], across(const("gt"), NH),
                                   along(adt[:, c * NH:(c + 1) * NH], P), ALU.mult).then_inc(seg_ready, 1)
            pool.wait_ge(jobs, 7)
            pool.tensor_tensor(acs_in, across(const("one"), NH), along(adt[:, NH:2 * NH], P), ALU.mult)\
                .then_inc(seg_ready, 1)
            s5_back(2)
            s5_back(3)

        STEPS = []
        for u in range(UNITS):
            STEPS += [("gate", u, 0), ("gate", u, 1), ("up", u, 0), ("up", u, 1)]
            STEPS += [("down", u - 1, 0), ("down", u - 1, 1)] if u else []
        STEPS += [("down", UNITS - 1, 0), ("down", UNITS - 1, 1)]
        N_STEPS = len(STEPS)
        assert N_STEPS % HALVES == 0 and N_STEPS % 3 == 0
        AT = {step: n for n, step in enumerate(STEPS)}
        GATED = [AT["gate", u, 1] for u in range(UNITS)]
        UPPED = [AT["up", u, 1] for u in range(UNITS)]
        DOWNED = [AT["down", u, 1] for u in range(UNITS)]
        LAST = UNITS - 1
        TURN_LAST = AT["down", LAST - 1, 0]

        def raw_of(n):
            i = 1 + (n + 3) % HALVES
            return i, half_slot(i)

        def loads_before(n, item):
            i, _ = raw_of(n % N_STEPS)
            before = sum(m % RAW == i for m in range(IN_STEPS))
            before += sum(f_half(m)[0] == i for m in range(F_STEPS)) + sum(in1_half(job)[0] == i for job in range(8))
            per_pass = N_STEPS // HALVES
            return item * (16 * per_pass) + 16 * (before + per_pass * (n // N_STEPS) + n % N_STEPS // HALVES + 1)

        def e_high(act, n, item):
            i, raw = raw_of(n % N_STEPS)
            act.wait_ge(half_loaded[i], loads_before(n, item))
            act.activation(split[:, n % 3, 0, :], raw, ACT.Copy).then_inc(hi_ready, 1)

        def e_low(dve, n, item):
            _, raw = raw_of(n % N_STEPS)
            dve.wait_ge(hi_ready, item * N_STEPS + (n + 1))
            dve.tensor_tensor(split[:, n % 3, 1, :], raw, split[:, n % 3, 0, :].bitcast(F32),
                              ALU.subtract).then_inc(lo_ready, 1)

        def passes(engine, body):
            with engine.Fori(0, NE) as e:
                body(e)
            engine.wait_ge(plan_ready, 1)
            n_over = engine.value_load(plan[0:1, 0:1], min_val=0, max_val=MAX_OVER)
            with engine.If(n_over > 0):
                with engine.Fori(0, n_over) as j:
                    body(j + NE)
            return n_over

        def sp_moe(sp):
            gate_d = t["l1_moe_w_gate"].rearrange("e (k p) n -> p (e k) n", p=P)
            up_d = t["l1_moe_w_up"].rearrange("e (k p) n -> p (e k) n", p=P)
            down_d = t["l1_moe_w_down"].rearrange("e f d -> (e f) d")

            def load(n, e):
                kind, u, half = STEPS[n]
                i, raw = raw_of(n)
                if kind == "down":
                    dst = raw.rearrange("p (k d) -> p k d", k=2)
                    src = down_d[bass.ds(e * FE + u * NB, NB), :].rearrange("(p k) d -> p k d", k=4)
                    src = src[:, 2 * half:2 * half + 2, :]
                else:
                    dst = raw.rearrange("p (k n) -> p k n", k=4)
                    src = (gate_d if kind == "gate" else up_d)[:, bass.ds(e * KT + 4 * half, 4),
                                                               u * NB:(u + 1) * NB]
                sp.dma_start(dst, src).then_inc(half_loaded[i], 16)

            sp.wait_ge(yc_ready, 1)
            sp.wait_ge(yd_ready, WT)
            for n in range(N_STEPS):
                if n == 4:
                    sp.wait_ge(y_done, 6)
                if n >= HALVES:
                    sp.wait_ge(lo_ready, n - HALVES + 1)
                load(n, 0)

            def body(item, e):
                for n in range(N_STEPS):
                    sp.wait_ge(lo_ready, item * N_STEPS + (n - HALVES + 1))
                    load(n, e)
            with sp.Fori(1, NE) as e:
                body(e, e)
            sp.wait_ge(plan_ready, 1)
            n_over = sp.value_load(plan[0:1, 0:1], min_val=0, max_val=MAX_OVER)
            with sp.If(n_over > 0):
                with sp.Fori(0, n_over) as j:
                    body(j + NE, sp.value_load(plan[0:1, bass.ds(j + 1, 1)], min_val=0, max_val=NE - 1))
            for n in range(3):
                sp.wait_ge(lo_ready, n_over * N_STEPS + (NE * N_STEPS + n - HALVES + 1))
                load(n, 0)
            for c in range(NC):
                sp.wait_ge(x_ready, 7 + c)
                sp.dma_start(out[c * P:(c + 1) * P, :], x_rows[:, c, :]).then_inc(out_done, 16)

        def pe_moe(pe):
            pe_norm(pe, 3)
            for c in range(NC):
                pe.wait_ge(xn_ready, 14 + 2 * c)
                for j in range(KT):
                    last = pe.matmul(ps[:, 4, c * NE:(c + 1) * NE], xn[:, j, c * P:(c + 1) * P],
                                     w_small[:, 1, j, :], start=j == 0, stop=j == KT - 1)
            last.then_inc(logits_done, 1)
            pe.wait_ge(sel_ready, 1)
            for n, terms in enumerate(((("lt", 0),), (("one", 0), ("lt", 1)), (("one", 0), ("one", 1)))):
                for i, (name, c) in enumerate(terms):
                    last = pe.matmul(ps[:, 5, n * NE:(n + 1) * NE], const(name), sel[:, c, :],
                                     start=i == 0, stop=i == len(terms) - 1)
            last.then_inc(ranks_done, 1)

            def gather(q, bank):
                for k in range(4):
                    f = (4 * q + k) * P
                    for c in range(NC):
                        last = pe.matmul(ps[:, bank, k * P:(k + 1) * P], xs[:, c, f:f + P], perm[:, c, :],
                                         start=c == 0, stop=c == NC - 1)
                last.then_inc(gather_done, 1)

            def scatter(c, bank):
                for h in range(2):
                    pe.matmul(ps[:, bank + h, :], perm_t[:, c, :], e_y[:, h, :],
                              start=True, stop=True).then_inc(comb_done, 1)

            def turn(u, item):
                pe.wait_ge(h_ready, item * UNITS + (u + 1))
                for k in range(4):
                    last = pe.transpose(ps[:, u % 2, k * P:(k + 1) * P],
                                        e_h[u % 2].rearrange("s (f k) -> s k f", k=4)[:, k, :], ident)
                last.then_inc(t_done, 1)

            def product(kind, u, half, item):
                n = AT[kind, u, half]
                if kind == "down":
                    pe.wait_ge(ht_lo, item * UNITS + (u + 1))
                pe.wait_ge(lo_ready, item * N_STEPS + (n + 1))
                w = split[:, n % 3, :, :]
                if kind == "down":
                    w = w.rearrange("p a (k d) -> p a k d", k=2)
                    for k in range(2):
                        for a, b in TERMS:
                            for h in range(2):
                                last = pe.matmul(ps[:, 6 + h, :], ht_parts[:, u % 2, a, 2 * half + k, :],
                                                 w[:, b, k, h * NB:(h + 1) * NB],
                                                 start=u == half == k == a == b == 0,
                                                 stop=u == LAST and half == k == 1 and a == 1)
                else:
                    w = w.rearrange("p a (k n) -> p a k n", k=4)
                    for j in range(4):
                        for a, b in TERMS:
                            last = pe.matmul(ps[:, 2 + 2 * (u % 2) + (kind == "up"), :],
                                             xg_parts[:, a, 4 * half + j, :], w[:, b, j, :],
                                             start=half == j == a == b == 0,
                                             stop=half == 1 and j == 3 and a == 1)
                last.then_inc(part_done, 1)

            pe.wait_ge(perm_ready, 4)
            for q in range(2):
                gather(q, 1 - q)

            def body(item):
                pe.wait_ge(xg_lo, item + 1)
                for u in range(UNITS):
                    if u == 1:
                        pe.wait_ge(comb_added, item * 4 + 2)
                    for half in range(2):
                        product("gate", u, half, item)
                    if u == 0:
                        pe.wait_ge(ey_ready, item * 2 + 2)
                        pe.wait_ge(pgt_copied, item + 1)
                        scatter(0, 4)
                    if u == 1:
                        pe.wait_ge(comb_added, item * 4 + 4)
                    if u == 4:
                        pe.wait_ge(pgt_copied, item + 2)
                    if u == 6:
                        pe.wait_ge(xg_ready, item * 2 + 3)
                    if u:
                        turn(u - 1, item)
                    for half in range(2):
                        product("up", u, half, item)
                    if u == 0:
                        scatter(1, 0)
                    if u == 3:
                        for c in range(NC):
                            last = pe.transpose(ps[:, 1, c * P:(c + 1) * P], perm_gate[:, c, :], ident)
                        last.then_inc(pgt_done, 1)
                    if u == 5:
                        pe.wait_ge(perm_ready, item * 4 + 8)
                        gather(0, 1)
                    if 0 < u:
                        product("down", u - 1, 0, item)
                        if u == LAST:
                            pe.wait_ge(xg_ready, item * 2 + 4)
                            turn(LAST, item)
                        product("down", u - 1, 1, item)
                    if u == 5:
                        gather(1, 0)
                for half in range(2):
                    product("down", LAST, half, item)
            n_over = passes(pe, body)
            pe.wait_ge(ey_ready, n_over * 2 + (NE * 2 + 2))
            scatter(0, 4)
            scatter(1, 0)

        def act_moe(act, order):
            act_norm(act, order, 3)
            act.wait_ge(router_max, 1)
            for c in range(NC):
                act.activation(e_exp[:, c, :], logits[:, c, :], ACT.Exp, bias=top[:, c:c + 1]).then_inc(router_exp, 1)

            def xg_high(passes_before):
                act.wait_ge(xg_ready, passes_before * 2 + 2)
                act.activation(xg_parts[:, 0, :, :], xg, ACT.Copy).then_inc(xg_hi, 1)

            def silu(u):
                act.activation(e_silu[u % 2], ps[:, 2 + 2 * (u % 2), :], ACT.Silu).then_inc(silu_ready, 1)

            def ht_high(u, item):
                act.wait_ge(t_done, item * UNITS + (u + 1))
                act.activation(ht_parts[:, u % 2, 0, :, :], ps[:, u % 2, :].rearrange("p (k n) -> p k n", k=4),
                               ACT.Copy).then_inc(ht_hi, 1)
            xg_high(0)

            def body(item):
                for n in range(N_STEPS):
                    if n == TURN_LAST:
                        ht_high(LAST, item)
                    act.wait_ge(part_done, item * N_STEPS + (n + 1))
                    if n == N_STEPS - 1:
                        for h in range(2):
                            act.activation(e_y[:, h, :], ps[:, 6 + h, :], ACT.Copy).then_inc(ey_ready, 1)
                    e_high(act, n + 3, item)
                    for u in range(UNITS):
                        if n == GATED[u]:
                            silu(u)
                            if u:
                                ht_high(u - 1, item)
                    if n == UPPED[3]:
                        act.wait_ge(pgt_done, item + 1)
                        act.activation(perm_t, ps[:, 1, 0:NC * P].rearrange("p (c n) -> p c n", c=NC), ACT.Copy)\
                            .then_inc(pgt_copied, 1)
                    if n == UPPED[LAST]:
                        xg_high(item + 1)
            passes(act, body)
            order.then(act.activation(root, sumsq, ACT.Sqrt, scale=1.0 / D, bias=eps_col))
            for c in range(NC):
                act.wait_ge(moe_ready, c + 1)
                order.mark(act.activation(xs[:, c, :], moe[:, c, :], ACT.Square, accum_out=sumsq[:, c:c + 1]))
            order.join()
            act.activation(root, sumsq, ACT.Sqrt, scale=1.0 / D, bias=eps_col).then_inc(out_root, 1)

        def dve_moe(dve, order):
            dve_norm(dve, order, 3, vec("g_ffn1"))
            dve.wait_ge(logits_done, 1)
            order.then(dve.tensor_copy(logits, ps[:, 4, 0:NC * NE].rearrange("p (c e) -> p c e", c=NC)))
            order.then(dve.tensor_reduce(top, logits, AX.X, ALU.max))
            dve.tensor_scalar(top, top, -1.0, None, ALU.mult).then_inc(router_max, 1)
            lower = const("lower8").rearrange("p (a b) -> p a b", a=NE)
            for c in range(NC):
                other, own = across(logits[:, c, :], NE), along(logits[:, c, :], NE)
                order.mark(dve.tensor_tensor(cmp1[:, c], other, own, ALU.is_gt))
                order.mark(dve.tensor_tensor(cmp2[:, c], other, own, ALU.is_equal))
            order.join()
            for c in range(NC):
                order.mark(dve.tensor_tensor(cmp2[:, c], cmp2[:, c], lower, ALU.mult))
            order.join()
            for c in range(NC):
                order.mark(dve.tensor_tensor(cmp1[:, c], cmp1[:, c], cmp2[:, c], ALU.add))
            order.join()
            for c in range(NC):
                order.mark(dve.tensor_reduce(beaten[:, c, :], cmp1[:, c], AX.X, ALU.add))
            order.join()
            dve.tensor_scalar(sel, beaten, 2.0, None, ALU.is_lt).then_inc(sel_ready, 1)
            dve.wait_ge(router_exp, 2)
            dve.wait_ge(sel_ready, 1)
            order.then(dve.tensor_tensor(e_exp, e_exp, sel, ALU.mult))
            order.then(dve.tensor_reduce(den, e_exp, AX.X, ALU.add))
            order.then(dve.reciprocal(den, den))
            order.mark(dve.tensor_tensor(gate_all[:, :, 0:NE], e_exp, along(den, NE), ALU.mult))
            dve.wait_ge(ranks_done, 1)
            order.then(dve.scalar_tensor_tensor(rank_all[:, :, 0:NE],
                                                ps[:, 5, 0:NC * NE].rearrange("p (c e) -> p c e", c=NC), 1.0,
                                                sel, ALU.add, ALU.mult))
            order.then(dve.tensor_scalar(rank_all[:, :, 0:NE], rank_all[:, :, 0:NE], -1.0, None, ALU.add))

            def make_perm(item):
                for c in range(NC):
                    rank, gate = (x[:, c, bass.ds(item, 1)] for x in (rank_all, gate_all))
                    dve.tensor_scalar(perm[:, c, :], const("iota"), rank, None, ALU.is_equal).then_inc(perm_ready, 1)
                    dve.tensor_scalar(perm_gate[:, c, :], const("iota"), rank, gate, ALU.is_equal,
                                      ALU.mult).then_inc(perm_ready, 1)

            def make_xg(q, item):
                dve.wait_ge(gather_done, item * 2 + (q + 1))
                dve.tensor_tensor(xg[:, 4 * q:4 * q + 4, :], ps[:, 1 - q, :].rearrange("p (k n) -> p k n", k=4),
                                  along(vec("g_ffn1")[:, 4 * q:4 * q + 4], P), ALU.mult).then_inc(xg_ready, 1)

            def xg_low(item):
                dve.wait_ge(xg_hi, item + 1)
                dve.tensor_tensor(xg_parts[:, 1, :, :], xg, xg_parts[:, 0, :, :].bitcast(F32),
                                  ALU.subtract).then_inc(xg_lo, 1)
            make_perm(0)
            order.mark(dve.tensor_copy(counts, ps[:, 5, NC * NE:(NC + 1) * NE]))
            for q in range(2):
                make_xg(q, 0)
            xg_low(0)
            order.mark(dve.memset(rank_all[:, :, NE:], 0.0))
            order.mark(dve.memset(gate_all[:, :, NE:], 0.0))
            order.then(dve.tensor_scalar(over, counts, float(P), None, ALU.is_gt))
            order.then(dve.tensor_tensor_scan(over_sum, const("one")[:, 0:NE], over, 0.0, ALU.mult, ALU.add))
            order.mark(dve.tensor_copy(plan_f[:, 0:1], over_sum[:, NE - 1:NE]))
            for j in range(MAX_OVER):
                order.then(dve.scalar_tensor_tensor(pick, over_sum, float(j + 1), over, ALU.is_equal, ALU.mult))
                order.mark(dve.tensor_tensor(counts, pick, const("iota")[:, 0:NE], ALU.mult))
                order.then(dve.scalar_tensor_tensor(chosen, rank_all[:, :, 0:NE], 1.0 - P, across(pick, NC),
                                                    ALU.add, ALU.mult))
                order.mark(dve.tensor_reduce(plan_f[:, j + 1:j + 2], counts, AX.X, ALU.add))
                order.then(dve.tensor_reduce(rank_all[:, :, NE + j], chosen, AX.X, ALU.add))
                order.then(dve.tensor_tensor(chosen, gate_all[:, :, 0:NE], across(pick, NC), ALU.mult))
                order.then(dve.tensor_reduce(gate_all[:, :, NE + j], chosen, AX.X, ALU.add))
            order.mark(dve.tensor_scalar(rank_all[:, :, NE:], rank_all[:, :, NE:], -1.0, None, ALU.add))
            order.join()
            dve.tensor_copy(plan, plan_f).then_inc(plan_ready, 1)

            def ht_low(u, item):
                dve.wait_ge(ht_hi, item * UNITS + (u + 1))
                dve.tensor_tensor(ht_parts[:, u % 2, 1, :, :], ps[:, u % 2, :].rearrange("p (k n) -> p k n", k=4),
                                  ht_parts[:, u % 2, 0, :, :].bitcast(F32), ALU.subtract).then_inc(ht_lo, 1)

            def add_rows(n, bank, before):
                m = moe[:, n // 2, (n % 2) * NB:(n % 2 + 1) * NB]
                dve.wait_ge(comb_done, before * 4 + (n + 1))
                dve.tensor_tensor(m, m, ps[:, bank, :], ALU.add).then_inc(comb_added, 1)

            def body(item):
                for n in range(N_STEPS):
                    if n == TURN_LAST:
                        ht_low(LAST, item)
                    for u in range(UNITS):
                        if n == UPPED[u]:
                            dve.wait_ge(part_done, item * N_STEPS + (n + 1))
                            dve.wait_ge(silu_ready, item * UNITS + (u + 1))
                            dve.tensor_tensor(e_h[u % 2], e_silu[u % 2], ps[:, 3 + 2 * (u % 2), :], ALU.mult)\
                                .then_inc(h_ready, 1)
                    e_low(dve, n + 3, item)
                    if n in (1, 3):
                        for h in range(2):
                            add_rows(n - 1 + h, (4 if n == 1 else 0) + h, item)
                    for u in range(UNITS):
                        if n == GATED[u] and u:
                            ht_low(u - 1, item)
                    if n == UPPED[4]:
                        dve.wait_ge(pgt_done, item + 1)
                        make_perm(item + 1)
                    if n == UPPED[5]:
                        make_xg(0, item + 1)
                    if n == DOWNED[4]:
                        make_xg(1, item + 1)
                    if n == DOWNED[5]:
                        xg_low(item + 1)
            dve.wait_ge(pgt_copied, 1)
            n_over = passes(dve, body)
            for c in range(NC):
                for h in range(2):
                    add_rows(2 * c + h, (4, 0)[c] + h, n_over + NE)
                dve.wait_ge(comb_added, n_over * 4 + (4 * NE + 2 * c + 2))
                dve.nop().then_inc(moe_ready, 1)
            dve.wait_ge(out_root, 4)
            order.then(dve.reciprocal(rstd, root))
            dve.wait_ge(s_gain, 64)
            for c in range(NC):
                order.then(dve.scalar_tensor_tensor(xs[:, c, :], moe[:, c, :], rstd[:, c:c + 1], gain_rows[:, :],
                                                    ALU.mult, ALU.mult))
                dve.tensor_tensor(x_rows[:, c, :], x_rows[:, c, :], xs[:, c, :], ALU.add).then_inc(x_ready, 1)

        def pool_moe(pool, order):
            pool.wait_ge(x_ready, 6)
            pool.dma_start(gain_rows[:, :], t["gain_ffn1"]).then_inc(s_gain, 16)
            order.then(pool.memset(moe, 0.0))
            pool.memset(e_y, 0.0).then_inc(ey_ready, 2)
            pool.memset(perm_t, 0.0).then_inc(pgt_copied, 1)

        @block.sync
        def _(sp):
            for c in range(NC):
                sp.dma_start(x_rows[:, c, :], t["x"][c * P:(c + 1) * P, :]).then_inc(s_x[c], 16)
            w = t["l0_w_in"].rearrange("(k p) n -> p k n", p=P)
            for n in range(IN_STEPS):
                if n >= RAW:
                    sp.wait_ge(in_lo, n - RAW + 1)
                sp.dma_start(half_slot(n % RAW).rearrange("p (k n) -> p k n", k=KT),
                             w[:, :, n * T:(n + 1) * T]).then_inc(half_loaded[n % RAW], 16)
                if n == RAW - 1:
                    for dst, name in ((lora_wa, "lora_wa"), (gln, "gmlp_ln"), (ws_t, "ws_t"),
                                      (bs_row[0:1, :], "bs_row"), (inv_mask, "inv_mask"),
                                      (lora_g, "l0_rwkv_g2")):
                        sp.dma_start(dst, t[name]).then_inc(s_b2, 16)
                    sp.dma_start(w_small[:, 0], t["w_dt"]).then_inc(s_b2, 16)
                    sp.dma_start(w_small[:, 1], t["router"]).then_inc(s_b2, 16)
            w = t["l0_w_out"].rearrange("(k p) n -> p k n", p=P)
            sp.wait_ge(in_lo, IN_STEPS - 1)
            for s in range(2):
                sp.dma_start(slot_tiles(s), w[:, :, s * NB:(s + 1) * NB]).then_inc(loaded[s], 16)
            sp_ffn(sp)
            sp_mix1(sp)
            sp_moe(sp)
            sp.wait_ge(out_done, 32)

        @block.gpsimd
        def _(pool):
            order = Order(pool, o_pool)
            pool_mix0(pool, order)
            pool.wait_ge(x_ready, 2)
            pool.dma_start(gain_rows[:, :], t["gain_ffn0"]).then_inc(s_gain, 16)
            pool_rotations(pool, order)
            pool_mix1(pool, order)
            pool_moe(pool, order)

        @block.scalar
        def _(act):
            order = Order(act, o_act)
            act.dma_start(consts[:, :], t["consts"]).then_inc(s_init, 16)
            act.dma_start(vecs[:, :], t["vecs"]).then_inc(s_init, 16)
            act_mix0(act, order)
            act_ffn(act, order)
            act_mix1(act, order)
            act_moe(act, order)

        @block.vector
        def _(dve):
            order = Order(dve, o_dve)
            dve_mix0(dve, order)
            dve_ffn(dve, order)
            dve_mix1(dve, order)
            dve_moe(dve, order)

        @block.tensor
        def _(pe):
            pe_mix0(pe)
            pe_ffn(pe)
            pe_mix1(pe)
            pe_moe(pe)


def layout(inputs):
    import numpy as np

    a = {k: np.asarray(v) for k, v in inputs.items()}
    f32 = np.float32

    def cols(v):
        return np.ascontiguousarray(np.reshape(v, (-1, P)).T)

    i = np.arange(P)
    s, u = i[:, None], i[None, :]
    c = {"ident": s == u, "le": s <= u, "lt": s < u, "gt": s > u, "blk": s // HD == u // HD,
         "iota": np.broadcast_to(u, (P, P)), "one": np.ones((P, P)),
         "lower8": np.broadcast_to(np.tri(NE, NE, -1).reshape(1, -1), (P, NE * NE)),
         "eps": np.broadcast_to(np.array([[EPS, GN_EPS, math.pi / 2]]), (P, 3))}
    masks = [(s // (2 * m) == u // (2 * m)) & (s % (2 * m) < m) & (u % (2 * m) >= m)
             for m in (2 ** e for e in range(LEVELS))]
    state_p = lambda v: np.ascontiguousarray(v.reshape(S5_TILES, P).T)
    per_state = lambda v: np.repeat(v, 64, axis=0)
    v = {"mu": cols(a["l0_rwkv_mu"]), "w0": cols(a["l0_rwkv_w0"]), "a0": cols(a["l0_rwkv_a0"]),
         "k_k": cols(a["l0_rwkv_k_k"]), "k_a": cols(a["l0_rwkv_k_a"]), "r_k": cols(a["l0_rwkv_r_k"]),
         "ln_w": cols(a["l0_rwkv_ln_w"]), "ln_b": cols(a["l0_rwkv_ln_b"]),
         "g_mix0": cols(a["l0_norm_pre_mix"]), "g_ffn0": cols(a["l0_norm_pre_ffn"]),
         "g_mix1": cols(a["l1_norm_pre_mix"]), "g_ffn1": cols(a["l1_norm_pre_ffn"]),
         "a_re": state_p(a["l1_s5_a_re"]), "a_im": state_p(a["l1_s5_a_im"]),
         "log_dt": state_p(per_state(a["l1_s5_log_dt"])), "s5_d": cols(a["l1_s5_d"]),
         "glu_b": cols(a["l1_s5_glu_b"]),
         "conv_w": np.concatenate([cols(w) for w in a["l1_m2_conv_w"]], axis=1),
         "conv_b": cols(a["l1_m2_conv_b"]), "m2_d": cols(per_state(a["l1_m2_d"])),
         "m2_norm": cols(a["l1_m2_norm_w"]),
         "dt_bias": np.broadcast_to(a["l1_m2_dt_bias"][None, :], (P, NH)),
         "a_log": np.broadcast_to(a["l1_m2_a_log"][None, :], (P, NH))}
    rows = lambda w: np.ascontiguousarray(np.broadcast_to(w[None, :], (P, D)))
    b_t = np.zeros((2, P, 4, P), f32)
    c_t = np.zeros((2, P, S5_TILES, 32), f32)
    for n, (b, cc) in enumerate((("l1_s5_b_re", "l1_s5_c_re"), ("l1_s5_b_im", "l1_s5_c_im"))):
        for g in range(2 * S5_TILES):
            j, half = divmod(g, 2)
            ch = 32 * (j % 4) + 16 * half
            b_t[n, ch:ch + 16, j // 4, 64 * half:64 * half + 64] = a[b][g].T
            c_t[n, 64 * half:64 * half + 64, j, 16 * half:16 * half + 16] = a[cc][g].T
    t = {
        "x": a["x"][0],
        "consts": np.concatenate([c[n] for n, _ in CONSTS], axis=1).astype(f32),
        "vecs": np.concatenate([v[n] for n, _ in VECS], axis=1),
        "inv_mask": np.stack(masks, axis=1).astype(f32),
        "lora_wa": np.concatenate([a["l0_rwkv_w2"], a["l0_rwkv_a2"]], axis=0),
        "l0_rwkv_g2": a["l0_rwkv_g2"],
        "gmlp_ln": np.ascontiguousarray(np.broadcast_to(
            np.stack([a["l0_gmlp_ln_w"].reshape(-1), a["l0_gmlp_ln_b"].reshape(-1)])[None], (P, 2, WID))),
        "ws_t": np.ascontiguousarray(a["l0_gmlp_ws"].transpose(2, 0, 1)),
        "bs_row": a["l0_gmlp_bs"].reshape(1, -1),
        "gain_mix0": rows(a["l0_norm_post_mix"]), "gain_ffn0": rows(a["l0_norm_post_ffn"]),
        "gain_mix1": rows(a["l1_norm_post_mix"]), "gain_ffn1": rows(a["l1_norm_post_ffn"]),
        "w_dt": np.ascontiguousarray(a["l1_w_in"][:, ODD_MAIN:].reshape(KT, P, NE).transpose(1, 0, 2)),
        "router": np.ascontiguousarray(a["l1_moe_router"].reshape(KT, P, NE).transpose(1, 0, 2)),
        "s5_b": b_t, "s5_c": c_t,
    }
    for name in ("l0_w_in", "l0_w_out", "l0_ffn_w_gate", "l0_ffn_w_up", "l0_ffn_w_down", "l1_w_in",
                 "l1_s5_glu_w", "l1_w_out", "l1_moe_w_gate", "l1_moe_w_up", "l1_moe_w_down"):
        t[name] = a[name]
    return {k: np.ascontiguousarray(x) for k, x in t.items()}


def kernel(**inputs):
    from concourse import bacc
    from concourse.bass_utils import run_bass_kernel_spmd

    nc = bacc.Bacc("TRN2", target_bir_lowering=False, num_devices=1)
    arrays = layout(inputs)
    aps = {n: nc.dram_tensor(f"{n}_dram", a.shape, mybir.dt.from_np(a.dtype), kind="ExternalInput").ap()
           for n, a in arrays.items()}
    out = nc.dram_tensor("out_dram", (T, D), F32, kind="ExternalOutput").ap()
    trunk(nc, aps, out)
    r = run_bass_kernel_spmd(nc, [{f"{n}_dram": a for n, a in arrays.items()}], core_ids=[0])
    return r.results[0]["out_dram"].reshape(1, T, D)
```
